# Optimizing a Trainium2 kernel written in Bass

```python
import jax, jax.numpy as jnp
from jax import lax
import numpy as np

D_MODEL = 1024
BATCH = 1
SEQ = 512
DEPTH = 1

ATTN_HEAD_DIM = 64
ATTN_WIDTH = D_MODEL // 2
ATTN_HEADS = ATTN_WIDTH // ATTN_HEAD_DIM
GLA_HEADS = 4
GLA_VAL_WIDTH = D_MODEL // 2
GLA_KEY_WIDTH = GLA_VAL_WIDTH // 2
GLA_DK = GLA_KEY_WIDTH // GLA_HEADS
GLA_DV = GLA_VAL_WIDTH // GLA_HEADS
GLA_GATE_RANK = 16
GLA_TAU = 16.0
GLA_CHUNK = 64
MIX_WIDTH = ATTN_WIDTH + GLA_VAL_WIDTH
IN_SPLITS = (ATTN_WIDTH, ATTN_WIDTH, ATTN_WIDTH,
             GLA_KEY_WIDTH, GLA_KEY_WIDTH, GLA_VAL_WIDTH, GLA_VAL_WIDTH, 2 * GLA_GATE_RANK)
IN_WIDTH = sum(IN_SPLITS)

DILATED_BRANCHES = ((128, 1), (512, 4), (2048, 16))
HALF_SPAN = 64
T5_BUCKETS = 32
T5_MAX_DISTANCE = 1024
NEG_INF = -1e30

N_EXPERTS = 32
TOP_K = 4
D_FF = D_MODEL
SWIGLU_LIMIT = 7.0
SWIGLU_ALPHA = 1.702
MOE_BLOCK = 128

NORM_EPS = 1e-5

kernel_name = "hybrid_dilated_attn_gla_moe_encoder"

def _rmsnorm(x, g):
    xf = x.astype(jnp.float32)
    y = xf * lax.rsqrt(jnp.mean(xf * xf, axis=-1, keepdims=True) + NORM_EPS)
    return (y * g.astype(jnp.float32)).astype(x.dtype)

def _t5_bucket(rel):
    nb = T5_BUCKETS // 2
    max_exact = nb // 2
    n = np.abs(rel)
    large = max_exact + (np.log(np.maximum(n, 1).astype(np.float32) / max_exact)
                         / np.log(T5_MAX_DISTANCE / max_exact) * (nb - max_exact)).astype(np.int32)
    large = np.minimum(large, nb - 1)
    return (np.where(rel > 0, nb, 0) + np.where(n < max_exact, n, large)).astype(np.int32)

def _dilated_branch(q, k, v, rel_bias, dil):
    B, S, H, Dh = q.shape
    L = S // dil
    blk = HALF_SPAN
    nb = -(-L // blk)
    Lp = nb * blk
    N = B * dil

    def to_res(t):
        return t.reshape(B, L, dil, H, Dh).transpose(0, 2, 3, 1, 4).reshape(N, H, L, Dh)

    def windows(t):
        tp = jnp.pad(to_res(t), ((0, 0), (0, 0), (blk, Lp - L + blk), (0, 0))).reshape(N, H, nb + 2, blk, Dh)
        return jnp.concatenate([tp[:, :, :-2], tp[:, :, 1:-1], tp[:, :, 2:]], axis=3)

    qb = jnp.pad(to_res(q), ((0, 0), (0, 0), (0, Lp - L), (0, 0))).reshape(N, H, nb, blk, Dh)
    kw, vw = windows(k), windows(v)

    s_idx = np.arange(blk)[:, None]
    t_idx = np.arange(3 * blk)[None, :]
    off = t_idx - blk - s_idx
    bias = jnp.transpose(rel_bias[_t5_bucket(off * dil)], (2, 0, 1)).astype(jnp.float32)
    ki = np.arange(nb)[:, None, None] * blk + t_idx - blk
    valid = (ki >= 0) & (ki < L) & (np.abs(off) <= HALF_SPAN)

    logits = jnp.einsum('nhbqd,nhbkd->nhbqk', qb, kw).astype(jnp.float32) * (Dh ** -0.5)
    logits = jnp.where(valid[None, None], logits + bias[None, :, None], NEG_INF)
    m = jnp.max(logits, axis=-1, keepdims=True)
    p = jnp.exp(logits - m)
    den = jnp.sum(p, axis=-1)
    out = jnp.einsum('nhbqk,nhbkd->nhbqd', p, vw.astype(jnp.float32)) / den[..., None]
    lse = m[..., 0] + jnp.log(den)
    out = out.reshape(N, H, Lp, Dh)[:, :, :L]
    lse = lse.reshape(N, H, Lp)[:, :, :L]
    out = out.reshape(B, dil, H, L, Dh).transpose(0, 3, 1, 2, 4).reshape(B, S, H, Dh)
    lse = lse.reshape(B, dil, H, L).transpose(0, 3, 1, 2).reshape(B, S, H)
    return out, lse

def _dilated_attention(q, k, v, rel_bias):
    B, S = q.shape[:2]
    res = [_dilated_branch(q, k, v, rel_bias, d) for (_, d) in DILATED_BRANCHES]
    outs = jnp.stack([r[0] for r in res])
    lses = jnp.stack([r[1] for r in res])
    w = jax.nn.softmax(lses, axis=0)
    out = jnp.sum(w[..., None] * outs, axis=0)
    return out.reshape(B, S, ATTN_WIDTH).astype(q.dtype)

def _gla_chunked(q, k, v, log_a):
    B, H, S, dk = q.shape
    dv = v.shape[-1]
    C = GLA_CHUNK
    nc = S // C
    q, k, log_a = (t.reshape(B, H, nc, C, dk) for t in (q, k, log_a))
    v = v.reshape(B, H, nc, C, dv)
    b = jnp.cumsum(log_a, axis=3)
    G = b[:, :, :, -1]
    qd = q * jnp.exp(b)
    kd = k * jnp.exp(-b)
    tri = np.tril(np.ones((C, C), dtype=bool))
    A = jnp.where(tri, jnp.einsum('bhncd,bhnsd->bhncs', qd, kd), 0.0)
    o_intra = jnp.einsum('bhncs,bhnse->bhnce', A, v)
    kst = k * jnp.exp(G[:, :, :, None, :] - b)
    dS = jnp.einsum('bhncd,bhnce->bhnde', kst, v)

    def step(state, inp):
        dS_n, decay_n = inp
        return decay_n[..., None] * state + dS_n, state

    _, S_prev = lax.scan(step, jnp.zeros((B, H, dk, dv), jnp.float32),
                         (dS.transpose(2, 0, 1, 3, 4), jnp.exp(G).transpose(2, 0, 1, 3)))
    S_prev = S_prev.transpose(1, 2, 0, 3, 4)
    o_inter = jnp.einsum('bhncd,bhnde->bhnce', qd, S_prev)
    return (o_intra + o_inter).reshape(B, H, S, dv)

def _bi_gla(q, k, v, out_gate, z_low, wg_f, bg_f, wg_b, bg_b, norm_g):
    B, S = q.shape[:2]
    f32 = jnp.float32

    def heads(t, d):
        return t.astype(f32).reshape(B, S, GLA_HEADS, d).transpose(0, 2, 1, 3)

    qh = heads(q, GLA_DK) * (GLA_DK ** -0.5)
    kh = heads(k, GLA_DK)
    vh = heads(v, GLA_DV)
    z = z_low.astype(f32)
    la_f = heads(jax.nn.log_sigmoid(z[..., :GLA_GATE_RANK] @ wg_f.astype(f32) + bg_f.astype(f32)) / GLA_TAU, GLA_DK)
    la_b = heads(jax.nn.log_sigmoid(z[..., GLA_GATE_RANK:] @ wg_b.astype(f32) + bg_b.astype(f32)) / GLA_TAU, GLA_DK)
    fwd = _gla_chunked(qh, kh, vh, la_f)
    flip = lambda t: jnp.flip(t, axis=2)
    bwd = flip(_gla_chunked(flip(qh), flip(kh), flip(vh), flip(la_b)))
    o = fwd + bwd
    o = o * lax.rsqrt(jnp.mean(o * o, axis=-1, keepdims=True) + NORM_EPS)
    o = o.transpose(0, 2, 1, 3).reshape(B, S, GLA_VAL_WIDTH) * norm_g.astype(f32)
    return (o * jax.nn.silu(out_gate.astype(f32))).astype(q.dtype)

def _moe(h, router_w, router_b, w1, b1, w2, b2):
    B, S, D = h.shape
    T = B * S
    xf = h.reshape(T, D)
    logits = (xf @ router_w + router_b).astype(jnp.float32)
    topv, topi = lax.top_k(logits, TOP_K)
    gates = jax.nn.softmax(topv, axis=-1)
    flat_e = topi.reshape(-1).astype(jnp.int32)
    flat_tok = jnp.broadcast_to(jnp.arange(T, dtype=jnp.int32)[:, None], (T, TOP_K)).reshape(-1)
    flat_g = gates.reshape(-1)
    order = jnp.argsort(flat_e)
    se = flat_e[order]
    counts = jnp.bincount(flat_e, length=N_EXPERTS)
    starts = jnp.cumsum(counts) - counts
    pcounts = (counts + MOE_BLOCK - 1) // MOE_BLOCK * MOE_BLOCK
    pends = jnp.cumsum(pcounts)
    pstarts = pends - pcounts
    dest = (pstarts[se] + jnp.arange(T * TOP_K, dtype=jnp.int32) - starts[se]).astype(jnp.int32)
    P = T * TOP_K + N_EXPERTS * MOE_BLOCK
    nblk = P // MOE_BLOCK
    buf_tok = jnp.zeros((P,), jnp.int32).at[dest].set(flat_tok[order])
    buf_gate = jnp.zeros((P,), jnp.float32).at[dest].set(flat_g[order])
    block_e = jnp.clip(jnp.searchsorted(pends, jnp.arange(nblk) * MOE_BLOCK, side='right'),
                       0, N_EXPERTS - 1).astype(jnp.int32)
    xin = xf[buf_tok].reshape(nblk, MOE_BLOCK, D)

    def expert_block(args):
        xb, e = args
        hh = xb @ w1[e] + b1[e]
        x_glu = jnp.minimum(hh[..., ::2], SWIGLU_LIMIT)
        x_lin = jnp.clip(hh[..., 1::2], -SWIGLU_LIMIT, SWIGLU_LIMIT)
        act = x_glu * jax.nn.sigmoid(SWIGLU_ALPHA * x_glu) * (x_lin + 1.0)
        return act @ w2[e] + b2[e]

    y = lax.map(expert_block, (xin, block_e)).reshape(P, D)
    out = jnp.zeros((T, D), jnp.float32).at[buf_tok].add(y.astype(jnp.float32) * buf_gate[:, None])
    return out.reshape(B, S, D).astype(h.dtype)

def setup_inputs(seed: int = 0) -> dict:
    key = jax.random.key(seed)
    ks = jax.random.split(key, 20)
    f32 = jnp.float32
    nrm = lambda k, shape, s: jax.random.normal(k, shape, f32) * s
    return {
        "x": nrm(ks[0], (BATCH, SEQ, D_MODEL), 1.0),
        "norm1_g": 1.0 + nrm(ks[1], (DEPTH, D_MODEL), 0.02),
        "w_in": nrm(ks[2], (DEPTH, D_MODEL, IN_WIDTH), D_MODEL ** -0.5),
        "rel_bias": nrm(ks[3], (T5_BUCKETS, ATTN_HEADS), 0.5),
        "gla_wg_fwd": nrm(ks[4], (DEPTH, GLA_GATE_RANK, GLA_KEY_WIDTH), GLA_GATE_RANK ** -0.5),
        "gla_bg_fwd": nrm(ks[5], (DEPTH, GLA_KEY_WIDTH), 0.1),
        "gla_wg_bwd": nrm(ks[6], (DEPTH, GLA_GATE_RANK, GLA_KEY_WIDTH), GLA_GATE_RANK ** -0.5),
        "gla_bg_bwd": nrm(ks[7], (DEPTH, GLA_KEY_WIDTH), 0.1),
        "gla_norm_g": 1.0 + nrm(ks[8], (DEPTH, GLA_VAL_WIDTH), 0.02),
        "w_out": nrm(ks[9], (DEPTH, MIX_WIDTH, D_MODEL), MIX_WIDTH ** -0.5),
        "norm2_g": 1.0 + nrm(ks[10], (DEPTH, D_MODEL), 0.02),
        "router_w": nrm(ks[11], (DEPTH, D_MODEL, N_EXPERTS), D_MODEL ** -0.5),
        "router_b": nrm(ks[12], (DEPTH, N_EXPERTS), 0.01),
        "moe_w1": nrm(ks[13], (DEPTH, N_EXPERTS, D_MODEL, 2 * D_FF), D_MODEL ** -0.5),
        "moe_b1": nrm(ks[14], (DEPTH, N_EXPERTS, 2 * D_FF), 0.01),
        "moe_w2": nrm(ks[15], (DEPTH, N_EXPERTS, D_FF, D_MODEL), D_FF ** -0.5),
        "moe_b2": nrm(ks[16], (DEPTH, N_EXPERTS, D_MODEL), 0.01),
        "final_g": 1.0 + nrm(ks[17], (D_MODEL,), 0.02),
    }

def reference(x, norm1_g, w_in, rel_bias, gla_wg_fwd, gla_bg_fwd, gla_wg_bwd, gla_bg_bwd,
              gla_norm_g, w_out, norm2_g, router_w, router_b, moe_w1, moe_b1, moe_w2, moe_b2,
              final_g):
    B, S, _ = x.shape
    split_pts = np.cumsum(IN_SPLITS)[:-1].tolist()
    for l in range(DEPTH):
        n = _rmsnorm(x, norm1_g[l])
        proj = n @ w_in[l]
        aq, ak, av, gq, gk, gv, gout, gz = jnp.split(proj, split_pts, axis=-1)
        hsplit = lambda t: t.reshape(B, S, ATTN_HEADS, ATTN_HEAD_DIM)
        a = _dilated_attention(hsplit(aq), hsplit(ak), hsplit(av), rel_bias)
        g = _bi_gla(gq, gk, gv, gout, gz, gla_wg_fwd[l], gla_bg_fwd[l],
                    gla_wg_bwd[l], gla_bg_bwd[l], gla_norm_g[l])
        x = x + jnp.concatenate([a, g], axis=-1) @ w_out[l]
        x = x + _moe(_rmsnorm(x, norm2_g[l]), router_w[l], router_b[l],
                     moe_w1[l], moe_b1[l], moe_w2[l], moe_b2[l])
    return _rmsnorm(x, final_g)


_drawn_inputs = setup_inputs


def setup_inputs(seed=0):
    import zlib

    import numpy as np

    out = dict(_drawn_inputs(seed))
    spreads = {}
    factors = {'moe_b1': 8.0, 'moe_b2': 8.0, 'final_g': 2.874}
    for name, (base, spread) in spreads.items():
        noise = np.random.default_rng([zlib.crc32(name.encode()), seed]).standard_normal(out[name].shape)
        drawn = base * np.exp(spread * noise) if base else spread * noise
        out[name] = __import__('jax').numpy.asarray(drawn.astype(out[name].dtype))
    for name, factor in factors.items():
        out[name] = (out[name] * factor).astype(out[name].dtype)
    return out
```

```python
from contextlib import ExitStack

import numpy as np

import concourse.bass as bass
from concourse import mybir

F32 = mybir.dt.float32
I32 = mybir.dt.int32
U32 = mybir.dt.uint32
ALU = mybir.AluOpType
ACT = mybir.ActivationFunctionType
AX = mybir.AxisListType

P = 128
D, SEQ = 1024, 512
NT, NK = SEQ // P, D // P
HA, DH = 8, 64
HG, DK, DV = 4, 64, 128
CH = 64
NCH = SEQ // CH
RANK, TAU = 16, 16.0
IN_W = 3104
OFF_AQ, OFF_AK, OFF_AV, OFF_GQK, OFF_GV, OFF_GO, OFF_GZ = 0, 512, 1024, 1536, 2048, 2560, 3072
EPS = 1e-5
E, TOPK, FF = 32, 4, 1024
NF = FF // P
LIMIT, ALPHA = 7.0, 1.702
SLOTS = 96
MAXB = E + SEQ * TOPK // SLOTS
COLS = MAXB + 2
ROWS = COLS * SLOTS
THR = (SEQ - 1) // SLOTS
PAD = 4 * SEQ * TOPK
NEG = -1e30
REL = 1024
TW = SEQ + 3 * P

CI, CU, CO, CIO, CTH = 0, 128, 256, 384, 448
NCF = CTH + THR
V1, V2, VB, VG, NV = 0, 8, 16, 20, 24


def shape_constants():
    cf = np.zeros((P, NCF), np.float32)
    cf[:, CI:CI + P] = np.eye(P)
    cf[:, CU:CU + P] = np.triu(np.ones((P, P)), 1)
    cf[:, CO:CO + P] = 1.0
    cf[:, CIO:CTH] = np.arange(CTH - CIO)
    cf[:, CTH:CTH + THR] = SLOTS * np.arange(1, THR + 1)
    s, c = np.arange(P)[:, None], np.arange(P)[None, :]
    same = s // CH == c // CH
    ci = np.zeros((P, 2 * P + NT * TOPK), np.int32)
    ci[:, 0:P] = same & (s <= c)
    ci[:, P:2 * P] = same & (s >= c)
    tok = np.arange(NT)[None, :, None] * P + np.arange(P)[:, None, None]
    ci[:, 2 * P:] = (tok * TOPK + np.arange(TOPK)).reshape(P, -1)
    rel = (SEQ - 1) - np.arange(REL)
    n = np.abs(rel)
    nb, exact = 16, 8
    large = exact + (np.log(np.maximum(n, 1).astype(np.float32) / exact)
                     / np.log(1024 / exact) * (nb - exact)).astype(np.int32)
    bucket = np.where(rel > 0, nb, 0) + np.where(n < exact, n, np.minimum(large, nb - 1))
    count = sum(((rel % d == 0) & (n <= 64 * d)).astype(np.int32) for d in (1, 4, 16))
    oh = np.zeros((33, REL), np.float32)
    oh[bucket, np.arange(REL)] = 1.0
    oh[32] = np.where(count > 0, np.log(np.maximum(count, 1).astype(np.float32)), NEG)
    return cf, ci, oh


def pre_jobs():
    jobs = [(("vec",), "v"), (("rel", 0), "v"), (("rel", 1), "a"), (("b1",), "v"), (("b2",), "a")]
    jobs += [(("nT", k), "va"[k % 2]) for k in range(NK)]
    jobs += [(("gqk", c), "a") for c in range(4)]
    jobs += [(("gz",), "v")] + [(("gate", i), "v") for i in range(4)]
    jobs += [(("gv", t), "a") for t in range(NT)] + [(("go", t), "a") for t in range(NT)]
    jobs += [(("aqk", c), "a") for c in range(8)] + [(("av", t), "a") for t in range(NT)]
    jobs += [(("kst", i), "a") for i in range(4)]
    jobs += [(("ds", i, par), "v") for i in range(4) for par in ((1, 0) if i < 2 else (0, 1))]
    for t in range(NT):
        jobs += [(("at", t, par), "v") for par in range(2)]
        if t:
            jobs += [(("o", t - 1, par), "a") for par in range(2)]
    jobs += [(("o", NT - 1, par), "a") for par in range(2)]
    for i in range(HA + 2):
        if i < HA:
            jobs += [(("s", i, t), "v") for t in range(NT)]
        if i == 0:
            jobs += [(("gT", h), "a") for h in range(HG)]
        if i >= 2:
            jobs += [(("pv", i - 2), "v")]
        if 1 <= i <= HA:
            jobs += [(("pt", i - 1, t), "va"[t % 2]) for t in range(NT)]
    jobs += [(("aT", c), "va"[c % 2]) for c in range(4)]
    jobs += [(("wo", t, n), "v") for t in range(NT) for n in range(2)]
    jobs += [(("hT", k), "va"[k % 2]) for k in range(NK)]
    jobs += [(("logit",), "v"), (("total",), "v"), (("rank",), "v")]
    return jobs


def encoder_block(nc, x, norm1_g, norm2_g, bg_f, bg_b, gla_g, w_in, rel_bias, wg_f, wg_b, w_out, router_w, router_b,
                  w1, b1, w2, b2, final_g, const_f, const_i, const_rel, out):
    ctx = ExitStack()

    def sem(name):
        return ctx.enter_context(nc.semaphore(name))

    ARENA = 24832
    FIXED = 28350
    arena = ctx.enter_context(nc.sbuf_tensor("arena", [P, ARENA], F32))
    fixed = ctx.enter_context(nc.sbuf_tensor("fixed", [P, FIXED], F32))

    def view(buf, at, *shape, parts=P, dt=F32):
        n = int(np.prod(shape))
        a = buf[0:parts, at:at + n]
        if dt is not F32:
            a = a.bitcast(dt)
        if len(shape) == 2:
            a = a.rearrange("p (a b) -> p a b", a=shape[0])
        if len(shape) == 3:
            a = a.rearrange("p (a b c) -> p a b c", a=shape[0], b=shape[1])
        return a

    R = [4096 * i for i in range(7)]
    win = {"gqk": view(arena, R[0], NK, 512), "gv": view(arena, R[1], NK, 512),
           "go": view(arena, R[2], NK, 512), "aq": view(arena, R[3], NK, 512),
           "ak": view(arena, R[4], NK, 512), "av": view(arena, R[5], NK, 512),
           "gz": view(arena, R[6], NK, 32)}
    gA, gT_ = view(arena, R[0], 4, 512), view(arena, R[0] + 2048, 4, 512)
    gB, QD = view(arena, R[1], 4, 512), view(arena, R[1] + 2048, 4, 512)
    KD, KS = view(arena, R[2], 4, 512), view(arena, R[2] + 2048, 4, 512)
    ST = view(arena, R[0], 4, NCH, DV)
    KN = view(arena, R[1], 4, NT, P)
    AB = view(arena, R[3], 4, 512)
    OS = view(arena, R[3] + 2048, NT, 512)
    WO = view(arena, R[4], NK, D)
    W1 = view(arena, 0, NK, 2 * FF)
    W2 = view(arena, R[4], NF, D)

    at = 0

    def take(n):
        nonlocal at
        at += n
        return at - n

    o_x, o_nt, o_qk, o_av = take(4096), take(4096), take(4096), take(2048)
    o_gqk, o_gv, o_go, o_zt = take(2048), take(2048), take(2048), take(512)
    o_t, o_a = take(4 * TW), take(2048)
    X = view(fixed, o_x, NT, D)
    NTt = view(fixed, o_nt, NK, SEQ)
    MIX = view(fixed, o_nt, NK, SEQ)
    XN = view(fixed, o_qk, NT, D)
    QK = view(fixed, o_qk, NK, SEQ)
    AV = view(fixed, o_av, NT, 512)
    SG = view(fixed, o_av, NT, 512)
    GQ, GK = view(fixed, o_gqk, 2, SEQ), view(fixed, o_gqk + 1024, 2, SEQ)
    GV, GO = view(fixed, o_gv, NT, 512), view(fixed, o_go, NT, 512)
    ZT = view(fixed, o_zt, SEQ, parts=32)
    LP = [view(fixed, o_gqk, NT, SEQ), view(fixed, o_gv, NT, SEQ)]
    PT = view(fixed, o_go, NT, NT, P)
    RELF = view(fixed, o_go, REL, parts=HA)
    OH = view(fixed, o_gv, REL, parts=33)
    TINIT = view(fixed, o_gqk, 2 * COLS, parts=SLOTS, dt=I32)
    TB = view(fixed, o_t, 4, TW)
    B1R, B2R = view(fixed, o_t, 2 * FF, parts=E), view(fixed, o_t + 2 * FF - 0, D, parts=E)
    AO = view(fixed, o_a, NT, 512)
    HN = view(fixed, o_qk, NT, D)
    HT = view(fixed, o_gqk, NK, SEQ)
    OHT = view(fixed, o_nt, NT * TOPK, E)
    OHV = view(fixed, o_nt + 512, NT * TOPK, E)
    MSEL = view(fixed, o_nt + 1024, NT, E)
    VAL = view(fixed, o_nt + 1152, NT, E)
    LG = view(fixed, o_nt + 1280, NT, E)
    MX = view(fixed, o_nt + 1408, NT, 8)
    IX = view(fixed, o_nt + 1440, NT, 8, dt=U32)
    IXF = view(fixed, o_nt + 1472, NT, 8)
    GT = view(fixed, o_nt + 1504, NT, TOPK)
    DE = view(fixed, o_nt + 1520, NT * TOPK)
    DEI = view(fixed, o_nt + 1536, NT * TOPK, dt=I32)
    ROW = view(fixed, o_nt + 1552, NT * TOPK, 2, dt=I32)
    CMP = view(fixed, o_nt + 1584, E, THR)
    NB = view(fixed, o_nt + 1744, E)
    BE = view(fixed, o_nt + 1776, E)
    BS = view(fixed, o_nt + 1808, E)
    EC = view(fixed, o_nt + 1840, MAXB, E, parts=1)
    EF = view(fixed, o_nt + 1840 + MAXB * E, MAXB, parts=1)
    g4 = view(fixed, o_nt + 1840 + MAXB * E + 64, NT, 1)
    XG = view(fixed, o_av, D, parts=SLOTS)
    XT = view(fixed, o_av + 1024, NK, SLOTS)
    HB = view(fixed, o_qk + 0, 2, 4, SLOTS)
    SGM = view(fixed, o_qk + 768, 2, 2, SLOTS)
    HG_ = view(fixed, o_qk + 1152, NF, SLOTS)
    YT = view(fixed, o_qk + 1920, NK, SLOTS)
    YN = view(fixed, o_gqk, D, parts=SLOTS)
    TAB = view(fixed, o_gqk + 1024, COLS, 2, parts=SLOTS, dt=I32)
    TABF = view(fixed, o_gqk + 1024, COLS, 2, parts=SLOTS)
    TOK = view(fixed, o_gqk + 1200, COLS, parts=SLOTS, dt=I32)
    GI = view(fixed, o_gqk + 1280, 1, parts=SLOTS, dt=I32)
    SI = view(fixed, o_gqk + 1281, 1, parts=SLOTS, dt=I32)
    GTC = view(fixed, o_gqk + 1282, 1, parts=SLOTS)
    BC = view(fixed, o_gqk + 1284, 24)
    FG = view(fixed, o_a, D)
    CF = view(fixed, take(NCF), NCF)
    CIt = view(fixed, take(2 * P + 16), 2 * P + 16, dt=I32)
    VT = view(fixed, take(NV), NV)
    BT = view(fixed, take(24 * E), 24, E)
    EG = view(fixed, take(32), 4, NCH)
    st4 = view(fixed, take(NT), NT)
    st16 = view(fixed, take(16), NT, HG)
    mx4 = view(fixed, take(8), 2, NT)
    den4 = view(fixed, take(16), 4, NT)
    rden = view(fixed, take(8), 2, NT)
    EMAP = view(fixed, take(64), 64, parts=1, dt=I32)
    RB = view(fixed, take(E), E)
    held = view(fixed, take(3), 3)
    RWs = view(fixed, o_t, NK, E)
    assert at <= FIXED, at
    VRW = view(fixed, o_zt, P, parts=NV)
    RX = view(fixed, o_zt + 128, HA, parts=33)
    WGt = view(fixed, o_t + 3 * FF, 2, 256, parts=32)
    JUNK = view(fixed, o_a, D)
    SCM = view(fixed, o_a, 512)
    ident = CF[:, CI:CI + P]
    ones = CF[:, CO:CO + P]
    above = CF[:, CU:CU + P]

    bank = [ctx.enter_context(nc.psum_tensor(f"bank{i}", [P, 512], F32)) for i in range(8)]

    rel_d = nc.dram_tensor("rel_d", [HA, REL], F32)
    hn_d = nc.dram_tensor("hn_d", [SEQ, D], F32)
    tab_d = nc.dram_tensor("tab_d", [ROWS, 2], I32)
    y_d = nc.dram_tensor("y_d", [SEQ * TOPK, D], F32)

    jobs = pre_jobs()
    index = {name: j for j, (name, _) in enumerate(jobs)}
    emptied = []
    count = {"v": 0, "a": 0}
    for _, e in jobs:
        count[e] += 1
        emptied.append(count[e])
    bank_full = sem("bank_full")
    bank_empty = {"v": sem("bank_empty_v"), "a": sem("bank_empty_a")}

    def bank_of(name):
        return bank[index[name] % 8]

    def wait_empty(eng, *names):
        most = {}
        for n in names:
            j = index[n]
            most[jobs[j][1]] = max(most.get(jobs[j][1], 0), emptied[j])
        for e, v in most.items():
            eng.wait_ge(bank_empty[e], v)

    def wait_full(eng, name):
        eng.wait_ge(bank_full, index[name] + 1)

    s_const, s_x, s_vec, s_oh, s_rel, s_braw, s_wg = (sem(n) for n in (
        "const_loaded", "x_loaded", "vec_loaded", "onehot_loaded", "relbias_loaded", "bias_loaded", "gatew_loaded"))
    s_win = {k: sem(f"win_{k}_loaded") for k in ("gqk", "gz", "gv", "go", "aq", "ak", "av")}
    s_relst, s_wo, s_rw = sem("rel_stored"), sem("wout_loaded"), sem("router_loaded")
    s_tb = [sem(f"toeplitz{i}_loaded") for i in range(4)]
    s_ms = sem("pool_memset")
    ch_v, ch_a = sem("vector_chain"), sem("scalar_chain")
    s_sq, s_sd, s_xn = sem("squares_summed"), sem("root_taken"), sem("x_normalized")
    s_var = sem("variance_ready")
    s_ln = sem("gate_log_ready")
    s_b, s_gd, s_ex, s_k = sem("decay_sum_ready"), sem("decay_rest_ready"), sem("decay_exp_ready"), sem("decayed_ready")
    s_sge, s_sgd = sem("gate_exp_ready"), sem("silu_ready")
    s_zero = sem("score_buffer_zero")
    s_os = sem("gla_out_ready")
    s_p, s_neg = sem("probs_ready"), sem("row_max_ready")
    s_hst = sem("h_stored")
    s_dt, s_dest = sem("dest_data_ready"), sem("dest_ready")
    s_exg, s_exr = sem("top_logits_ready"), sem("top_exp_ready")
    s_tinit, s_scat, s_tab, s_tabr = sem("table_cleared"), sem("table_written"), sem("table_loaded"), sem("table_ready")
    s_emap = sem("expert_map_ready")
    s_w1 = [sem(f"w1_slot{k}_loaded") for k in range(NK)]
    s_w2 = [sem(f"w2_slot{k}_loaded") for k in range(NF // 2)]
    s_used = sem("weight_slot_used")
    s_idx, s_gath, s_yst = sem("indices_copied"), sem("tokens_gathered"), sem("y_stored")
    s_xtp, s_xt = sem("x_transposed"), sem("xt_ready")
    s_hf, s_sig, s_act = sem("hidden_full"), sem("sigmoid_ready"), sem("act_ready")
    s_gi = sem("glu_input_ready")
    s_yf, s_yt, s_ytp, s_yn = sem("y_full"), sem("yt_ready"), sem("y_transposed"), sem("y_ready")
    s_yl = [sem(f"y_rows{t}_loaded") for t in range(NT)]
    s_acc, s_fin, s_out, s_fg = sem("sum_ready"), sem("final_ready"), sem("out_stored"), sem("final_g_loaded")

    PE_PER_BLOCK = NK + NF // 2
    STEPS = 13
    s_sum = sem("final_chain")

    block = ctx.enter_context(nc.Block())

    @block.sync
    def _(sp):
        sp.dma_start(CF, const_f).then_inc(s_const, 16)
        sp.dma_start(X, x.rearrange("(t p) d -> p t d", p=P)).then_inc(s_x, 16)
        for src, at_row in ((norm1_g, V1), (norm2_g, V2), (bg_f, VB), (bg_b, VB + 2), (gla_g, VG)):
            sp.dma_start(VRW[at_row:at_row + src.shape[0], :], src).then_inc(s_vec, 16)
        wv = w_in.rearrange("(k p) n -> p k n", p=P)
        for name, off, w in (("gqk", OFF_GQK, 512), ("gz", OFF_GZ, 32), ("gv", OFF_GV, 512),
                             ("go", OFF_GO, 512), ("aq", OFF_AQ, 512), ("ak", OFF_AK, 512),
                             ("av", OFF_AV, 512)):
            sp.dma_start(win[name], wv[:, :, off:off + w]).then_inc(s_win[name], 16)
        wait_full(sp, ("av", NT - 1))
        sp.dma_start(WO, w_out.rearrange("(k p) n -> p k n", p=P)).then_inc(s_wo, 16)
        wait_empty(sp, *[("gT", h) for h in range(HG)])
        for k in range(NK):
            sp.dma_start(W1[:, k, :], w1[0, k * P:(k + 1) * P, :]).then_inc(s_w1[k], 16)
        wait_full(sp, ("wo", NT - 1, 1))
        for f in range(NF // 2):
            sp.dma_start(W2[:, 2 * f:2 * f + 2, :],
                         w2[0, 2 * f * P:(2 * f + 2) * P, :].rearrange("(a p) n -> p a n", p=P)).then_inc(s_w2[f], 16)
        sp.wait_ge(s_emap, 1)
        blocks = sp.value_load(EMAP[0:1, MAXB:MAXB + 1], min_val=E, max_val=MAXB)
        with sp.Fori(1, blocks) as g:
            e = sp.value_load(EMAP[0:1, bass.ds(g, 1)], min_val=0, max_val=E - 1)
            for k in range(NK):
                sp.wait_ge(s_used, PE_PER_BLOCK * g - PE_PER_BLOCK + k + 1)
                sp.dma_start(W1[:, k, :],
                             w1[bass.ds(e, 1), k * P:(k + 1) * P, :].rearrange("e p n -> (e p) n")
                             ).then_inc(s_w1[k], 16)
            for f in range(NF // 2):
                sp.wait_ge(s_used, PE_PER_BLOCK * g - PE_PER_BLOCK + NK + f + 1)
                sp.dma_start(W2[:, 2 * f:2 * f + 2, :],
                             w2[bass.ds(e, 1), 2 * f * P:(2 * f + 2) * P, :].rearrange("e (a p) n -> p (e a) n", p=P)
                             ).then_inc(s_w2[f], 16)
        nb = sp.value_load(EMAP[0:1, MAXB:MAXB + 1], min_val=E, max_val=MAXB)
        sp.wait_ge(s_used, PE_PER_BLOCK * nb)
        sp.wait_ge(s_yst, 16 * nb + 16)
        yv = y_d.ap().rearrange("(t p k) d -> t p (k d)", p=P, k=TOPK)
        for t in range(NT):
            sp.dma_start(view(arena, 4096 * t, TOPK * D), yv[t]).then_inc(s_yl[t], 16)
        for t in range(NT):
            sp.wait_ge(s_fin, t + 1)
            sp.dma_start(out[t * P:(t + 1) * P, :], X[:, t, :]).then_inc(s_out, 16)
        sp.wait_ge(s_out, 16 * NT)

    @block.tensor
    def _(pe):
        done = [0]

        def begin(name):
            j = index[name]
            assert j == done[0], (name, jobs[done[0]])
            done[0] += 1
            if j >= 8:
                pe.wait_ge(bank_empty[jobs[j - 8][1]], emptied[j - 8])
            return bank[j % 8]

        def full(ins):
            ins.then_inc(bank_full, 1)

        pe.wait_ge(s_const, 32)
        pe.wait_ge(s_vec, 16 * 5)
        b = begin(("vec",))
        full(pe.transpose(b[:, 0:NV], VRW, ident[0:NV, 0:NV]))
        pe.wait_ge(s_oh, 16)
        pe.wait_ge(s_rel, 16)
        for i in range(2):
            b = begin(("rel", i))
            full(pe.matmul(b[0:HA, :], RX, OH[:, 512 * i:512 * (i + 1)], start=True, stop=True))
        pe.wait_ge(s_braw, 32)
        b = begin(("b1",))
        for j in range(2 * NF):
            m = pe.transpose(b[:, j * E:(j + 1) * E], B1R[:, bass.ds(j // 2 * 256 + j % 2, P, 2)], ident[0:E, 0:E])
        full(m)
        b = begin(("b2",))
        for j in range(NK):
            m = pe.transpose(b[:, j * E:(j + 1) * E], B2R[:, j * P:(j + 1) * P], ident[0:E, 0:E])
        full(m)
        for k in range(NK):
            b = begin(("nT", k))
            for t in range(NT):
                if k == 0:
                    pe.wait_ge(s_xn, t + 1)
                m = pe.transpose(b[:, t * P:(t + 1) * P], XN[:, t, k * P:(k + 1) * P], ident)
            full(m)
        wait_empty(pe, *[("nT", k) for k in range(NK)])

        def features(name, w, c):
            b = begin(name)
            for k in range(NK):
                m = pe.matmul(b[:, :], w[:, k, c * P:(c + 1) * P], NTt[:, k, :], start=k == 0, stop=k == NK - 1)
            full(m)

        def tokens(name, w, t):
            b = begin(name)
            for k in range(NK):
                m = pe.matmul(b[:, :], NTt[:, k, t * P:(t + 1) * P], w[:, k, :], start=k == 0, stop=k == NK - 1)
            full(m)

        pe.wait_ge(s_win["gqk"], 16)
        for c in range(4):
            features(("gqk", c), win["gqk"], c)
        pe.wait_ge(s_win["gz"], 16)
        b = begin(("gz",))
        for k in range(NK):
            m = pe.matmul(b[0:32, :], win["gz"][:, k, :], NTt[:, k, :], start=k == 0, stop=k == NK - 1)
        full(m)
        wait_empty(pe, ("gz",))
        pe.wait_ge(s_wg, 32)
        for i in range(4):
            b = begin(("gate", i))
            full(pe.matmul(b[:, :], WGt[:, i // 2, (i % 2) * P:(i % 2 + 1) * P], ZT, start=True, stop=True))
        for name in ("gv", "go"):
            pe.wait_ge(s_win[name], 16)
            for t in range(NT):
                tokens((name, t), win[name], t)
        for c in range(8):
            if c % 4 == 0:
                pe.wait_ge(s_win["aq" if c < 4 else "ak"], 16)
            features(("aqk", c), win["aq" if c < 4 else "ak"], c % 4)
        pe.wait_ge(s_win["av"], 16)
        for t in range(NT):
            tokens(("av", t), win["av"], t)

        for i in range(4):
            pe.wait_ge(s_k, i + 1)
            b = begin(("kst", i))
            for t in range(NT):
                m = pe.transpose(b[:, t * P:(t + 1) * P], KS[:, i, t * P:(t + 1) * P], ident)
            full(m)
        for i in range(4):
            wait_empty(pe, ("kst", i))
            for par in ((1, 0) if i < 2 else (0, 1)):
                b = begin(("ds", i, par))
                r = slice(CH * par, CH * par + CH)
                for t in range(NT):
                    for hh in range(2):
                        h = 2 * (i % 2) + hh
                        m = pe.matmul(b[DK * hh:DK * hh + DK, t * DV:(t + 1) * DV],
                                      KN[r, i, t, DK * hh:DK * hh + DK], GV[r, t, h * DV:(h + 1) * DV],
                                      start=True, stop=True)
                full(m)

        def scores(t):
            for par in range(2):
                b = begin(("at", t, par))
                r = slice(DK * par, DK * par + DK)
                for fc in range(2):
                    for d in range(2):
                        i = 2 * d + fc
                        n = 2 * fc + d
                        m = pe.matmul(b[:, n * P:(n + 1) * P], KD[r, i, t * P:(t + 1) * P],
                                      QD[r, i, t * P:(t + 1) * P], start=True, stop=True)
                full(m)

        def gla_out(t):
            wait_empty(pe, ("at", t, 1))
            if t == 0:
                wait_empty(pe, ("ds", 3, 1))
            for par in range(2):
                b = begin(("o", t, par))
                r = slice(DK * par, DK * par + DK)
                for fc in range(2):
                    col = slice(fc * DV, (fc + 1) * DV)
                    h = 2 * fc + par
                    for d in range(2):
                        slot = 2 * fc + d
                        m = pe.matmul(b[:, col], AB[:, 2 * (t % 2) + par, slot * P:(slot + 1) * P],
                                      GV[:, t, h * DV:(h + 1) * DV], start=d == 0, stop=False, skip_group_check=True)
                    parts = [(d, half) for d in range(2) for half in range(2)
                             if (d, 2 * t + half) not in ((0, 0), (1, NCH - 1))]
                    for q, (d, half) in enumerate(parts):
                        i, n = 2 * d + fc, 2 * t + half
                        m = pe.matmul(b[CH * half:CH * half + CH, col], QD[r, i, n * CH:(n + 1) * CH],
                                      ST[r, i, n, :], start=False, stop=q == len(parts) - 1, skip_group_check=True)
                full(m)

        for t in range(NT):
            scores(t)
            if t:
                gla_out(t - 1)
        gla_out(NT - 1)

        for i in range(HA + 2):
            if i < HA:
                r = slice(DH * (i % 2), DH * (i % 2) + DH)
                for t in range(NT):
                    b = begin(("s", i, t))
                    full(pe.matmul(b[:, :], QK[r, i // 2, t * P:(t + 1) * P], QK[r, 4 + i // 2, :],
                                   start=True, stop=True))
            if i == 0:
                for h in range(HG):
                    b = begin(("gT", h))
                    for t in range(NT):
                        if h == 0:
                            pe.wait_ge(s_os, t + 1)
                        m = pe.transpose(b[:, t * P:(t + 1) * P], OS[:, t, h * DV:(h + 1) * DV], ident)
                    full(m)
            if i >= 2:
                h = i - 2
                wait_empty(pe, *[("pt", h, t) for t in range(NT)])
                b = begin(("pv", h))
                for t in range(NT):
                    for kb in range(NT):
                        m = pe.matmul(b[:, t * DH:(t + 1) * DH], PT[:, t, kb, :],
                                      AV[:, kb, h * DH:(h + 1) * DH], start=kb == 0, stop=kb == NT - 1)
                full(m)
            if 1 <= i <= HA:
                h = i - 1
                for t in range(NT):
                    pe.wait_ge(s_p, NT * h + t + 1)
                    b = begin(("pt", h, t))
                    for kb in range(NT):
                        m = pe.transpose(b[:, kb * P:(kb + 1) * P], LP[h % 2][:, t, kb * P:(kb + 1) * P], ident)
                    full(m)
        wait_empty(pe, ("pv", HA - 1))
        for c in range(4):
            b = begin(("aT", c))
            for t in range(NT):
                m = pe.transpose(b[:, t * P:(t + 1) * P], AO[:, t, c * P:(c + 1) * P], ident)
            full(m)
        wait_empty(pe, *[("aT", c) for c in range(4)], *[("gT", h) for h in range(HG)])
        pe.wait_ge(s_wo, 16)
        for t in range(NT):
            for n in range(2):
                b = begin(("wo", t, n))
                for k in range(NK):
                    m = pe.matmul(b[:, :], MIX[:, k, t * P:(t + 1) * P], WO[:, k, n * 512:(n + 1) * 512],
                                  start=k == 0, stop=k == NK - 1)
                full(m)
        for k in range(NK):
            b = begin(("hT", k))
            for t in range(NT):
                if k == 0:
                    pe.wait_ge(s_xn, NT + t + 1)
                m = pe.transpose(b[:, t * P:(t + 1) * P], HN[:, t, k * P:(k + 1) * P], ident)
            full(m)
        wait_empty(pe, *[("hT", k) for k in range(NK)])
        pe.wait_ge(s_rw, 32)
        b = begin(("logit",))
        for t in range(NT):
            for k in range(NK):
                m = pe.matmul(b[:, t * E:(t + 1) * E], HT[:, k, t * P:(t + 1) * P], RWs[:, k, :],
                              start=k == 0, stop=k == NK - 1)
        full(m)
        pe.wait_ge(s_dt, 1)
        b = begin(("total",))
        for t in range(NT):
            m = pe.matmul(b[:, 0:E], ones, MSEL[:, t, :], start=t == 0, stop=t == NT - 1)
        full(m)
        b = begin(("rank",))
        for t in range(NT):
            for u in range(t + 1):
                m = pe.matmul(b[:, t * E:(t + 1) * E], above if u == t else ones, MSEL[:, u, :],
                              start=u == 0, stop=u == t)
        full(m)
        assert done[0] == len(jobs)

        hid, yb, tb = bank[0:4], bank[4:6], bank[6:8]

        def x_transposes(n):
            pe.wait_ge(s_gath, n)
            for q in range(2):
                for c in range(4):
                    k = 4 * q + c
                    m = pe.transpose(tb[q][:, c * SLOTS:(c + 1) * SLOTS], XG[:, k * P:(k + 1) * P],
                                     ident[0:SLOTS, 0:SLOTS])
                m.then_inc(s_xtp, 1)

        def y_transposes():
            for q in range(2):
                for c in range(4):
                    k = 4 * q + c
                    m = pe.transpose(tb[q][0:SLOTS, c * P:(c + 1) * P], YT[:, k, :], ident)
                m.then_inc(s_ytp, 1)

        wait_empty(pe, ("logit",), ("rank",), ("total",), ("hT", 7), ("hT", 6))
        x_transposes(16)
        blocks = pe.value_load(EMAP[0:1, MAXB:MAXB + 1], min_val=E, max_val=MAXB)
        with pe.Fori(0, blocks) as g:
            pe.wait_ge(s_xt, 2 * g + 2)
            for k in range(NK):
                pe.wait_ge(s_w1[k], 16 * g + 16)
                for j in range(2 * NF):
                    f, lin = j // 2, j % 2
                    m = pe.matmul(hid[j // 4][:, (j % 4) * SLOTS:(j % 4 + 1) * SLOTS],
                                  W1[:, k, bass.ds(f * 256 + lin, P, 2)], XT[:, k, :],
                                  start=k == 0 and j % 4 == 0, stop=k == NK - 1, skip_group_check=True)
                    if k == NK - 1 and j % 4 == 3 and j < 2 * NF - 1:
                        m.then_inc(s_hf, 1)
                m.then_inc(s_used, 1)
                if k == 0:
                    pe.wait_ge(s_yt, 2 * g + 2)
                    y_transposes()
            pe.wait_ge(s_yn, 2 * g + 2)
            x_transposes(16 * g + 32)
            for f in range(NF):
                if f % 2 == 0:
                    pe.wait_ge(s_w2[f // 2], 16 * g + 16)
                    pe.wait_ge(s_act, 4 * g + f // 2 + 1)
                for c in range(NK):
                    m = pe.matmul(yb[c // 4][:, (c % 4) * SLOTS:(c % 4 + 1) * SLOTS],
                                  W2[:, f, c * P:(c + 1) * P], HG_[:, f, :],
                                  start=f == 0 and c % 4 == 0, stop=f == NF - 1, skip_group_check=True)
                    if f == NF - 1 and c == 3:
                        m.then_inc(s_yf, 1)
                if f % 2:
                    m.then_inc(s_used, 1)
        nb = pe.value_load(EMAP[0:1, MAXB:MAXB + 1], min_val=E, max_val=MAXB)
        pe.wait_ge(s_yt, 2 * nb + 2)
        pe.wait_ge(s_xt, 2 * nb + 2)
        y_transposes()

    @block.gpsimd
    def _(pool):
        pool.memset(held, 0.0)
        pool.memset(RX, 1.0).then_inc(s_ms, 1)
        pool.memset(WGt, 0.0).then_inc(s_ms, 1)
        pool.wait_ge(s_ms, 2)
        pool.dma_start(RX[0:E, :], rel_bias).then_inc(s_rel, 16)
        pool.dma_start(WGt[0:RANK, 0, :], wg_f).then_inc(s_wg, 16)
        pool.dma_start(WGt[RANK:2 * RANK, 1, :], wg_b).then_inc(s_wg, 16)
        pool.memset(TINIT, PAD).then_inc(s_ms, 1)
        pool.wait_ge(s_ms, 3)
        pool.dma_start(tab_d.ap().rearrange("(a b) c -> a (b c)", a=SLOTS), TINIT).then_inc(s_tinit, 16)
        pool.wait_ge(s_sq, NT)
        pool.memset(AO[:, 0:2, :], 1.0).then_inc(s_ms, 1)
        pool.wait_ge(s_ms, 4)
        pool.memset(AO[:, 0, bass.ds(0, NCH, CH)], 0.0).then_inc(s_ms, 1)
        pool.memset(AO[:, 1, bass.ds(CH - 1, NCH, CH)], 0.0).then_inc(s_ms, 1)
        wait_full(pool, ("aqk", 3))
        pool.memset(AB, 0.0).then_inc(s_zero, 1)

        def hold():
            pool.tensor_tensor(held[:, 2:3], held[:, 0:1], held[:, 1:2], ALU.add)

        last_slot, last_token, last_row = (pool.to_reg(n - 1) for n in (ROWS, SEQ, SEQ * TOPK))
        pool.wait_ge(s_tinit, 16)
        pool.wait_ge(s_dest, 1)
        for c in range(NT * TOPK):
            pool.indirect_dma_start(out=tab_d.ap(), out_offset=bass.IndirectOffsetOnAxis(DEI[:, c:c + 1], 0),
                                    in_=ROW[:, c, :], in_offset=None,
                                    bounds_check=last_slot, oob_is_err=False).then_inc(s_scat, 16)
        pool.wait_ge(s_scat, 16 * NT * TOPK)
        wait_full(pool, ("logit",))
        pool.dma_start(TAB, tab_d.ap().rearrange("(g s) c -> s g c", s=SLOTS)).then_inc(s_tab, 16)
        pool.wait_ge(s_tabr, 1)
        pool.memset(XG, 0.0).then_inc(s_idx, 1)
        pool.tensor_copy(GI, TOK[:, 1:2]).then_inc(s_idx, 1)
        pool.wait_ge(s_idx, 2)
        pool.wait_ge(s_hst, 16)
        pool.indirect_dma_start(out=XG, out_offset=None, in_=hn_d.ap(),
                                in_offset=bass.IndirectOffsetOnAxis(GI, 0),
                                bounds_check=last_token, oob_is_err=False).then_inc(s_gath, 16)
        blocks = pool.value_load(EMAP[0:1, MAXB:MAXB + 1], min_val=E, max_val=MAXB)
        with pool.Fori(0, blocks) as g:
            pool.wait_ge(s_gath, 16 * g + 16)
            pool.wait_ge(s_xtp, 2 * g + 2)
            pool.tensor_copy(GI, TOK[:, bass.ds(g + 2, 1)]).then_inc(s_idx, 1)
            pool.wait_ge(s_idx, 2 * g + 3)
            hold()
            pool.indirect_dma_start(out=XG, out_offset=None, in_=hn_d.ap(),
                                    in_offset=bass.IndirectOffsetOnAxis(GI, 0),
                                    bounds_check=last_token, oob_is_err=False).then_inc(s_gath, 16)
            pool.wait_ge(s_yn, 2 * g + 2)
            pool.tensor_copy(SI, TAB[:, bass.ds(g, 1), 0]).then_inc(s_idx, 1)
            pool.wait_ge(s_idx, 2 * g + 4)
            hold()
            pool.indirect_dma_start(out=y_d.ap(), out_offset=bass.IndirectOffsetOnAxis(SI, 0),
                                    in_=YN, in_offset=None,
                                    bounds_check=last_row, oob_is_err=False).then_inc(s_yst, 16)
            pool.wait_ge(s_yst, 16 * g + 16)
        nb = pool.value_load(EMAP[0:1, MAXB:MAXB + 1], min_val=E, max_val=MAXB)
        pool.wait_ge(s_gath, 16 * nb + 16)
        pool.wait_ge(s_yn, 2 * nb + 2)
        pool.tensor_copy(SI, TAB[:, bass.ds(nb, 1), 0]).then_inc(s_idx, 1)
        pool.wait_ge(s_idx, 2 * nb + 3)
        hold()
        pool.indirect_dma_start(out=y_d.ap(), out_offset=bass.IndirectOffsetOnAxis(SI, 0),
                                in_=YN, in_offset=None,
                                bounds_check=last_row, oob_is_err=False).then_inc(s_yst, 16)
        pool.wait_ge(s_yst, 16 * nb + 16)

    @block.scalar
    def _(act):
        chain = [0]

        def link(ins):
            chain[0] += 1
            ins.then_inc(ch_a, 1)
            act.wait_ge(ch_a, chain[0])

        def emptied_by(ins):
            ins.then_inc(bank_empty["a"], 1)

        def plain(name, dst, scale=1.0):
            wait_full(act, name)
            emptied_by(act.activation(dst, bank_of(name)[:, :], ACT.Copy, scale=scale))

        act.dma_start(CIt, const_i).then_inc(s_const, 16)
        act.dma_start(OH, const_rel).then_inc(s_oh, 16)
        act.dma_start(B1R, b1).then_inc(s_braw, 16)
        act.dma_start(B2R, b2).then_inc(s_braw, 16)
        act.wait_ge(s_x, 16)
        for t in range(NT):
            if t:
                act.wait_ge(s_sq, t)
            act.activation(JUNK, X[:, t, :], ACT.Square, accum_out=st4[:, t:t + 1]).then_inc(s_sq, 1)
        act.wait_ge(s_var, 1)
        act.activation(st4, st4, ACT.Sqrt).then_inc(s_sd, 1)
        wait_full(act, ("rel", 1))
        emptied_by(act.activation(RELF[:, 512:1024], bank_of(("rel", 1))[0:HA, :], ACT.Copy))
        wait_empty(act, ("rel", 0), ("rel", 1))
        act.dma_start(rel_d.ap(), RELF).then_inc(s_relst, 16)
        wait_full(act, ("b2",))
        emptied_by(act.activation(BT[:, 2 * NF:24, :], bank_of(("b2",))[:, 0:NK * E].rearrange("p (a b) -> p a b", b=E), ACT.Copy))
        wait_empty(act, ("vec",))
        for k in range(1, NK, 2):
            plain(("nT", k), NTt[:, k, :], VT[:, V1 + k:V1 + k + 1])
        act.wait_ge(s_tinit, 16)
        for c in range(4):
            plain(("gqk", c), (GQ if c < 2 else GK)[:, c % 2, :], 0.125 if c < 2 else 1.0)
        for i in range(4):
            wait_empty(act, ("gate", i))
            link(act.activation(gT_[:, i, :], gA[:, i, :], ACT.Abs))
            link(act.activation(gT_[:, i, :], gT_[:, i, :], ACT.Exp, scale=-1.0))
            act.activation(gT_[:, i, :], gT_[:, i, :], ACT.Ln, bias=1.0).then_inc(s_ln, 1)
        wait_full(act, ("rel", 1))
        act.wait_ge(s_relst, 16)
        wait_empty(act, ("b1",), ("b2",))
        wait_full(act, ("gate", 3))
        for h in range(4):
            act.dma_start(TB[:, h, :], bass.AP(rel_d, h * REL, [[1, P], [1, TW]])).then_inc(s_tb[h], 16)
        for t in range(NT):
            plain(("gv", t), GV[:, t, :])
        for t in range(NT):
            plain(("go", t), GO[:, t, :])
        wait_empty(act, ("go", NT - 1))
        for t in range(NT):
            act.activation(SG[:, t, :], GO[:, t, :], ACT.Exp, scale=-1.0).then_inc(s_sge, 1)
        for i in range(4):
            act.wait_ge(s_b, i + 1)
            act.wait_ge(s_gd, i + 1)
            first = 0 if i >= 2 else CH - 1
            act.activation(EG[:, i, :], gB[:, i, bass.ds(first, NCH, CH)], ACT.Exp, scale=1.0 / TAU).then_inc(s_ex, 1)
            act.activation(QD[:, i, :], gB[:, i, :], ACT.Exp, scale=1.0 / TAU).then_inc(s_ex, 1)
            act.activation(KD[:, i, :], gB[:, i, :], ACT.Exp, scale=-1.0 / TAU).then_inc(s_ex, 1)
            act.activation(KS[:, i, :], KS[:, i, :], ACT.Exp, scale=1.0 / TAU).then_inc(s_ex, 1)
        for c in range(8):
            plain(("aqk", c), QK[:, c, :], 0.125 if c < 4 else 1.0)
        act.wait_ge(s_sgd, NT)
        for t in range(NT):
            plain(("av", t), AV[:, t, :])
        for i in range(4):
            wait_full(act, ("kst", i))
            emptied_by(act.activation(KN[:, i, :, :], bank_of(("kst", i))[:, :].rearrange("p (a b) -> p a b", b=P), ACT.Copy))
        for t in range(NT):
            for par in range(2):
                wait_full(act, ("o", t, par))
                emptied_by(act.activation(OS[:, t, :].rearrange("p (f q e) -> p q f e", f=2, q=2)[:, par, :, :],
                                          bank_of(("o", t, par))[:, 0:256].rearrange("p (f e) -> p f e", f=2), ACT.Copy))
        act.wait_ge(s_var, 2)
        act.activation(st16, st16, ACT.Sqrt).then_inc(s_sd, 1)

        def probs(h):
            act.wait_ge(s_neg, h + 1)
            if h >= 2:
                wait_empty(act, ("pt", h - 2, NT - 1))
            for t in range(NT):
                act.activation(LP[h % 2][:, t, :], LP[h % 2][:, t, :], ACT.Exp, bias=mx4[:, h % 2, t:t + 1],
                               accum_out=den4[:, h % 4, t:t + 1]).then_inc(s_p, 1)
            if h < 4:
                act.dma_start(TB[:, h, :], bass.AP(rel_d, (h + 4) * REL, [[1, P], [1, TW]])
                              ).then_inc(s_tb[h], 16)

        for i in range(HA + 2):
            if i == 0:
                for h in range(HG):
                    plain(("gT", h), MIX[:, 4 + h, :], VT[:, VG + h:VG + h + 1])
            if i < HA:
                probs(i)
            if 1 <= i <= HA:
                h = i - 1
                for t in (1, 3):
                    wait_full(act, ("pt", h, t))
                    emptied_by(act.activation(PT[:, t, :, :], bank_of(("pt", h, t))[:, :].rearrange("p (a b) -> p a b", b=P), ACT.Copy))
        for c in (1, 3):
            plain(("aT", c), MIX[:, c, :])
        wait_full(act, ("s", HA - 1, NT - 1))
        act.wait_ge(s_neg, HA)
        act.dma_start(RWs, router_w.rearrange("(k p) e -> p k e", p=P)).then_inc(s_rw, 16)
        act.dma_start(RB, bass.AP(router_b.tensor, 0, [[0, P], [1, E]])).then_inc(s_rw, 16)
        wait_full(act, ("aT", 3))
        for t in range(NT):
            wait_empty(act, ("wo", t, 1))
            act.activation(JUNK, X[:, t, :], ACT.Square, accum_out=st4[:, t:t + 1]).then_inc(s_sq, 1)
            act.wait_ge(s_var, 3 + t)
            act.activation(st4[:, t:t + 1], st4[:, t:t + 1], ACT.Sqrt).then_inc(s_sd, 1)
        act.wait_ge(s_xn, 2 * NT)
        act.dma_start(hn_d.ap().rearrange("(t p) d -> p t d", p=P), HN).then_inc(s_hst, 16)
        for k in range(1, NK, 2):
            plain(("hT", k), HT[:, k, :], VT[:, V2 + k:V2 + k + 1])
        act.wait_ge(s_exg, 1)
        act.activation(GT, GT, ACT.Exp).then_inc(s_exr, 1)
        act.dma_start(FG, bass.AP(final_g.tensor, 0, [[0, P], [1, D]])).then_inc(s_fg, 16)

        act.wait_ge(s_emap, 1)
        blocks = act.value_load(EMAP[0:1, MAXB:MAXB + 1], min_val=E, max_val=MAXB)
        with act.Fori(0, blocks) as g:
            act.wait_ge(s_idx, 2 * g + 3)
            act.wait_ge(s_gi, 5 * g + 1)
            for q in range(2):
                act.wait_ge(s_ytp, 2 * g + q + 1)
                act.activation(YN[:, q * 512:(q + 1) * 512], bank[6 + q][0:SLOTS, :], ACT.Copy,
                               scale=GTC).then_inc(s_yn, 1)
            for q in range(4):
                act.wait_ge(s_gi, 5 * g + 2 + q)
                act.activation(SGM[:, q % 2, :, :], HB[:, q % 2, 0:4:2, :], ACT.Sigmoid,
                               scale=ALPHA).then_inc(s_sig, 1)
        nb = act.value_load(EMAP[0:1, MAXB:MAXB + 1], min_val=E, max_val=MAXB)
        act.wait_ge(s_yst, 16 * nb)
        act.wait_ge(s_gi, 5 * nb + 1)
        for q in range(2):
            act.wait_ge(s_ytp, 2 * nb + q + 1)
            act.activation(YN[:, q * 512:(q + 1) * 512], bank[6 + q][0:SLOTS, :], ACT.Copy,
                           scale=GTC).then_inc(s_yn, 1)
        for t in range(NT):
            act.wait_ge(s_acc, t + 1)
            act.activation(view(fixed, o_nt, D), X[:, t, :], ACT.Square,
                           accum_out=st4[:, t:t + 1]).then_inc(s_sq, 1)
            act.wait_ge(s_var, 7 + t)
            act.activation(st4[:, t:t + 1], st4[:, t:t + 1], ACT.Sqrt).then_inc(s_sd, 1)

    @block.vector
    def _(v):
        chain = [0]

        def link(ins):
            chain[0] += 1
            ins.then_inc(ch_v, 1)
            v.wait_ge(ch_v, chain[0])

        def emptied_by(ins):
            ins.then_inc(bank_empty["v"], 1)

        def chunks(a):
            return a.rearrange("p (n c) -> p n c", c=CH)

        def bcast(a, n):
            return a.unsqueeze(len(a.shape)).to_broadcast([*a.shape, n])

        def inv_root(stat, n, nth, k):
            v.tensor_scalar(stat, stat, 1.0 / k, EPS, ALU.mult, ALU.add).then_inc(s_var, 1)
            v.wait_ge(s_sd, nth)
            link(v.reciprocal(stat, stat))

        v.wait_ge(s_const, 32)
        wait_full(v, ("vec",))
        emptied_by(v.tensor_copy(VT, bank_of(("vec",))[:, 0:NV]))
        wait_full(v, ("rel", 0))
        emptied_by(v.tensor_copy(RELF[:, 0:512], bank_of(("rel", 0))[0:HA, :]))
        wait_full(v, ("b1",))
        emptied_by(v.tensor_copy(BT[:, 0:2 * NF, :], bank_of(("b1",))[:, :].rearrange("p (a b) -> p a b", b=E)))
        v.wait_ge(s_sq, NT)
        inv_root(st4, NT, 1, D)
        for t in range(NT):
            v.tensor_scalar(XN[:, t, :], X[:, t, :], st4[:, t:t + 1], None, ALU.mult).then_inc(s_xn, 1)
        wait_empty(v, ("vec",))
        for k in range(0, NK, 2):
            wait_full(v, ("nT", k))
            emptied_by(v.tensor_scalar(NTt[:, k, :], bank_of(("nT", k))[:, :], VT[:, V1 + k:V1 + k + 1], None, ALU.mult))
        wait_full(v, ("gz",))
        emptied_by(v.tensor_copy(ZT, bank_of(("gz",))[0:32, :]))
        for i in range(4):
            wait_full(v, ("gate", i))
            emptied_by(v.tensor_scalar(gA[:, i, :], bank_of(("gate", i))[:, :], VT[:, VB + i:VB + i + 1], None,
                                       ALU.add))
        v.wait_ge(s_ms, 6)
        wait_full(v, ("go", NT - 1))
        for i in range(4):
            v.wait_ge(s_ln, i + 1)
            link(v.scalar_tensor_tensor(gA[:, i, :], gA[:, i, :], 0.0, gT_[:, i, :], ALU.min, ALU.subtract))
            rev = slice(None, None, -1 if i >= 2 else 1)
            v.tensor_tensor_scan(gB[:, i, rev], AO[:, i // 2, rev], gA[:, i, rev], 0.0,
                                 ALU.mult, ALU.add).then_inc(s_b, 1)
            v.wait_ge(s_b, i + 1)
            first = 0 if i >= 2 else CH - 1
            v.tensor_tensor(chunks(KS[:, i, :]), bcast(gB[:, i, bass.ds(first, NCH, CH)], CH), chunks(gB[:, i, :]),
                            ALU.subtract).then_inc(s_gd, 1)
        for t in range(NT):
            v.wait_ge(s_sge, t + 1)
            link(v.tensor_scalar(SG[:, t, :], SG[:, t, :], 1.0, None, ALU.add))
            link(v.reciprocal(SG[:, t, :], SG[:, t, :]))
            v.tensor_tensor(GO[:, t, :], GO[:, t, :], SG[:, t, :], ALU.mult).then_inc(s_sgd, 1)
        wait_empty(v, ("gqk", 3))
        for i in range(4):
            v.wait_ge(s_ex, 4 * i + 4)
            v.tensor_tensor(KS[:, i, :], KS[:, i, :], GK[:, i % 2, :], ALU.mult).then_inc(s_k, 1)
            v.tensor_tensor(KD[:, i, :], KD[:, i, :], GK[:, i % 2, :], ALU.mult).then_inc(ch_v, 1)
            v.tensor_tensor(QD[:, i, :], QD[:, i, :], GQ[:, i % 2, :], ALU.mult).then_inc(ch_v, 1)
            chain[0] += 2
        v.wait_ge(ch_v, chain[0])
        for i in range(4):
            back = i >= 2
            wait_full(v, ("ds", i, 1 if back else 0))
            v.wait_ge(s_ex, 4 * i + 4)
            order = range(NCH - 1, 0, -1) if back else range(NCH - 1)
            for q, n in enumerate(order):
                add = bank_of(("ds", i, n % 2))[:, (n // 2) * DV:(n // 2 + 1) * DV]
                to = n - 1 if back else n + 1
                if q == 0:
                    ins = v.tensor_copy(ST[:, i, to, :], add)
                else:
                    ins = v.scalar_tensor_tensor(ST[:, i, to, :], ST[:, i, n, :], EG[:, i, n:n + 1], add,
                                                 ALU.mult, ALU.add)
                if q < NCH - 3:
                    link(ins)
                else:
                    emptied_by(ins)
                    wait_empty(v, ("ds", i, n % 2))
        mask = CIt[:, 0:2 * P].rearrange("p (d c) -> p d c", d=2)
        v.wait_ge(s_zero, 1)
        for t in range(NT):
            for par in range(2):
                wait_full(v, ("at", t, par))
                if t >= 2:
                    wait_full(v, ("o", t - 2, 1))
                for fc in range(2):
                    ins = v.copy_predicated(
                        AB[:, 2 * (t % 2) + par, fc * 256:(fc + 1) * 256].rearrange("p (d c) -> p d c", d=2), mask,
                        bank_of(("at", t, par))[:, fc * 256:(fc + 1) * 256].rearrange("p (d c) -> p d c", d=2))
                    if fc == 0:
                        link(ins)
                emptied_by(ins)
        for t in range(NT):
            wait_empty(v, ("o", t, 1))
            link(v.tensor_tensor(AO[:, 2, :], OS[:, t, :], OS[:, t, :], ALU.mult))
            link(v.tensor_reduce(st16[:, t, :], AO[:, 2, :].rearrange("p (h e) -> p h e", h=HG), AX.X, ALU.add))
        inv_root(st16, 16, 2, DV)
        for t in range(NT):
            o3 = OS[:, t, :].rearrange("p (h e) -> p h e", h=HG)
            link(v.tensor_tensor(o3, o3, bcast(st16[:, t, :], DV), ALU.mult))
            v.tensor_tensor(OS[:, t, :], OS[:, t, :], GO[:, t, :], ALU.mult).then_inc(s_os, 1)

        for i in range(HA + 2):
            if i < HA:
                h = i
                v.wait_ge(s_tb[h % 4], 16 * (h // 4 + 1))
                for t in range(NT):
                    wait_full(v, ("s", h, t))
                    if t == 0 and h >= 2:
                        wait_full(v, ("pt", h - 2, NT - 1))
                    emptied_by(v.tensor_tensor_reduce(
                        out=LP[h % 2][:, t, :], in0=bank_of(("s", h, t))[:, :],
                        in1=TB[:, h % 4, t * P:t * P + SEQ][:, ::-1], scale=1.0, scalar=-3.0e38,
                        op0=ALU.add, op1=ALU.max, accum_out=mx4[:, h % 2, t:t + 1]))
                wait_empty(v, ("s", h, NT - 1))
                v.tensor_scalar(mx4[:, h % 2, :], mx4[:, h % 2, :], -1.0, None, ALU.mult).then_inc(s_neg, 1)
            if i >= 2:
                h = i - 2
                v.wait_ge(s_p, NT * h + NT)
                link(v.reciprocal(rden[:, h % 2, :], den4[:, h % 4, :]))
                wait_full(v, ("pv", h))
                emptied_by(v.tensor_tensor(AO[:, :, h * DH:(h + 1) * DH],
                                           bank_of(("pv", h))[:, 0:NT * DH].rearrange("p (t e) -> p t e", t=NT),
                                           bcast(rden[:, h % 2, :], DH), ALU.mult))
            if 1 <= i <= HA:
                h = i - 1
                for t in (0, 2):
                    wait_full(v, ("pt", h, t))
                    emptied_by(v.tensor_copy(PT[:, t, :, :], bank_of(("pt", h, t))[:, :].rearrange("p (a b) -> p a b", b=P)))
        for c in (0, 2):
            wait_full(v, ("aT", c))
            emptied_by(v.tensor_copy(MIX[:, c, :], bank_of(("aT", c))[:, :]))
        for t in range(NT):
            for n in range(2):
                wait_full(v, ("wo", t, n))
                emptied_by(v.tensor_tensor(X[:, t, n * 512:(n + 1) * 512], bank_of(("wo", t, n))[:, :],
                                           X[:, t, n * 512:(n + 1) * 512], ALU.add))
            wait_empty(v, ("wo", t, 1))
            v.wait_ge(s_sq, NT + t + 1)
            inv_root(st4[:, t:t + 1], 1, 3 + t, D)
            v.tensor_scalar(HN[:, t, :], X[:, t, :], st4[:, t:t + 1], None, ALU.mult).then_inc(s_xn, 1)
        for k in range(0, NK, 2):
            wait_full(v, ("hT", k))
            emptied_by(v.tensor_scalar(HT[:, k, :], bank_of(("hT", k))[:, :], VT[:, V2 + k:V2 + k + 1], None, ALU.mult))
        wait_full(v, ("logit",))
        v.wait_ge(s_rw, 32)
        wait_full(v, ("wo", NT - 1, 1))
        lb = bank_of(("logit",))[:, 0:NT * E].rearrange("p (t e) -> p t e", t=NT)
        emptied_by(v.tensor_tensor(LG, lb, RB.unsqueeze(1).to_broadcast([P, NT, E]), ALU.add))
        wait_empty(v, ("logit",))
        for t in range(NT):
            link(v.max(MX[:, t, :], LG[:, t, :]))
            link(v.max_index(IX[:, t, :], MX[:, t, :], LG[:, t, :]))
        link(v.tensor_copy(IXF, IX))
        io = CF[:, CIO:CIO + E]
        for t in range(NT):
            link(v.tensor_tensor(OHT[:, TOPK * t:TOPK * (t + 1), :], bcast(IXF[:, t, 0:TOPK], E),
                                 io.unsqueeze(1).to_broadcast([P, TOPK, E]), ALU.is_equal))
        v.tensor_reduce(MSEL, OHT.rearrange("p (t k) e -> p t e k", t=NT), AX.X, ALU.add).then_inc(s_dt, 1)
        v.tensor_tensor(GT, MX[:, :, 0:TOPK], MX[:, :, 0:1].to_broadcast([P, NT, TOPK]), ALU.subtract).then_inc(s_exg, 1)
        v.wait_ge(s_exr, 1)
        link(v.tensor_reduce(g4[:, :, 0], GT, AX.X, ALU.add))
        link(v.reciprocal(g4[:, :, 0], g4[:, :, 0]))
        rowf = view(fixed, o_nt + 1552, NT * TOPK, 2)
        link(v.tensor_tensor(rowf[:, :, 1].rearrange("p (t k) -> p t k", t=NT), GT,
                             g4[:, :, 0:1].to_broadcast([P, NT, TOPK]), ALU.mult))
        link(v.tensor_copy(ROW[:, :, 0], CIt[:, 2 * P:]))
        wait_full(v, ("total",))
        cnt = bank_of(("total",))[:, 0:E]
        emptied_by(v.tensor_tensor(CMP, bcast(cnt, THR), CF[:, CTH:CTH + THR].unsqueeze(1).to_broadcast([P, E, THR]),
                                   ALU.is_gt))
        wait_empty(v, ("total",))
        link(v.tensor_reduce(NB, CMP, AX.X, ALU.add))
        link(v.tensor_scalar(NB, NB, 1.0, None, ALU.add))
        link(v.tensor_tensor_scan(BE, ones[:, 0:E], NB, 0.0, ALU.mult, ALU.add))
        link(v.tensor_tensor(BS, BE, NB, ALU.subtract))
        link(v.tensor_scalar(BS, BS, 1.0, float(SLOTS), ALU.add, ALU.mult))
        wait_full(v, ("rank",))
        rk = bank_of(("rank",))[:, 0:NT * E].rearrange("p (t e) -> p t e", t=NT)
        emptied_by(v.tensor_tensor(VAL, rk, BS.unsqueeze(1).to_broadcast([P, NT, E]), ALU.add))
        wait_empty(v, ("rank",))
        for t in range(NT):
            link(v.tensor_tensor(OHV[:, TOPK * t:TOPK * (t + 1), :], OHT[:, TOPK * t:TOPK * (t + 1), :],
                                 VAL[:, t, :].unsqueeze(1).to_broadcast([P, TOPK, E]), ALU.mult))
        link(v.tensor_reduce(DE, OHV, AX.X, ALU.add))
        v.tensor_copy(DEI, DE).then_inc(s_dest, 1)
        ends = BE[0:1, :].unsqueeze(1).to_broadcast([1, MAXB, E])
        link(v.tensor_tensor(EC, ends, bcast(CF[0:1, CIO:CIO + MAXB], E), ALU.is_le))
        link(v.tensor_reduce(EF, EC, AX.X, ALU.add))
        link(v.tensor_scalar(EF, EF, float(E - 1), None, ALU.min))
        link(v.tensor_copy(EMAP[:, 0:MAXB], EF))
        v.tensor_copy(EMAP[:, MAXB:MAXB + 1], BE[0:1, E - 1:E]).then_inc(s_emap, 1)
        v.wait_ge(s_hst, 16)
        v.memset(YT[:, 0:4, :], 0.0).then_inc(s_yt, 1)
        v.memset(YT[:, 4:8, :], 0.0).then_inc(s_yt, 1)
        v.wait_ge(s_tab, 16)
        v.tensor_scalar(TOK, TAB[:, :, 0], 2, None, ALU.logical_shift_right).then_inc(s_tabr, 1)

        def gain(q):
            return bcast(VT[:, V2 + 4 * q:V2 + 4 * q + 4], SLOTS)

        def four(b):
            return b[:, 0:4 * SLOTS].rearrange("p (a b) -> p a b", a=4)

        def next_tokens(base):
            for q in range(2):
                v.wait_ge(s_xtp, base + q + 1)
                v.tensor_tensor(XT[:, 4 * q:4 * q + 4, :], four(bank[6 + q]), gain(q), ALU.mult).then_inc(s_xt, 1)

        next_tokens(0)
        blocks = v.value_load(EMAP[0:1, MAXB:MAXB + 1], min_val=E, max_val=MAXB)
        before = chain[0]
        with v.Fori(0, blocks) as g:
            steps = [0]

            def step(ins):
                steps[0] += 1
                ins.then_inc(ch_v, 1)
                v.wait_ge(ch_v, STEPS * g + before + steps[0])

            e = v.value_load(EMAP[0:1, bass.ds(g, 1)], min_val=0, max_val=E - 1)
            v.wait_ge(s_yt, 2 * g + 2)
            v.tensor_copy(GTC, TABF[:, bass.ds(g, 1), 1]).then_inc(s_gi, 1)
            step(v.tensor_copy(BC, BT[:, :, bass.ds(e, 1)].rearrange("p a b -> p (a b)")))

            def clamp(q):
                if q < 3:
                    v.wait_ge(s_hf, 3 * g + q + 1)
                else:
                    v.wait_ge(s_used, PE_PER_BLOCK * g + NK)
                if q >= 2:
                    v.wait_ge(s_act, 4 * g + q - 1)
                z = HB[:, q % 2, :, :]
                step(v.tensor_tensor(z, four(bank[q]), bcast(BC[:, 4 * q:4 * q + 4], SLOTS), ALU.add))
                v.tensor_scalar(z[:, 0:4:2, :], z[:, 0:4:2, :], LIMIT, None, ALU.min).then_inc(s_gi, 1)
                step(v.tensor_scalar(z[:, 1:4:2, :], z[:, 1:4:2, :], LIMIT, -LIMIT, ALU.min, ALU.max))
                v.wait_ge(s_gi, 5 * g + 2 + q)
                step(v.scalar_tensor_tensor(z[:, 1:4:2, :], z[:, 1:4:2, :], 1.0, z[:, 0:4:2, :], ALU.add, ALU.mult))

            def swiglu(q):
                v.wait_ge(s_sig, 4 * g + q + 1)
                v.tensor_tensor(HG_[:, 2 * q:2 * q + 2, :], HB[:, q % 2, 1:4:2, :], SGM[:, q % 2, :, :],
                                ALU.mult).then_inc(s_act, 1)

            clamp(0)
            for q in range(1, 4):
                clamp(q)
                swiglu(q - 1)
            swiglu(3)
            next_tokens(2 * g + 2)
            for q in range(2):
                if q == 0:
                    v.wait_ge(s_yf, g + 1)
                else:
                    v.wait_ge(s_used, PE_PER_BLOCK * g + PE_PER_BLOCK)
                v.tensor_tensor(YT[:, 4 * q:4 * q + 4, :], four(bank[4 + q]),
                                bcast(BC[:, 16 + 4 * q:20 + 4 * q], SLOTS), ALU.add).then_inc(s_yt, 1)
            assert steps[0] == STEPS
        nb = v.value_load(EMAP[0:1, MAXB:MAXB + 1], min_val=E, max_val=MAXB)
        v.tensor_copy(GTC, TABF[:, bass.ds(nb, 1), 1]).then_inc(s_gi, 1)
        sums = [0]

        def final_step(ins):
            sums[0] += 1
            ins.then_inc(s_sum, 1)
            v.wait_ge(s_sum, sums[0])

        def add_rows(t):
            v.wait_ge(s_yl[t], 16)
            rows = view(arena, 4096 * t, TOPK, D)
            for k in range(TOPK):
                ins = v.tensor_tensor(X[:, t, :], X[:, t, :], rows[:, k, :], ALU.add)
                if k < TOPK - 1:
                    final_step(ins)
                else:
                    ins.then_inc(s_acc, 1)

        def final_norm(t):
            v.wait_ge(s_sq, 2 * NT + t + 1)
            st = st4[:, t:t + 1]
            v.tensor_scalar(st, st, 1.0 / D, EPS, ALU.mult, ALU.add).then_inc(s_var, 1)
            v.wait_ge(s_sd, 7 + t)
            final_step(v.reciprocal(st, st))
            v.scalar_tensor_tensor(X[:, t, :], X[:, t, :], st, FG, ALU.mult, ALU.mult).then_inc(s_fin, 1)

        v.wait_ge(s_fg, 16)
        for t in range(NT):
            add_rows(t)
            if t:
                final_norm(t - 1)
        final_norm(NT - 1)

    ctx.close()


def kernel(**inputs):
    import concourse.bacc as bacc
    from concourse.bass_utils import run_bass_kernel_spmd

    cf, ci, oh = shape_constants()
    a = {k: np.ascontiguousarray(v) for k, v in inputs.items()}
    arrays = {
        "x": a["x"].reshape(SEQ, D), "norm1_g": a["norm1_g"].reshape(NK, P), "norm2_g": a["norm2_g"].reshape(NK, P),
        "bg_f": a["gla_bg_fwd"].reshape(2, P), "bg_b": a["gla_bg_bwd"].reshape(2, P),
        "gla_g": a["gla_norm_g"].reshape(4, P), "w_in": a["w_in"].reshape(D, IN_W), "rel_bias": a["rel_bias"],
        "wg_f": a["gla_wg_fwd"].reshape(RANK, 256), "wg_b": a["gla_wg_bwd"].reshape(RANK, 256),
        "w_out": a["w_out"].reshape(D, D), "router_w": a["router_w"].reshape(D, E),
        "router_b": a["router_b"].reshape(1, E), "w1": a["moe_w1"].reshape(E, D, 2 * FF),
        "b1": a["moe_b1"].reshape(E, 2 * FF), "w2": a["moe_w2"].reshape(E, FF, D), "b2": a["moe_b2"].reshape(E, D),
        "final_g": a["final_g"].reshape(1, D), "const_f": cf, "const_i": ci, "const_rel": oh,
    }
    nc = bacc.Bacc("TRN2", target_bir_lowering=False, num_devices=1)
    args = [nc.dram_tensor(f"in_{n}", v.shape, mybir.dt.from_np(v.dtype), kind="ExternalInput").ap()
            for n, v in arrays.items()]
    args.append(nc.dram_tensor("out_y", (SEQ, D), F32, kind="ExternalOutput").ap())
    encoder_block(nc, *args)
    r = run_bass_kernel_spmd(nc, [{f"in_{n}": v for n, v in arrays.items()}], core_ids=[0])
    return r.results[0]["out_y"].reshape(1, SEQ, D)
```

```python
from contextlib import ExitStack

import numpy as np

import concourse.bass as bass
from concourse import mybir

F32 = mybir.dt.float32
I32 = mybir.dt.int32
U32 = mybir.dt.uint32
ALU = mybir.AluOpType
ACT = mybir.ActivationFunctionType
AX = mybir.AxisListType

P = 128
D, SEQ = 1024, 512
NT, NK = SEQ // P, D // P
HA, DH = 8, 64
HG, DK, DV = 4, 64, 128
CH = 64
NCH = SEQ // CH
RANK, TAU = 16, 16.0
IN_W = 3104
OFF_AQ, OFF_AK, OFF_AV, OFF_GQK, OFF_GV, OFF_GO, OFF_GZ = 0, 512, 1024, 1536, 2048, 2560, 3072
EPS = 1e-5
E, TOPK, FF = 32, 4, 1024
NF = FF // P
LIMIT, ALPHA = 7.0, 1.702
SLOTS = 96
MAXB = E + SEQ * TOPK // SLOTS
COLS = MAXB + 2
GR = 32
NG = SLOTS // GR
NJ = P // GR
THR = (SEQ - 1) // SLOTS
PAD = 4096
NEG = -1e30
REL = 1024
TW = SEQ + 3 * P

CI, CU, CO, CIO, CTH = 0, 128, 256, 384, 480
NCF = CTH + THR
CSEL = 0
CQ = CSEL + NG * P
CTK = CQ + P
CJ = CTK + NT * TOPK
NCL = CJ + 1
V1, V2, VB, VG, NV = 0, 8, 16, 20, 24


def shape_constants():
    cf, cl = np.zeros((P, NCF), np.float32), np.zeros((P, NCL), np.float32)
    cf[:, CI:CI + P] = np.eye(P)
    cf[:, CU:CU + P] = np.triu(np.ones((P, P)), 1)
    cf[:, CO:CO + P] = 1.0
    cf[:, CIO:CTH] = np.arange(CTH - CIO)
    cf[:, CTH:CTH + THR] = SLOTS * np.arange(1, THR + 1)
    p = np.arange(P)
    for g in range(NG):
        cl[:, CSEL + g * P:CSEL + (g + 1) * P] = p[:, None] == GR * g + p[None, :] % GR
    cl[:, CQ:CQ + P] = p[:, None] == p[None, :] // GR
    cl[:, CTK:CTK + NT * TOPK] = np.repeat(P * np.arange(NT), TOPK)[None, :] + p[:, None] - PAD
    cl[:, CJ] = NJ * PAD + p // GR
    s, c = np.arange(P)[:, None], np.arange(P)[None, :]
    same = s // CH == c // CH
    ci = np.zeros((P, 2 * P), np.int32)
    ci[:, 0:P] = same & (s <= c)
    ci[:, P:2 * P] = same & (s >= c)
    rel = (SEQ - 1) - np.arange(REL)
    n = np.abs(rel)
    nb, exact = 16, 8
    large = exact + (np.log(np.maximum(n, 1).astype(np.float32) / exact)
                     / np.log(1024 / exact) * (nb - exact)).astype(np.int32)
    bucket = np.where(rel > 0, nb, 0) + np.where(n < exact, n, np.minimum(large, nb - 1))
    count = sum(((rel % d == 0) & (n <= 64 * d)).astype(np.int32) for d in (1, 4, 16))
    oh = np.zeros((33, REL), np.float32)
    oh[bucket, np.arange(REL)] = 1.0
    oh[32] = np.where(count > 0, np.log(np.maximum(count, 1).astype(np.float32)), NEG)
    return cf, cl, ci, oh


def pre_jobs():
    jobs = [(("vec",), "v"), (("rel", 0), "v"), (("rel", 1), "a")]
    jobs += [(("nT", k), "va"[k % 2]) for k in range(NK)]
    jobs += [(("gqk", c), "a") for c in range(4)]
    jobs += [(("gz",), "v")] + [(("gate", i), "v") for i in range(4)]
    jobs += [(("gv", t), "a") for t in range(NT)] + [(("go", t), "a") for t in range(NT)]
    jobs += [(("aqk", c), "a") for c in range(8)] + [(("av", t), "a") for t in range(NT)]
    jobs += [(("kst", i), "a") for i in range(4)]
    jobs += [(("ds", i, par), "v") for i in range(4) for par in ((1, 0) if i < 2 else (0, 1))]
    for t in range(NT):
        jobs += [(("at", t, par), "v") for par in range(2)]
        if t:
            jobs += [(("o", t - 1, par), "a") for par in range(2)]
    jobs += [(("o", NT - 1, par), "a") for par in range(2)]
    for i in range(HA + 2):
        if i < HA:
            jobs += [(("s", i, t), "v") for t in range(NT)]
        if i == 0:
            jobs += [(("gT", h), "a") for h in range(HG)]
        if i >= 2:
            jobs += [(("pv", i - 2), "v")]
        if 1 <= i <= HA:
            jobs += [(("pt", i - 1, t), "va"[t % 2]) for t in range(NT)]
    jobs += [(("aT", c), "va"[c % 2]) for c in range(4)]
    for t in range(NT + 2):
        if t < NT:
            jobs += [(("wo", t, n), "v") for n in range(2)]
        if t >= 2:
            jobs += [(("lg", t - 2), "v")]
        if 1 <= t <= NT:
            jobs += [(("hT", t - 1, q), "va"[q]) for q in range(2)]
    jobs += [(("total",), "v"), (("rank",), "v"), (("tab",), "v"), (("gmT",), "a"), (("rep",), "v")]
    return jobs


def encoder_block(nc, x, norm1_g, norm2_g, bg_f, bg_b, gla_g, w_in, rel_bias, wg_f, wg_b, w_out, router_w, router_b,
                  w1, b1, w2, b2, final_g, const_f, const_late, const_i, const_rel, out):
    ctx = ExitStack()

    def sem(name):
        return ctx.enter_context(nc.semaphore(name))

    ARENA = 24832
    FIXED = 28350
    arena = ctx.enter_context(nc.sbuf_tensor("arena", [P, ARENA], F32))
    fixed = ctx.enter_context(nc.sbuf_tensor("fixed", [P, FIXED], F32))

    def view(buf, at, *shape, parts=P, dt=F32):
        n = int(np.prod(shape))
        a = buf[0:parts, at:at + n]
        if dt is not F32:
            a = a.bitcast(dt)
        if len(shape) == 2:
            a = a.rearrange("p (a b) -> p a b", a=shape[0])
        if len(shape) == 3:
            a = a.rearrange("p (a b c) -> p a b c", a=shape[0], b=shape[1])
        if len(shape) == 4:
            a = a.rearrange("p (a b c d) -> p a b c d", a=shape[0], b=shape[1], c=shape[2])
        return a

    R = [4096 * i for i in range(7)]
    win = {"gqk": view(arena, R[0], NK, 512), "gv": view(arena, R[1], NK, 512),
           "go": view(arena, R[2], NK, 512), "aq": view(arena, R[3], NK, 512),
           "ak": view(arena, R[4], NK, 512), "av": view(arena, R[5], NK, 512),
           "gz": view(arena, R[6], NK, 32)}
    gA, gT_ = view(arena, R[0], 4, 512), view(arena, R[0] + 2048, 4, 512)
    gB, QD = view(arena, R[1], 4, 512), view(arena, R[1] + 2048, 4, 512)
    KD, KS = view(arena, R[2], 4, 512), view(arena, R[2] + 2048, 4, 512)
    ST = view(arena, R[0], 4, NCH, DV)
    KN = view(arena, R[1], 4, NT, P)
    AB = view(arena, R[3], 4, 512)
    OS = view(arena, R[3] + 2048, NT, 512)
    WO = view(arena, R[4], NK, D)
    W1 = view(arena, 0, NK, 2 * FF)
    W2 = view(arena, R[4], NF, D)

    at = 0

    def take(n):
        nonlocal at
        at += n
        return at - n

    o_x, o_nt, o_qk, o_av = take(4096), take(4096), take(4096), take(2048)
    o_gqk, o_gv, o_go, o_zt = take(2048), take(2048), take(2048), take(512)
    o_t, o_a = take(4 * TW), take(2048)
    X = view(fixed, o_x, NT, D)
    NTt = view(fixed, o_nt, NK, SEQ)
    MIX = view(fixed, o_nt, NK, SEQ)
    XN = view(fixed, o_qk, NT, D)
    QK = view(fixed, o_qk, NK, SEQ)
    AV = view(fixed, o_av, NT, 512)
    SG = view(fixed, o_av, NT, 512)
    GQ, GK = view(fixed, o_gqk, 2, SEQ), view(fixed, o_gqk + 1024, 2, SEQ)
    GV, GO = view(fixed, o_gv, NT, 512), view(fixed, o_go, NT, 512)
    ZT = view(fixed, o_zt, SEQ, parts=32)
    LP = [view(fixed, o_gqk, NT, SEQ), view(fixed, o_gv, NT, SEQ)]
    PT = view(fixed, o_go, NT, NT, P)
    RELF = view(fixed, o_go, REL, parts=HA)
    OH = view(fixed, o_gv, REL, parts=33)
    TB = view(fixed, o_t, 4, TW)
    AO = view(fixed, o_a, NT, 512)
    HN = view(fixed, o_qk, NT, D)
    HT = view(fixed, o_gqk, 2, NK, P)
    OHT = view(fixed, o_gqk + 3584, NT, TOPK, E)
    OHV = view(fixed, o_nt + 512, NT, TOPK, E)
    MSEL = view(fixed, o_gqk + 4096, NT, E)
    RK = view(fixed, o_nt + 1152, NT, E)
    LG = view(fixed, o_gqk + 4224, NT, E)
    MX = view(fixed, o_gqk + 4352, NT, 8)
    IX = view(fixed, o_gqk + 4384, NT, 8, dt=U32)
    IXF = view(fixed, o_gqk + 4416, NT, 8)
    GT = view(fixed, o_nt + 1504, NT, TOPK)
    RA, SA, OV, CA = (view(fixed, o_nt + 1520 + 16 * i, NT * TOPK) for i in range(4))
    OVC = view(fixed, o_nt + 1584, NT * TOPK, THR)
    CMP = view(fixed, o_nt + 1664, E, THR)
    NB = view(fixed, o_nt + 1824, E)
    BE = view(fixed, o_nt + 1856, E)
    BS = view(fixed, o_nt + 1888, E)
    EF = view(fixed, o_nt + 1920, MAXB, parts=1)
    g4 = view(fixed, o_nt + 1984, NT, 1)
    EC = view(fixed, o_nt + 2048, MAXB, E, parts=1)
    GM = view(fixed, o_nt + 3800, NT, E)
    ONS = view(fixed, o_gqk + 2048, NT * TOPK, SLOTS)
    ONC = view(fixed, o_av, 2, NT * TOPK, COLS)
    T96 = view(fixed, o_av + 1760, 2, COLS, parts=SLOTS)
    XG = view(fixed, o_qk, D, parts=SLOTS)
    XT = view(fixed, o_qk + 1024, NK, SLOTS)
    HB = view(fixed, o_nt, NG, 2 * FF // NJ)
    SGM = view(fixed, o_nt + 1536, NG, FF // NJ)
    ACTV = view(fixed, o_nt + 2304, NG, FF // NJ)
    ATT = view(fixed, o_gqk, NG, 2, NJ, GR)
    YN = view(fixed, o_gqk + 768, NG, D // NJ)
    o_l = o_t + 2304
    CL = view(fixed, o_l, NCL)
    SID = view(fixed, o_l + NCL, NG, COLS, dt=I32)
    GAT = view(fixed, o_l + NCL + NG * COLS, NG, COLS)
    TOK = view(fixed, o_l + NCL + 2 * NG * COLS, COLS, parts=SLOTS, dt=I32)
    B1T = view(fixed, o_t, 2 * FF // NJ)
    B1Q = view(fixed, o_t + 512, 2 * FF // NJ, parts=NJ)
    FG = view(fixed, o_a, D)
    CF = view(fixed, take(NCF), NCF)
    CIt = view(fixed, take(2 * P), 2 * P, dt=I32)
    VT = view(fixed, take(NV), NV)
    GI = view(fixed, take(1), 1, parts=SLOTS, dt=I32)
    SI = view(fixed, take(NG), NG, dt=I32)
    GTC = view(fixed, take(NG), NG)
    GMT = view(fixed, o_a + 1024, SEQ, parts=E)
    B2R = view(fixed, o_t + 1024, D, parts=E)
    EG = view(fixed, take(32), 4, NCH)
    st4 = view(fixed, take(NT), NT)
    st16 = view(fixed, take(16), NT, HG)
    mx4 = view(fixed, take(8), 2, NT)
    den4 = view(fixed, take(16), 4, NT)
    rden = view(fixed, take(8), 2, NT)
    EMAP = view(fixed, take(64), 64, parts=1, dt=I32)
    RB = view(fixed, take(E), E)
    held = view(fixed, take(3 + NG), 3 + NG)
    RWs = view(fixed, o_t + 2048, NK, E)
    assert at <= FIXED, at
    VRW = view(fixed, o_zt, P, parts=NV)
    RX = view(fixed, o_zt + 128, HA, parts=33)
    WGt = view(fixed, o_t + 3 * FF, 2, 256, parts=32)
    JUNK = view(fixed, o_a, D)
    SCM = view(fixed, o_a, 512)
    ident = CF[:, CI:CI + P]
    ones = CF[:, CO:CO + P]
    above = CF[:, CU:CU + P]

    bank = [ctx.enter_context(nc.psum_tensor(f"bank{i}", [P, 512], F32)) for i in range(8)]

    rel_d = nc.dram_tensor("rel_d", [HA, REL], F32)
    hn_d = nc.dram_tensor("hn_d", [SEQ, D], F32)
    sum_d = nc.dram_tensor("sum_d", [SEQ * NJ, D // NJ], F32)

    jobs = pre_jobs()
    index = {name: j for j, (name, _) in enumerate(jobs)}
    emptied = []
    count = {"v": 0, "a": 0}
    for _, e in jobs:
        count[e] += 1
        emptied.append(count[e])
    bank_full = sem("bank_full")
    bank_empty = {"v": sem("bank_empty_v"), "a": sem("bank_empty_a")}

    def bank_of(name):
        return bank[index[name] % 8]

    def wait_empty(eng, *names):
        most = {}
        for n in names:
            j = index[n]
            most[jobs[j][1]] = max(most.get(jobs[j][1], 0), emptied[j])
        for e, v in most.items():
            eng.wait_ge(bank_empty[e], v)

    def wait_full(eng, name):
        eng.wait_ge(bank_full, index[name] + 1)

    s_const, s_x, s_vec, s_oh, s_rel, s_braw, s_wg = (sem(n) for n in (
        "const_loaded", "x_loaded", "vec_loaded", "onehot_loaded", "relbias_loaded", "bias_loaded", "gatew_loaded"))
    s_win = {k: sem(f"win_{k}_loaded") for k in ("gqk", "gz", "gv", "go", "aq", "ak", "av")}
    s_relst, s_wo, s_rw = sem("rel_stored"), sem("wout_loaded"), sem("router_loaded")
    s_tb = [sem(f"toeplitz{i}_loaded") for i in range(4)]
    s_ms = sem("pool_memset")
    ch_v, ch_a = sem("vector_chain"), sem("scalar_chain")
    s_sq, s_sd, s_xn = sem("squares_summed"), sem("root_taken"), sem("x_normalized")
    s_var = sem("variance_ready")
    s_ln = sem("gate_log_ready")
    s_b, s_gd, s_ex, s_k = sem("decay_sum_ready"), sem("decay_rest_ready"), sem("decay_exp_ready"), sem("decayed_ready")
    s_sge, s_sgd = sem("gate_exp_ready"), sem("silu_ready")
    s_zero = sem("score_buffer_zero")
    s_os = sem("gla_out_ready")
    s_p, s_neg = sem("probs_ready"), sem("row_max_ready")
    s_hst = sem("h_stored")
    s_dt, s_ons, s_onc, s_gm = sem("choices_ready"), sem("slot_onehot_ready"), sem("column_onehot_ready"), sem("gates_by_expert_ready")
    s_rw2 = sem("router_scaled")
    s_exg, s_exr = sem("top_logits_ready"), sem("top_exp_ready")
    s_tabr = sem("table_ready")
    s_acc0 = sem("residual_stored")
    s_emap = sem("expert_map_ready")
    s_w1 = [sem(f"w1_slot{k}_loaded") for k in range(NK)]
    s_w2 = [sem(f"w2_slot{k}_loaded") for k in range(NF // 2)]
    s_used = sem("weight_slot_used")
    s_idx, s_gath, s_yst = sem("indices_copied"), sem("tokens_gathered"), sem("y_added")
    s_xtp, s_xt = sem("x_transposed"), sem("xt_ready")
    s_b1 = sem("b1_loaded")
    s_b1p, s_b1t = sem("b1_spread"), sem("b1_ready")
    s_hf, s_sig, s_act = sem("hidden_full"), sem("sigmoid_ready"), sem("act_ready")
    s_gi, s_gc = sem("glu_input_ready"), sem("gates_copied")
    s_atp, s_at = sem("act_transposed"), sem("act_t_ready")
    s_yf, s_yn = sem("y_full"), sem("y_ready")
    s_b2, s_gb = sem("b2_loaded"), sem("b2_terms_full")
    s_yl = [sem(f"sum{t}_loaded") for t in range(NT)]
    s_acc, s_fin, s_out, s_fg = sem("sum_ready"), sem("final_ready"), sem("out_stored"), sem("final_g_loaded")

    PE_PER_BLOCK = NK + NF // 2
    STEPS = 9
    s_sum = sem("final_chain")

    block = ctx.enter_context(nc.Block())

    @block.sync
    def _(sp):
        sp.dma_start(CF, const_f).then_inc(s_const, 16)
        sp.dma_start(X, x.rearrange("(t p) d -> p t d", p=P)).then_inc(s_x, 16)
        for src, at_row in ((norm1_g, V1), (norm2_g, V2), (bg_f, VB), (bg_b, VB + 2), (gla_g, VG)):
            sp.dma_start(VRW[at_row:at_row + src.shape[0], :], src).then_inc(s_vec, 16)
        wv = w_in.rearrange("(k p) n -> p k n", p=P)
        for name, off, w in (("gqk", OFF_GQK, 512), ("gz", OFF_GZ, 32), ("gv", OFF_GV, 512),
                             ("go", OFF_GO, 512), ("aq", OFF_AQ, 512), ("ak", OFF_AK, 512),
                             ("av", OFF_AV, 512)):
            sp.dma_start(win[name], wv[:, :, off:off + w]).then_inc(s_win[name], 16)
        wait_full(sp, ("av", NT - 1))
        sp.dma_start(WO, w_out.rearrange("(k p) n -> p k n", p=P)).then_inc(s_wo, 16)
        wait_empty(sp, *[("gT", h) for h in range(HG)])
        for k in range(NK):
            sp.dma_start(W1[:, k, :], w1[0, k * P:(k + 1) * P, :]).then_inc(s_w1[k], 16)
        wait_empty(sp, ("s", HA - 1, NT - 1))
        sp.dma_start(B1Q, b1[0, :].rearrange("(j n) -> j n", j=NJ)).then_inc(s_b1, 16)
        sp.dma_start(B2R, b2).then_inc(s_b2, 16)
        wait_full(sp, ("wo", NT - 1, 1))
        for f in range(NF // 2):
            sp.dma_start(W2[:, 2 * f:2 * f + 2, :],
                         w2[0, 2 * f * P:(2 * f + 2) * P, :].rearrange("(a p) n -> p a n", p=P)).then_inc(s_w2[f], 16)
        sp.wait_ge(s_emap, 1)
        blocks = sp.value_load(EMAP[0:1, MAXB:MAXB + 1], min_val=E, max_val=MAXB)
        with sp.Fori(1, blocks) as g:
            e = sp.value_load(EMAP[0:1, bass.ds(g, 1)], min_val=0, max_val=E - 1)
            sp.wait_ge(s_b1p, g)
            sp.dma_start(B1Q, b1[bass.ds(e, 1), :].rearrange("e (j n) -> (e j) n", j=NJ)).then_inc(s_b1, 16)
            for k in range(NK):
                sp.wait_ge(s_used, PE_PER_BLOCK * g - PE_PER_BLOCK + k + 1)
                sp.dma_start(W1[:, k, :],
                             w1[bass.ds(e, 1), k * P:(k + 1) * P, :].rearrange("e p n -> (e p) n")
                             ).then_inc(s_w1[k], 16)
            for f in range(NF // 2):
                sp.wait_ge(s_used, PE_PER_BLOCK * g - PE_PER_BLOCK + NK + f + 1)
                sp.dma_start(W2[:, 2 * f:2 * f + 2, :],
                             w2[bass.ds(e, 1), 2 * f * P:(2 * f + 2) * P, :].rearrange("e (a p) n -> p (e a) n", p=P)
                             ).then_inc(s_w2[f], 16)
        nb = sp.value_load(EMAP[0:1, MAXB:MAXB + 1], min_val=E, max_val=MAXB)
        sp.wait_ge(s_b1p, nb)
        sp.dma_start(B1Q, b1[0, :].rearrange("(j n) -> j n", j=NJ)).then_inc(s_b1, 16)
        sp.wait_ge(s_yst, 48 * nb)
        rows = sum_d.ap().rearrange("(t p j) n -> t p (j n)", p=P, j=NJ)
        for t in range(NT):
            sp.dma_start(X[:, t, :], rows[t]).then_inc(s_yl[t], 16)
        for t in range(NT):
            sp.wait_ge(s_fin, t + 1)
            sp.dma_start(out[t * P:(t + 1) * P, :], X[:, t, :]).then_inc(s_out, 16)
        sp.wait_ge(s_out, 16 * NT)

    @block.tensor
    def _(pe):
        done = [0]

        def begin(name):
            j = index[name]
            assert j == done[0], (name, jobs[done[0]])
            done[0] += 1
            if j >= 8:
                pe.wait_ge(bank_empty[jobs[j - 8][1]], emptied[j - 8])
            return bank[j % 8]

        def full(ins):
            ins.then_inc(bank_full, 1)

        pe.wait_ge(s_const, 32)
        pe.wait_ge(s_vec, 16 * 5)
        b = begin(("vec",))
        full(pe.transpose(b[:, 0:NV], VRW, ident[0:NV, 0:NV]))
        pe.wait_ge(s_oh, 16)
        pe.wait_ge(s_rel, 16)
        for i in range(2):
            b = begin(("rel", i))
            full(pe.matmul(b[0:HA, :], RX, OH[:, 512 * i:512 * (i + 1)], start=True, stop=True))
        for k in range(NK):
            b = begin(("nT", k))
            for t in range(NT):
                if k == 0:
                    pe.wait_ge(s_xn, t + 1)
                m = pe.transpose(b[:, t * P:(t + 1) * P], XN[:, t, k * P:(k + 1) * P], ident)
            full(m)
        wait_empty(pe, *[("nT", k) for k in range(NK)])

        def features(name, w, c):
            b = begin(name)
            for k in range(NK):
                m = pe.matmul(b[:, :], w[:, k, c * P:(c + 1) * P], NTt[:, k, :], start=k == 0, stop=k == NK - 1)
            full(m)

        def tokens(name, w, t):
            b = begin(name)
            for k in range(NK):
                m = pe.matmul(b[:, :], NTt[:, k, t * P:(t + 1) * P], w[:, k, :], start=k == 0, stop=k == NK - 1)
            full(m)

        pe.wait_ge(s_win["gqk"], 16)
        for c in range(4):
            features(("gqk", c), win["gqk"], c)
        pe.wait_ge(s_win["gz"], 16)
        b = begin(("gz",))
        for k in range(NK):
            m = pe.matmul(b[0:32, :], win["gz"][:, k, :], NTt[:, k, :], start=k == 0, stop=k == NK - 1)
        full(m)
        wait_empty(pe, ("gz",))
        pe.wait_ge(s_wg, 32)
        for i in range(4):
            b = begin(("gate", i))
            full(pe.matmul(b[:, :], WGt[:, i // 2, (i % 2) * P:(i % 2 + 1) * P], ZT, start=True, stop=True))
        for name in ("gv", "go"):
            pe.wait_ge(s_win[name], 16)
            for t in range(NT):
                tokens((name, t), win[name], t)
        for c in range(8):
            if c % 4 == 0:
                pe.wait_ge(s_win["aq" if c < 4 else "ak"], 16)
            features(("aqk", c), win["aq" if c < 4 else "ak"], c % 4)
        pe.wait_ge(s_win["av"], 16)
        for t in range(NT):
            tokens(("av", t), win["av"], t)

        for i in range(4):
            pe.wait_ge(s_k, i + 1)
            b = begin(("kst", i))
            for t in range(NT):
                m = pe.transpose(b[:, t * P:(t + 1) * P], KS[:, i, t * P:(t + 1) * P], ident)
            full(m)
        for i in range(4):
            wait_empty(pe, ("kst", i))
            for par in ((1, 0) if i < 2 else (0, 1)):
                b = begin(("ds", i, par))
                r = slice(CH * par, CH * par + CH)
                for t in range(NT):
                    for hh in range(2):
                        h = 2 * (i % 2) + hh
                        m = pe.matmul(b[DK * hh:DK * hh + DK, t * DV:(t + 1) * DV],
                                      KN[r, i, t, DK * hh:DK * hh + DK], GV[r, t, h * DV:(h + 1) * DV],
                                      start=True, stop=True)
                full(m)

        def scores(t):
            for par in range(2):
                b = begin(("at", t, par))
                r = slice(DK * par, DK * par + DK)
                for fc in range(2):
                    for d in range(2):
                        i = 2 * d + fc
                        n = 2 * fc + d
                        m = pe.matmul(b[:, n * P:(n + 1) * P], KD[r, i, t * P:(t + 1) * P],
                                      QD[r, i, t * P:(t + 1) * P], start=True, stop=True)
                full(m)

        def gla_out(t):
            wait_empty(pe, ("at", t, 1))
            if t == 0:
                wait_empty(pe, ("ds", 3, 1))
            for par in range(2):
                b = begin(("o", t, par))
                r = slice(DK * par, DK * par + DK)
                for fc in range(2):
                    col = slice(fc * DV, (fc + 1) * DV)
                    h = 2 * fc + par
                    for d in range(2):
                        slot = 2 * fc + d
                        m = pe.matmul(b[:, col], AB[:, 2 * (t % 2) + par, slot * P:(slot + 1) * P],
                                      GV[:, t, h * DV:(h + 1) * DV], start=d == 0, stop=False, skip_group_check=True)
                    parts = [(d, half) for d in range(2) for half in range(2)
                             if (d, 2 * t + half) not in ((0, 0), (1, NCH - 1))]
                    for q, (d, half) in enumerate(parts):
                        i, n = 2 * d + fc, 2 * t + half
                        m = pe.matmul(b[CH * half:CH * half + CH, col], QD[r, i, n * CH:(n + 1) * CH],
                                      ST[r, i, n, :], start=False, stop=q == len(parts) - 1, skip_group_check=True)
                full(m)

        for t in range(NT):
            scores(t)
            if t:
                gla_out(t - 1)
        gla_out(NT - 1)

        for i in range(HA + 2):
            if i < HA:
                r = slice(DH * (i % 2), DH * (i % 2) + DH)
                for t in range(NT):
                    b = begin(("s", i, t))
                    full(pe.matmul(b[:, :], QK[r, i // 2, t * P:(t + 1) * P], QK[r, 4 + i // 2, :],
                                   start=True, stop=True))
            if i == 0:
                for h in range(HG):
                    b = begin(("gT", h))
                    for t in range(NT):
                        if h == 0:
                            pe.wait_ge(s_os, t + 1)
                        m = pe.transpose(b[:, t * P:(t + 1) * P], OS[:, t, h * DV:(h + 1) * DV], ident)
                    full(m)
            if i >= 2:
                h = i - 2
                wait_empty(pe, *[("pt", h, t) for t in range(NT)])
                b = begin(("pv", h))
                for t in range(NT):
                    for kb in range(NT):
                        m = pe.matmul(b[:, t * DH:(t + 1) * DH], PT[:, t, kb, :],
                                      AV[:, kb, h * DH:(h + 1) * DH], start=kb == 0, stop=kb == NT - 1)
                full(m)
            if 1 <= i <= HA:
                h = i - 1
                for t in range(NT):
                    pe.wait_ge(s_p, NT * h + t + 1)
                    b = begin(("pt", h, t))
                    for kb in range(NT):
                        m = pe.transpose(b[:, kb * P:(kb + 1) * P], LP[h % 2][:, t, kb * P:(kb + 1) * P], ident)
                    full(m)
        wait_empty(pe, ("pv", HA - 1))
        for c in range(4):
            b = begin(("aT", c))
            for t in range(NT):
                m = pe.transpose(b[:, t * P:(t + 1) * P], AO[:, t, c * P:(c + 1) * P], ident)
            full(m)
        wait_empty(pe, *[("aT", c) for c in range(4)], *[("gT", h) for h in range(HG)])
        pe.wait_ge(s_wo, 16)
        for t in range(NT + 2):
            if t < NT:
                for n in range(2):
                    b = begin(("wo", t, n))
                    for k in range(NK):
                        m = pe.matmul(b[:, :], MIX[:, k, t * P:(t + 1) * P], WO[:, k, n * 512:(n + 1) * 512],
                                      start=k == 0, stop=k == NK - 1)
                    full(m)
            if t >= 2:
                u = t - 2
                pe.wait_ge(s_rw2, 1)
                wait_empty(pe, ("hT", u, 0), ("hT", u, 1))
                b = begin(("lg", u))
                for k in range(NK):
                    m = pe.matmul(b[:, 0:E], HT[:, u % 2, k, :], RWs[:, k, :], start=k == 0, stop=k == NK - 1)
                full(m)
            if 1 <= t <= NT:
                u = t - 1
                pe.wait_ge(s_xn, NT + u + 1)
                for q in range(2):
                    b = begin(("hT", u, q))
                    for c in range(4):
                        k = 4 * q + c
                        m = pe.transpose(b[:, c * P:(c + 1) * P], HN[:, u, k * P:(k + 1) * P], ident)
                    full(m)
        pe.wait_ge(s_dt, NT)
        b = begin(("total",))
        for t in range(NT):
            m = pe.matmul(b[:, 0:E], ones, MSEL[:, t, :], start=t == 0, stop=t == NT - 1)
        full(m)
        b = begin(("rank",))
        for t in range(NT):
            for u in range(t + 1):
                m = pe.matmul(b[:, t * E:(t + 1) * E], above if u == t else ones, MSEL[:, u, :],
                              start=u == 0, stop=u == t)
        full(m)
        pe.wait_ge(s_ons, 1)
        pe.wait_ge(s_onc, 2)
        b = begin(("tab",))
        for a in range(NT * TOPK):
            m = pe.matmul(b[0:SLOTS, 0:2 * COLS], ONS[:, a, :], ONC[:, :, a, :], start=a == 0, stop=a == NT * TOPK - 1)
        full(m)
        pe.wait_ge(s_gm, 1)
        b = begin(("gmT",))
        for t in range(NT):
            m = pe.transpose(b[0:E, t * P:(t + 1) * P], GM[:, t, :], ident)
        full(m)
        wait_empty(pe, ("tab",))
        b = begin(("rep",))
        for g in range(NG):
            m = pe.matmul(b[:, g * 2 * COLS:(g + 1) * 2 * COLS], CL[0:SLOTS, CSEL + g * P:CSEL + (g + 1) * P],
                          T96, start=True, stop=True)
        full(m)
        assert done[0] == len(jobs)

        def x_transposes(n):
            pe.wait_ge(s_gath, n)
            for q in range(2):
                for c in range(4):
                    k = 4 * q + c
                    m = pe.transpose(bank[6 + q][:, c * SLOTS:(c + 1) * SLOTS], XG[:, k * P:(k + 1) * P],
                                     ident[0:SLOTS, 0:SLOTS])
                m.then_inc(s_xtp, 1)

        def b1_spread(n):
            pe.wait_ge(s_b1, n)
            pe.matmul(bank[5][:, :], CL[0:NJ, CQ:CQ + P], B1Q, start=True, stop=True).then_inc(s_b1p, 1)

        def hidden(r, k):
            for j in range(NJ):
                m = pe.matmul(bank[r][GR * j:GR * (j + 1), :], XT[:, k, GR * r:GR * (r + 1)],
                              W1[:, k, 512 * j:512 * (j + 1)], start=k == 0, stop=k == NK - 1)
            return m

        def product(r, f2):
            for c in range(2):
                for j in range(NJ):
                    m = pe.matmul(bank[3 + r // 2][GR * j:GR * (j + 1), 256 * (r % 2):256 * (r % 2 + 1)],
                                  ATT[:, r, c, f2, :], W2[:, 2 * f2 + c, 256 * j:256 * (j + 1)],
                                  start=f2 == 0 and c == 0 and r != 1, stop=f2 == NF // 2 - 1 and c == 1,
                                  skip_group_check=True)
            return m

        wait_empty(pe, ("rep",), ("gmT",))
        b1_spread(16)
        x_transposes(16)
        blocks = pe.value_load(EMAP[0:1, MAXB:MAXB + 1], min_val=E, max_val=MAXB)
        with pe.Fori(0, blocks) as g:
            pe.wait_ge(s_xt, 2 * g + 2)
            for k in range(NK - 2):
                pe.wait_ge(s_w1[k], 16 * g + 16)
                for r in range(NG):
                    m = hidden(r, k)
                m.then_inc(s_used, 1)
            pe.wait_ge(s_w1[NK - 2], 16 * g + 16)
            pe.wait_ge(s_w1[NK - 1], 16 * g + 16)
            for r in range(NG):
                for k in (NK - 2, NK - 1):
                    m = hidden(r, k)
                    if r == NG - 1:
                        m.then_inc(s_used, 1)
                if r < NG - 1:
                    m.then_inc(s_hf, 1)
            def act_transposes(r):
                pe.wait_ge(s_act, NG * g + r + 1)
                for c in range(2):
                    m = pe.transpose(bank[r][:, c * P:(c + 1) * P], ACTV[:, r, c * P:(c + 1) * P], ident)
                m.then_inc(s_atp, 1)

            act_transposes(0)
            x_transposes(16 * g + 32)
            pe.wait_ge(s_at, NG * g + 1)
            pe.wait_ge(s_w2[0], 16 * g + 16)
            product(0, 0)
            pe.wait_ge(s_b1t, g + 1)
            b1_spread(16 * g + 32)
            act_transposes(1)
            pe.wait_ge(s_w2[1], 16 * g + 16)
            product(0, 1)
            pe.wait_ge(s_at, NG * g + 2)
            product(1, 0)
            product(1, 1)
            act_transposes(2)
            pe.wait_ge(s_w2[2], 16 * g + 16)
            product(0, 2)
            product(1, 2)
            pe.wait_ge(s_at, NG * g + 3)
            for f2 in range(3):
                product(2, f2).then_inc(s_used, 1)
            pe.wait_ge(s_w2[3], 16 * g + 16)
            product(0, 3)
            product(1, 3).then_inc(s_yf, 1)
            product(2, 3).then_inc(s_used, 1)
        nb = pe.value_load(EMAP[0:1, MAXB:MAXB + 1], min_val=E, max_val=MAXB)
        pe.wait_ge(s_yn, NG * nb)
        pe.wait_ge(s_xt, 2 * nb + 2)
        pe.wait_ge(s_b1t, nb + 1)
        pe.wait_ge(s_b2, 16)
        for t in range(NT):
            for n in range(2):
                pe.matmul(bank[2 * t + n][:, :], GMT[:, t * P:(t + 1) * P], B2R[:, n * 512:(n + 1) * 512],
                          start=True, stop=True).then_inc(s_gb, 1)

    @block.gpsimd
    def _(pool):
        pool.memset(held, 0.0)
        pool.memset(RX, 1.0).then_inc(s_ms, 1)
        pool.memset(WGt, 0.0).then_inc(s_ms, 1)
        pool.wait_ge(s_ms, 2)
        pool.dma_start(RX[0:E, :], rel_bias).then_inc(s_rel, 16)
        pool.dma_start(WGt[0:RANK, 0, :], wg_f).then_inc(s_wg, 16)
        pool.dma_start(WGt[RANK:2 * RANK, 1, :], wg_b).then_inc(s_wg, 16)
        pool.wait_ge(s_sq, NT)
        pool.memset(AO[:, 0:2, :], 1.0).then_inc(s_ms, 1)
        pool.wait_ge(s_ms, 3)
        pool.memset(AO[:, 0, bass.ds(0, NCH, CH)], 0.0).then_inc(s_ms, 1)
        pool.memset(AO[:, 1, bass.ds(CH - 1, NCH, CH)], 0.0).then_inc(s_ms, 1)
        wait_full(pool, ("aqk", 3))
        pool.memset(AB, 0.0).then_inc(s_zero, 1)

        def hold(n):
            pool.tensor_tensor(held[:, 2 + n:3 + n], held[:, 0:1], held[:, 1:2], ALU.add)

        last_token, last_row = (pool.to_reg(n - 1) for n in (SEQ, SEQ * NJ))
        pool.wait_ge(s_hst, 16)
        wait_full(pool, ("hT", NT - 1, 1))
        pool.memset(XG, 0.0).then_inc(s_idx, 1)
        pool.wait_ge(s_tabr, 1)
        pool.tensor_copy(GI, TOK[:, 0:1]).then_inc(s_idx, 1)
        pool.wait_ge(s_idx, 2)
        pool.indirect_dma_start(out=XG, out_offset=None, in_=hn_d.ap(),
                                in_offset=bass.IndirectOffsetOnAxis(GI, 0),
                                bounds_check=last_token, oob_is_err=False).then_inc(s_gath, 16)
        pool.wait_ge(s_tabr, 2)
        pool.wait_ge(s_acc0, 16)
        blocks = pool.value_load(EMAP[0:1, MAXB:MAXB + 1], min_val=E, max_val=MAXB)
        with pool.Fori(0, blocks) as g:
            pool.wait_ge(s_gath, 16 * g + 16)
            pool.wait_ge(s_xtp, 2 * g + 2)
            pool.tensor_copy(GI, TOK[:, bass.ds(g + 1, 1)]).then_inc(s_idx, 1)
            pool.wait_ge(s_idx, 2 * g + 3)
            hold(NG)
            pool.indirect_dma_start(out=XG, out_offset=None, in_=hn_d.ap(),
                                    in_offset=bass.IndirectOffsetOnAxis(GI, 0),
                                    bounds_check=last_token, oob_is_err=False).then_inc(s_gath, 16)
            pool.tensor_copy(SI, SID[:, :, bass.ds(g, 1)].rearrange("p a b -> p (a b)")).then_inc(s_idx, 1)
            pool.wait_ge(s_idx, 2 * g + 4)
            for r in range(NG):
                pool.wait_ge(s_yn, NG * g + r + 1)
                hold(r)
                pool.indirect_dma_start(out=sum_d.ap(), out_offset=bass.IndirectOffsetOnAxis(SI[:, r:r + 1], 0),
                                        in_=YN[:, r, :], in_offset=None, bounds_check=last_row, oob_is_err=False,
                                        compute_op=ALU.add).then_inc(s_yst, 16)
            pool.wait_ge(s_yst, 48 * g + 48)

    @block.scalar
    def _(act):
        chain = [0]

        def link(ins):
            chain[0] += 1
            ins.then_inc(ch_a, 1)
            act.wait_ge(ch_a, chain[0])

        def emptied_by(ins):
            ins.then_inc(bank_empty["a"], 1)

        def plain(name, dst, scale=1.0):
            wait_full(act, name)
            emptied_by(act.activation(dst, bank_of(name)[:, :], ACT.Copy, scale=scale))

        act.dma_start(CIt, const_i).then_inc(s_const, 16)
        act.dma_start(OH, const_rel).then_inc(s_oh, 16)
        act.wait_ge(s_x, 16)
        for t in range(NT):
            if t:
                act.wait_ge(s_sq, t)
            act.activation(JUNK, X[:, t, :], ACT.Square, accum_out=st4[:, t:t + 1]).then_inc(s_sq, 1)
        act.wait_ge(s_var, 1)
        act.activation(st4, st4, ACT.Sqrt).then_inc(s_sd, 1)
        wait_full(act, ("rel", 1))
        emptied_by(act.activation(RELF[:, 512:1024], bank_of(("rel", 1))[0:HA, :], ACT.Copy))
        wait_empty(act, ("rel", 0), ("rel", 1))
        act.dma_start(rel_d.ap(), RELF).then_inc(s_relst, 16)
        wait_empty(act, ("vec",))
        for k in range(1, NK, 2):
            plain(("nT", k), NTt[:, k, :], VT[:, V1 + k:V1 + k + 1])
        for c in range(4):
            plain(("gqk", c), (GQ if c < 2 else GK)[:, c % 2, :], 0.125 if c < 2 else 1.0)
        for i in range(4):
            wait_empty(act, ("gate", i))
            link(act.activation(gT_[:, i, :], gA[:, i, :], ACT.Abs))
            link(act.activation(gT_[:, i, :], gT_[:, i, :], ACT.Exp, scale=-1.0))
            act.activation(gT_[:, i, :], gT_[:, i, :], ACT.Ln, bias=1.0).then_inc(s_ln, 1)
        wait_full(act, ("rel", 1))
        act.wait_ge(s_relst, 16)
        wait_full(act, ("gate", 3))
        for h in range(4):
            act.dma_start(TB[:, h, :], bass.AP(rel_d, h * REL, [[1, P], [1, TW]])).then_inc(s_tb[h], 16)
        for t in range(NT):
            plain(("gv", t), GV[:, t, :])
        for t in range(NT):
            plain(("go", t), GO[:, t, :])
        wait_empty(act, ("go", NT - 1))
        for t in range(NT):
            act.activation(SG[:, t, :], GO[:, t, :], ACT.Exp, scale=-1.0).then_inc(s_sge, 1)
        for i in range(4):
            act.wait_ge(s_b, i + 1)
            act.wait_ge(s_gd, i + 1)
            first = 0 if i >= 2 else CH - 1
            act.activation(EG[:, i, :], gB[:, i, bass.ds(first, NCH, CH)], ACT.Exp, scale=1.0 / TAU).then_inc(s_ex, 1)
            act.activation(QD[:, i, :], gB[:, i, :], ACT.Exp, scale=1.0 / TAU).then_inc(s_ex, 1)
            act.activation(KD[:, i, :], gB[:, i, :], ACT.Exp, scale=-1.0 / TAU).then_inc(s_ex, 1)
            act.activation(KS[:, i, :], KS[:, i, :], ACT.Exp, scale=1.0 / TAU).then_inc(s_ex, 1)
        for c in range(8):
            plain(("aqk", c), QK[:, c, :], 0.125 if c < 4 else 1.0)
        act.wait_ge(s_sgd, NT)
        for t in range(NT):
            plain(("av", t), AV[:, t, :])
        for i in range(4):
            wait_full(act, ("kst", i))
            emptied_by(act.activation(KN[:, i, :, :], bank_of(("kst", i))[:, :].rearrange("p (a b) -> p a b", b=P), ACT.Copy))
        for t in range(NT):
            for par in range(2):
                wait_full(act, ("o", t, par))
                emptied_by(act.activation(OS[:, t, :].rearrange("p (f q e) -> p q f e", f=2, q=2)[:, par, :, :],
                                          bank_of(("o", t, par))[:, 0:256].rearrange("p (f e) -> p f e", f=2), ACT.Copy))
        act.wait_ge(s_var, 2)
        act.activation(st16, st16, ACT.Sqrt).then_inc(s_sd, 1)

        def probs(h):
            act.wait_ge(s_neg, h + 1)
            if h >= 2:
                wait_empty(act, ("pt", h - 2, NT - 1))
            for t in range(NT):
                act.activation(LP[h % 2][:, t, :], LP[h % 2][:, t, :], ACT.Exp, bias=mx4[:, h % 2, t:t + 1],
                               accum_out=den4[:, h % 4, t:t + 1]).then_inc(s_p, 1)
            if h < 4:
                act.dma_start(TB[:, h, :], bass.AP(rel_d, (h + 4) * REL, [[1, P], [1, TW]])
                              ).then_inc(s_tb[h], 16)

        for i in range(HA + 2):
            if i == 0:
                for h in range(HG):
                    plain(("gT", h), MIX[:, 4 + h, :], VT[:, VG + h:VG + h + 1])
            if i < HA:
                probs(i)
            if 1 <= i <= HA:
                h = i - 1
                for t in (1, 3):
                    wait_full(act, ("pt", h, t))
                    emptied_by(act.activation(PT[:, t, :, :], bank_of(("pt", h, t))[:, :].rearrange("p (a b) -> p a b", b=P), ACT.Copy))
        for c in (1, 3):
            plain(("aT", c), MIX[:, c, :])
        wait_full(act, ("s", HA - 1, NT - 1))
        act.wait_ge(s_neg, HA)
        act.dma_start(RWs, router_w.rearrange("(k p) e -> p k e", p=P)).then_inc(s_rw, 16)
        act.dma_start(CL, const_late).then_inc(s_rw, 16)
        act.dma_start(RB, bass.AP(router_b.tensor, 0, [[0, P], [1, E]])).then_inc(s_rw, 16)
        def transposed(t):
            wait_full(act, ("hT", t, 1))
            emptied_by(act.activation(HT[:, t % 2, 4:8, :],
                                      bank_of(("hT", t, 1))[:, :].rearrange("p (a b) -> p a b", b=P), ACT.Copy))

        wait_full(act, ("aT", 3))
        for t in range(NT):
            wait_empty(act, ("wo", t, 1))
            act.activation(JUNK, X[:, t, :], ACT.Square, accum_out=st4[:, t:t + 1]).then_inc(s_sq, 1)
            act.wait_ge(s_var, 3 + t)
            act.activation(st4[:, t:t + 1], st4[:, t:t + 1], ACT.Sqrt).then_inc(s_sd, 1)
            if t:
                transposed(t - 1)
        transposed(NT - 1)
        act.wait_ge(s_xn, 2 * NT)
        act.dma_start(hn_d.ap().rearrange("(t p) d -> p t d", p=P), HN).then_inc(s_hst, 16)
        act.dma_start(sum_d.ap().rearrange("(t p j) n -> p t (j n)", p=P, j=NJ), X).then_inc(s_acc0, 16)
        act.wait_ge(s_exg, 1)
        act.activation(GT, GT, ACT.Exp).then_inc(s_exr, 1)
        wait_full(act, ("gmT",))
        emptied_by(act.activation(GMT, bank_of(("gmT",))[0:E, :], ACT.Copy))
        act.dma_start(FG, bass.AP(final_g.tensor, 0, [[0, P], [1, D]])).then_inc(s_fg, 16)

        act.wait_ge(s_b1p, 1)
        act.activation(B1T, bank[5][:, :], ACT.Copy).then_inc(s_b1t, 1)
        act.wait_ge(s_emap, 1)
        blocks = act.value_load(EMAP[0:1, MAXB:MAXB + 1], min_val=E, max_val=MAXB)
        with act.Fori(0, blocks) as g:
            def sigmoid(r):
                act.wait_ge(s_gi, NG * g + r + 1)
                act.activation(SGM[:, r, :], HB[:, r, 0:512:2], ACT.Sigmoid, scale=ALPHA).then_inc(s_sig, 1)

            def transposed_act(r):
                act.wait_ge(s_atp, NG * g + r + 1)
                act.activation(ATT[:, r, :, :, :].rearrange("p c j t -> p (c j t)"),
                               bank[r][:, 0:256], ACT.Copy).then_inc(s_at, 1)

            sigmoid(0)
            sigmoid(1)
            transposed_act(0)
            sigmoid(2)
            transposed_act(1)
            transposed_act(2)
            act.wait_ge(s_b1p, g + 2)
            act.wait_ge(s_act, NG * g + NG)
            act.activation(B1T, bank[5][:, :], ACT.Copy).then_inc(s_b1t, 1)
            act.wait_ge(s_idx, 2 * g + 3)
            act.wait_ge(s_gc, g + 1)
            for r in range(NG):
                if r < 2:
                    act.wait_ge(s_yf, g + 1)
                else:
                    act.wait_ge(s_used, PE_PER_BLOCK * g + PE_PER_BLOCK)
                act.activation(YN[:, r, :], bank[3 + r // 2][:, 256 * (r % 2):256 * (r % 2 + 1)], ACT.Copy,
                               scale=GTC[:, r:r + 1]).then_inc(s_yn, 1)
        for t in range(NT):
            act.wait_ge(s_acc, t + 1)
            act.activation(HB[:, 0:2, :].rearrange("p a b -> p (a b)"), X[:, t, :], ACT.Square,
                           accum_out=st4[:, t:t + 1]).then_inc(s_sq, 1)
            act.wait_ge(s_var, 7 + t)
            act.activation(st4[:, t:t + 1], st4[:, t:t + 1], ACT.Sqrt).then_inc(s_sd, 1)

    @block.vector
    def _(v):
        chain = [0]

        def link(ins):
            chain[0] += 1
            ins.then_inc(ch_v, 1)
            v.wait_ge(ch_v, chain[0])

        def emptied_by(ins):
            ins.then_inc(bank_empty["v"], 1)

        def chunks(a):
            return a.rearrange("p (n c) -> p n c", c=CH)

        def bcast(a, n):
            return a.unsqueeze(len(a.shape)).to_broadcast([*a.shape, n])

        def inv_root(stat, n, nth, k):
            v.tensor_scalar(stat, stat, 1.0 / k, EPS, ALU.mult, ALU.add).then_inc(s_var, 1)
            v.wait_ge(s_sd, nth)
            link(v.reciprocal(stat, stat))

        v.wait_ge(s_const, 32)
        wait_full(v, ("vec",))
        emptied_by(v.tensor_copy(VT, bank_of(("vec",))[:, 0:NV]))
        wait_full(v, ("rel", 0))
        emptied_by(v.tensor_copy(RELF[:, 0:512], bank_of(("rel", 0))[0:HA, :]))
        v.wait_ge(s_sq, NT)
        inv_root(st4, NT, 1, D)
        for t in range(NT):
            v.tensor_scalar(XN[:, t, :], X[:, t, :], st4[:, t:t + 1], None, ALU.mult).then_inc(s_xn, 1)
        wait_empty(v, ("vec",))
        for k in range(0, NK, 2):
            wait_full(v, ("nT", k))
            emptied_by(v.tensor_scalar(NTt[:, k, :], bank_of(("nT", k))[:, :], VT[:, V1 + k:V1 + k + 1], None, ALU.mult))
        wait_full(v, ("gz",))
        emptied_by(v.tensor_copy(ZT, bank_of(("gz",))[0:32, :]))
        for i in range(4):
            wait_full(v, ("gate", i))
            emptied_by(v.tensor_scalar(gA[:, i, :], bank_of(("gate", i))[:, :], VT[:, VB + i:VB + i + 1], None,
                                       ALU.add))
        v.wait_ge(s_ms, 5)
        wait_full(v, ("go", NT - 1))
        for i in range(4):
            v.wait_ge(s_ln, i + 1)
            link(v.scalar_tensor_tensor(gA[:, i, :], gA[:, i, :], 0.0, gT_[:, i, :], ALU.min, ALU.subtract))
            rev = slice(None, None, -1 if i >= 2 else 1)
            v.tensor_tensor_scan(gB[:, i, rev], AO[:, i // 2, rev], gA[:, i, rev], 0.0,
                                 ALU.mult, ALU.add).then_inc(s_b, 1)
            v.wait_ge(s_b, i + 1)
            first = 0 if i >= 2 else CH - 1
            v.tensor_tensor(chunks(KS[:, i, :]), bcast(gB[:, i, bass.ds(first, NCH, CH)], CH), chunks(gB[:, i, :]),
                            ALU.subtract).then_inc(s_gd, 1)
        for t in range(NT):
            v.wait_ge(s_sge, t + 1)
            link(v.tensor_scalar(SG[:, t, :], SG[:, t, :], 1.0, None, ALU.add))
            link(v.reciprocal(SG[:, t, :], SG[:, t, :]))
            v.tensor_tensor(GO[:, t, :], GO[:, t, :], SG[:, t, :], ALU.mult).then_inc(s_sgd, 1)
        wait_empty(v, ("gqk", 3))
        for i in range(4):
            v.wait_ge(s_ex, 4 * i + 4)
            v.tensor_tensor(KS[:, i, :], KS[:, i, :], GK[:, i % 2, :], ALU.mult).then_inc(s_k, 1)
            v.tensor_tensor(KD[:, i, :], KD[:, i, :], GK[:, i % 2, :], ALU.mult).then_inc(ch_v, 1)
            v.tensor_tensor(QD[:, i, :], QD[:, i, :], GQ[:, i % 2, :], ALU.mult).then_inc(ch_v, 1)
            chain[0] += 2
        v.wait_ge(ch_v, chain[0])
        for i in range(4):
            back = i >= 2
            wait_full(v, ("ds", i, 1 if back else 0))
            v.wait_ge(s_ex, 4 * i + 4)
            order = range(NCH - 1, 0, -1) if back else range(NCH - 1)
            for q, n in enumerate(order):
                add = bank_of(("ds", i, n % 2))[:, (n // 2) * DV:(n // 2 + 1) * DV]
                to = n - 1 if back else n + 1
                if q == 0:
                    ins = v.tensor_copy(ST[:, i, to, :], add)
                else:
                    ins = v.scalar_tensor_tensor(ST[:, i, to, :], ST[:, i, n, :], EG[:, i, n:n + 1], add,
                                                 ALU.mult, ALU.add)
                if q < NCH - 3:
                    link(ins)
                else:
                    emptied_by(ins)
                    wait_empty(v, ("ds", i, n % 2))
        mask = CIt[:, 0:2 * P].rearrange("p (d c) -> p d c", d=2)
        v.wait_ge(s_zero, 1)
        for t in range(NT):
            for par in range(2):
                wait_full(v, ("at", t, par))
                if t >= 2:
                    wait_full(v, ("o", t - 2, 1))
                for fc in range(2):
                    ins = v.copy_predicated(
                        AB[:, 2 * (t % 2) + par, fc * 256:(fc + 1) * 256].rearrange("p (d c) -> p d c", d=2), mask,
                        bank_of(("at", t, par))[:, fc * 256:(fc + 1) * 256].rearrange("p (d c) -> p d c", d=2))
                    if fc == 0:
                        link(ins)
                emptied_by(ins)
        for t in range(NT):
            wait_empty(v, ("o", t, 1))
            link(v.tensor_tensor(AO[:, 2, :], OS[:, t, :], OS[:, t, :], ALU.mult))
            link(v.tensor_reduce(st16[:, t, :], AO[:, 2, :].rearrange("p (h e) -> p h e", h=HG), AX.X, ALU.add))
        inv_root(st16, 16, 2, DV)
        for t in range(NT):
            o3 = OS[:, t, :].rearrange("p (h e) -> p h e", h=HG)
            link(v.tensor_tensor(o3, o3, bcast(st16[:, t, :], DV), ALU.mult))
            v.tensor_tensor(OS[:, t, :], OS[:, t, :], GO[:, t, :], ALU.mult).then_inc(s_os, 1)

        for i in range(HA + 2):
            if i < HA:
                h = i
                v.wait_ge(s_tb[h % 4], 16 * (h // 4 + 1))
                for t in range(NT):
                    wait_full(v, ("s", h, t))
                    if t == 0 and h >= 2:
                        wait_full(v, ("pt", h - 2, NT - 1))
                    emptied_by(v.tensor_tensor_reduce(
                        out=LP[h % 2][:, t, :], in0=bank_of(("s", h, t))[:, :],
                        in1=TB[:, h % 4, t * P:t * P + SEQ][:, ::-1], scale=1.0, scalar=-3.0e38,
                        op0=ALU.add, op1=ALU.max, accum_out=mx4[:, h % 2, t:t + 1]))
                wait_empty(v, ("s", h, NT - 1))
                v.tensor_scalar(mx4[:, h % 2, :], mx4[:, h % 2, :], -1.0, None, ALU.mult).then_inc(s_neg, 1)
            if i >= 2:
                h = i - 2
                v.wait_ge(s_p, NT * h + NT)
                link(v.reciprocal(rden[:, h % 2, :], den4[:, h % 4, :]))
                wait_full(v, ("pv", h))
                emptied_by(v.tensor_tensor(AO[:, :, h * DH:(h + 1) * DH],
                                           bank_of(("pv", h))[:, 0:NT * DH].rearrange("p (t e) -> p t e", t=NT),
                                           bcast(rden[:, h % 2, :], DH), ALU.mult))
            if 1 <= i <= HA:
                h = i - 1
                for t in (0, 2):
                    wait_full(v, ("pt", h, t))
                    emptied_by(v.tensor_copy(PT[:, t, :, :], bank_of(("pt", h, t))[:, :].rearrange("p (a b) -> p a b", b=P)))
        for c in (0, 2):
            wait_full(v, ("aT", c))
            emptied_by(v.tensor_copy(MIX[:, c, :], bank_of(("aT", c))[:, :]))
        v.wait_ge(s_rw, 48)
        for k in range(NK):
            ins = v.tensor_scalar(RWs[:, k, :], RWs[:, k, :], VT[:, V2 + k:V2 + k + 1], None, ALU.mult)
        ins.then_inc(s_rw2, 1)
        io = CF[:, CIO:CIO + E]

        def top4(t):
            wait_full(v, ("lg", t))
            emptied_by(v.tensor_tensor(LG[:, t, :], bank_of(("lg", t))[:, 0:E], RB, ALU.add))
            wait_empty(v, ("lg", t))
            link(v.max(MX[:, t, :], LG[:, t, :]))
            link(v.max_index(IX[:, t, :], MX[:, t, :], LG[:, t, :]))
            link(v.tensor_copy(IXF[:, t, :], IX[:, t, :]))
            link(v.tensor_tensor(OHT[:, t, :, :], bcast(IXF[:, t, 0:TOPK], E),
                                 io.unsqueeze(1).to_broadcast([P, TOPK, E]), ALU.is_equal))
            v.tensor_reduce(MSEL[:, t, :], OHT[:, t, :, :].rearrange("p k e -> p e k"), AX.X, ALU.add).then_inc(s_dt, 1)

        for t in range(NT + 2):
            if t < NT:
                for n in range(2):
                    wait_full(v, ("wo", t, n))
                    emptied_by(v.tensor_tensor(X[:, t, n * 512:(n + 1) * 512], bank_of(("wo", t, n))[:, :],
                                               X[:, t, n * 512:(n + 1) * 512], ALU.add))
                wait_empty(v, ("wo", t, 1))
                v.wait_ge(s_sq, NT + t + 1)
                inv_root(st4[:, t:t + 1], 1, 3 + t, D)
                v.tensor_scalar(HN[:, t, :], X[:, t, :], st4[:, t:t + 1], None, ALU.mult).then_inc(s_xn, 1)
            if t >= 2:
                top4(t - 2)
            if 1 <= t <= NT:
                wait_full(v, ("hT", t - 1, 0))
                emptied_by(v.tensor_copy(HT[:, (t - 1) % 2, 0:4, :],
                                         bank_of(("hT", t - 1, 0))[:, :].rearrange("p (a b) -> p a b", b=P)))
        v.tensor_tensor(GT, MX[:, :, 0:TOPK], MX[:, :, 0:1].to_broadcast([P, NT, TOPK]), ALU.subtract).then_inc(s_exg, 1)
        wait_full(v, ("total",))
        cnt = bank_of(("total",))[:, 0:E]
        thr = CF[:, CTH:CTH + THR].unsqueeze(1)
        emptied_by(v.tensor_tensor(CMP, bcast(cnt, THR), thr.to_broadcast([P, E, THR]), ALU.is_gt))
        wait_empty(v, ("total",))
        link(v.tensor_reduce(NB, CMP, AX.X, ALU.add))
        link(v.tensor_scalar(NB, NB, 1.0, None, ALU.add))
        link(v.tensor_tensor_scan(BE, ones[:, 0:E], NB, 0.0, ALU.mult, ALU.add))
        link(v.tensor_tensor(BS, BE, NB, ALU.subtract))
        wait_full(v, ("rank",))
        emptied_by(v.tensor_copy(RK, bank_of(("rank",))[:, 0:NT * E].rearrange("p (t e) -> p t e", t=NT)))
        wait_empty(v, ("rank",))

        def chosen(dst, by_expert):
            link(v.tensor_tensor(OHV, OHT, by_expert, ALU.mult))
            link(v.tensor_reduce(dst.rearrange("p (t k) -> p t k", t=NT), OHV, AX.X, ALU.add))

        chosen(RA, RK.unsqueeze(2).to_broadcast([P, NT, TOPK, E]))
        link(v.tensor_tensor(OVC, bcast(RA, THR), thr.to_broadcast([P, NT * TOPK, THR]), ALU.is_ge))
        link(v.tensor_reduce(OV, OVC, AX.X, ALU.add))
        link(v.scalar_tensor_tensor(SA, OV, -float(SLOTS), RA, ALU.mult, ALU.add))
        slots = CF[:, CIO:CIO + SLOTS].unsqueeze(1).to_broadcast([P, NT * TOPK, SLOTS])
        v.tensor_tensor(ONS, bcast(SA, SLOTS), slots, ALU.is_equal).then_inc(s_ons, 1)
        chosen(CA, BS.unsqueeze(1).unsqueeze(1).to_broadcast([P, NT, TOPK, E]))
        link(v.tensor_tensor(CA, CA, OV, ALU.add))
        v.wait_ge(s_exr, 1)
        link(v.tensor_reduce(g4[:, :, 0], GT, AX.X, ALU.add))
        link(v.reciprocal(g4[:, :, 0], g4[:, :, 0]))
        link(v.tensor_tensor(GT, GT, g4[:, :, 0:1].to_broadcast([P, NT, TOPK]), ALU.mult))
        cols = CF[:, CIO:CIO + COLS].unsqueeze(1).to_broadcast([P, NT * TOPK, COLS])
        link(v.tensor_tensor(ONC[:, 0, :, :], bcast(CA, COLS), cols, ALU.is_equal))
        v.tensor_tensor(ONC[:, 1, :, :], ONC[:, 0, :, :], bcast(GT.rearrange("p t k -> p (t k)"), COLS),
                        ALU.mult).then_inc(s_onc, 1)
        v.wait_ge(s_onc, 1)
        v.tensor_tensor(ONC[:, 0, :, :], ONC[:, 0, :, :], bcast(CL[:, CTK:CTK + NT * TOPK], COLS),
                        ALU.mult).then_inc(s_onc, 1)
        link(v.tensor_tensor(OHV, OHT, bcast(GT, E), ALU.mult))
        v.tensor_reduce(GM, OHV.rearrange("p t k e -> p t e k"), AX.X, ALU.add).then_inc(s_gm, 1)
        ends = BE[0:1, :].unsqueeze(1).to_broadcast([1, MAXB, E])
        link(v.tensor_tensor(EC, ends, bcast(CF[0:1, CIO:CIO + MAXB], E), ALU.is_le))
        link(v.tensor_reduce(EF, EC, AX.X, ALU.add))
        link(v.tensor_scalar(EF, EF, float(E - 1), None, ALU.min))
        link(v.tensor_copy(EMAP[:, 0:MAXB], EF))
        v.tensor_copy(EMAP[:, MAXB:MAXB + 1], BE[0:1, E - 1:E]).then_inc(s_emap, 1)
        wait_full(v, ("tab",))
        emptied_by(v.tensor_copy(T96, bank_of(("tab",))[0:SLOTS, 0:2 * COLS].rearrange("p (a b) -> p a b", a=2)))
        wait_empty(v, ("tab",))
        v.tensor_scalar(TOK, T96[:, 0, :], float(PAD), None, ALU.add).then_inc(s_tabr, 1)
        wait_full(v, ("rep",))
        rep_ = bank_of(("rep",))[:, 0:NG * 2 * COLS].rearrange("p (g a b) -> p g a b", g=NG, a=2)
        link(v.tensor_scalar(SID, rep_[:, :, 0, :], float(NJ), CL[:, CJ:CJ + 1], ALU.mult, ALU.add))
        emptied_by(v.tensor_copy(GAT, rep_[:, :, 1, :]))
        wait_empty(v, ("rep",))
        v.memset(held[:, 0:1], 0.0).then_inc(s_tabr, 1)

        def gain(q):
            return bcast(VT[:, V2 + 4 * q:V2 + 4 * q + 4], SLOTS)

        def four(b):
            return b[:, 0:4 * SLOTS].rearrange("p (a b) -> p a b", a=4)

        def next_tokens(base):
            for q in range(2):
                v.wait_ge(s_xtp, base + q + 1)
                v.tensor_tensor(XT[:, 4 * q:4 * q + 4, :], four(bank[6 + q]), gain(q), ALU.mult).then_inc(s_xt, 1)

        next_tokens(0)
        blocks = v.value_load(EMAP[0:1, MAXB:MAXB + 1], min_val=E, max_val=MAXB)
        before = chain[0]
        with v.Fori(0, blocks) as g:
            steps = [0]

            def step(ins):
                steps[0] += 1
                ins.then_inc(ch_v, 1)
                v.wait_ge(ch_v, STEPS * g + before + steps[0])

            v.wait_ge(s_xt, 2 * g + 2)
            v.wait_ge(s_b1t, g + 1)

            def clamp(r):
                if r < NG - 1:
                    v.wait_ge(s_hf, 2 * g + r + 1)
                else:
                    v.wait_ge(s_used, PE_PER_BLOCK * g + NK)
                z = HB[:, r, :]
                glu, lin = z[:, 0:512:2], z[:, 1:512:2]
                step(v.tensor_tensor(z, bank[r][:, :], B1T, ALU.add))
                v.tensor_scalar(glu, glu, LIMIT, None, ALU.min).then_inc(s_gi, 1)
                step(v.tensor_scalar(lin, lin, LIMIT, -LIMIT, ALU.min, ALU.max))
                v.wait_ge(s_gi, NG * g + r + 1)
                step(v.scalar_tensor_tensor(lin, lin, 1.0, glu, ALU.add, ALU.mult))

            def swiglu(r):
                v.wait_ge(s_sig, NG * g + r + 1)
                v.tensor_tensor(ACTV[:, r, :], HB[:, r, 1:512:2], SGM[:, r, :], ALU.mult).then_inc(s_act, 1)

            for r in range(NG):
                clamp(r)
                swiglu(r)
                if r == 0:
                    v.tensor_copy(GTC, GAT[:, :, bass.ds(g, 1)].rearrange("p a b -> p (a b)")).then_inc(s_gc, 1)
            next_tokens(2 * g + 2)
            assert steps[0] == STEPS
        sums = [0]

        def final_step(ins):
            sums[0] += 1
            ins.then_inc(s_sum, 1)
            v.wait_ge(s_sum, sums[0])

        def add_rows(t):
            v.wait_ge(s_yl[t], 16)
            for n in range(2):
                half = X[:, t, 512 * n:512 * (n + 1)]
                v.wait_ge(s_gb, 2 * t + n + 1)
                ins = v.tensor_tensor(half, bank[2 * t + n][:, :], half, ALU.add)
            ins.then_inc(s_acc, 1)

        def final_norm(t):
            v.wait_ge(s_sq, 2 * NT + t + 1)
            st = st4[:, t:t + 1]
            v.tensor_scalar(st, st, 1.0 / D, EPS, ALU.mult, ALU.add).then_inc(s_var, 1)
            v.wait_ge(s_sd, 7 + t)
            final_step(v.reciprocal(st, st))
            v.scalar_tensor_tensor(X[:, t, :], X[:, t, :], st, FG, ALU.mult, ALU.mult).then_inc(s_fin, 1)

        v.wait_ge(s_fg, 16)
        for t in range(NT):
            add_rows(t)
            if t:
                final_norm(t - 1)
        final_norm(NT - 1)

    ctx.close()


def kernel(**inputs):
    import concourse.bacc as bacc
    from concourse.bass_utils import run_bass_kernel_spmd

    cf, cl, ci, oh = shape_constants()
    a = {k: np.ascontiguousarray(v) for k, v in inputs.items()}
    arrays = {
        "x": a["x"].reshape(SEQ, D), "norm1_g": a["norm1_g"].reshape(NK, P), "norm2_g": a["norm2_g"].reshape(NK, P),
        "bg_f": a["gla_bg_fwd"].reshape(2, P), "bg_b": a["gla_bg_bwd"].reshape(2, P),
        "gla_g": a["gla_norm_g"].reshape(4, P), "w_in": a["w_in"].reshape(D, IN_W), "rel_bias": a["rel_bias"],
        "wg_f": a["gla_wg_fwd"].reshape(RANK, 256), "wg_b": a["gla_wg_bwd"].reshape(RANK, 256),
        "w_out": a["w_out"].reshape(D, D), "router_w": a["router_w"].reshape(D, E),
        "router_b": a["router_b"].reshape(1, E), "w1": a["moe_w1"].reshape(E, D, 2 * FF),
        "b1": a["moe_b1"].reshape(E, 2 * FF), "w2": a["moe_w2"].reshape(E, FF, D), "b2": a["moe_b2"].reshape(E, D),
        "final_g": a["final_g"].reshape(1, D), "const_f": cf, "const_late": cl, "const_i": ci, "const_rel": oh,
    }
    nc = bacc.Bacc("TRN2", target_bir_lowering=False, num_devices=1)
    args = [nc.dram_tensor(f"in_{n}", v.shape, mybir.dt.from_np(v.dtype), kind="ExternalInput").ap()
            for n, v in arrays.items()]
    args.append(nc.dram_tensor("out_y", (SEQ, D), F32, kind="ExternalOutput").ap())
    encoder_block(nc, *args)
    r = run_bass_kernel_spmd(nc, [{f"in_{n}": v for n, v in arrays.items()}], core_ids=[0])
    return r.results[0]["out_y"].reshape(1, SEQ, D)
```

```python
from contextlib import ExitStack

import numpy as np

import concourse.bass as bass
from concourse import mybir

F32 = mybir.dt.float32
I32 = mybir.dt.int32
U32 = mybir.dt.uint32
ALU = mybir.AluOpType
ACT = mybir.ActivationFunctionType
AX = mybir.AxisListType

P = 128
D, SEQ = 1024, 512
NT, NK = SEQ // P, D // P
HA, DH = 8, 64
NP = HA // 2
HG, DK, DV = 4, 64, 128
CH = 64
NCH = SEQ // CH
RANK, TAU = 16, 16.0
IN_W = 3104
OFF_AQ, OFF_AK, OFF_AV, OFF_GQK, OFF_GV, OFF_GO, OFF_GZ = 0, 512, 1024, 1536, 2048, 2560, 3072
EPS = 1e-5
E, TOPK, FF = 32, 4, 1024
NF = FF // P
LIMIT, ALPHA = 7.0, 1.702
SLOTS = 96
MAXB = E + SEQ * TOPK // SLOTS
COLS = MAXB + 2
GR = 32
NG = SLOTS // GR
NJ = P // GR
THR = (SEQ - 1) // SLOTS
PAD = 4096
NEG = -1e30
REL = 1024
TW = SEQ + 3 * P

CI, CU, CO, CIO, CTH = 0, 128, 256, 384, 480
NCF = CTH + THR
CSEL = 0
CTK = CSEL + NG * P
CJ = CTK + NT * TOPK
NCL = CJ + 1
V1, V2, VB, VG, NV = 0, 8, 16, 20, 24


def shape_constants():
    cf, cl = np.zeros((P, NCF), np.float32), np.zeros((P, NCL), np.float32)
    cf[:, CI:CI + P] = np.eye(P)
    cf[:, CU:CU + P] = np.triu(np.ones((P, P)), 1)
    cf[:, CO:CO + P] = 1.0
    cf[:, CIO:CTH] = np.arange(CTH - CIO)
    cf[:, CTH:CTH + THR] = SLOTS * np.arange(1, THR + 1)
    p = np.arange(P)
    for g in range(NG):
        cl[:, CSEL + g * P:CSEL + (g + 1) * P] = p[:, None] == GR * g + p[None, :] % GR
    cl[:, CTK:CTK + NT * TOPK] = np.repeat(P * np.arange(NT), TOPK)[None, :] + p[:, None] - PAD
    cl[:, CJ] = NJ * PAD + p // GR
    s, c = np.arange(P)[:, None], np.arange(P)[None, :]
    same = s // CH == c // CH
    ci = np.zeros((P, 2 * P), np.int32)
    ci[:, 0:P] = same & (s <= c)
    ci[:, P:2 * P] = same & (s >= c)
    rel = (SEQ - 1) - np.arange(REL)
    n = np.abs(rel)
    nb, exact = 16, 8
    large = exact + (np.log(np.maximum(n, 1).astype(np.float32) / exact)
                     / np.log(1024 / exact) * (nb - exact)).astype(np.int32)
    bucket = np.where(rel > 0, nb, 0) + np.where(n < exact, n, np.minimum(large, nb - 1))
    count = sum(((rel % d == 0) & (n <= 64 * d)).astype(np.int32) for d in (1, 4, 16))
    oh = np.zeros((33, REL), np.float32)
    oh[bucket, np.arange(REL)] = 1.0
    oh[32] = np.where(count > 0, np.log(np.maximum(count, 1).astype(np.float32)), NEG)
    return cf, cl, ci, oh


ATTENTION_ORDER = (("s", 2), ("pt", 0), ("gT", 0), ("pt", 1), ("pv", 0), ("s", 3), ("pt", 2), ("pv", 1),
                   ("pv", 2), ("pt", 3), ("pv", 3))


def pre_jobs():
    jobs = [(("vec",), "v"), (("rel", 0), "v"), (("rel", 1), "a")]
    jobs += [(("nT", k), "va"[k % 2]) for k in range(NK)]
    jobs += [(("gqk", c), "a") for c in range(4)]
    jobs += [(("gz",), "v")] + [(("gate", i), "v") for i in range(4)]
    jobs += [(("gv", t), "a") for t in range(NT)] + [(("go", t), "a") for t in range(NT)]
    jobs += [(("aqk", c), "a") for c in range(8)] + [(("av", t), "a") for t in range(NT)]
    jobs += [(("s", hh, t), "v") for t in range(NT) for hh in range(2)]
    jobs += [(("kst", i), "a") for i in range(4)]
    jobs += [(("ds", i, par), "v") for i in range(4) for par in ((1, 0) if i < 2 else (0, 1))]
    jobs += [(("s", 2 + hh, t), "v") for t in range(NT) for hh in range(2)]
    for t in range(NT):
        jobs += [(("at", t, par), "v") for par in range(2)]
        if t:
            jobs += [(("o", t - 1, par), "a") for par in range(2)]
    jobs += [(("o", NT - 1, par), "a") for par in range(2)]
    for kind, i in ATTENTION_ORDER:
        if kind == "s":
            jobs += [(("s", 2 * i + hh, t), "v") for t in range(NT) for hh in range(2)]
        if kind == "pt":
            jobs += [(("pt", 2 * i + hh, kb), "vaaa"[kb]) for hh in range(2) for kb in range(NT)]
        if kind == "pv":
            jobs += [(("pv", i), "a")]
        if kind == "gT":
            jobs += [(("gT", h), "a") for h in range(HG)]
    for t in range(NT + 2):
        if t < NT:
            jobs += [(("wo", t, n), "v") for n in range(2)]
        if t >= 2:
            jobs += [(("lg", t - 2), "v")]
        if 1 <= t <= NT:
            jobs += [(("hT", t - 1, q), "va"[q]) for q in range(2)]
    jobs += [(("total",), "v"), (("rank",), "v"), (("tab",), "v"), (("gmT",), "a"), (("rep",), "v")]
    return jobs


def encoder_block(nc, x, norm1_g, norm2_g, bg_f, bg_b, gla_g, w_in, rel_bias, wg_f, wg_b, w_out, router_w, router_b,
                  w1, b1, w2, b2, final_g, const_f, const_late, const_i, const_rel, out):
    ctx = ExitStack()

    def sem(name):
        return ctx.enter_context(nc.semaphore(name))

    ARENA = 24832
    FIXED = 28376
    arena = ctx.enter_context(nc.sbuf_tensor("arena", [P, ARENA], F32))
    fixed = ctx.enter_context(nc.sbuf_tensor("fixed", [P, FIXED], F32))

    def view(buf, at, *shape, parts=P, dt=F32):
        n = int(np.prod(shape))
        a = buf[0:parts, at:at + n]
        if dt is not F32:
            a = a.bitcast(dt)
        if len(shape) == 2:
            a = a.rearrange("p (a b) -> p a b", a=shape[0])
        if len(shape) == 3:
            a = a.rearrange("p (a b c) -> p a b c", a=shape[0], b=shape[1])
        if len(shape) == 4:
            a = a.rearrange("p (a b c d) -> p a b c d", a=shape[0], b=shape[1], c=shape[2])
        return a

    R = [4096 * i for i in range(7)]
    win = {"gqk": view(arena, R[0], NK, 512), "gv": view(arena, R[1], NK, 512),
           "go": view(arena, R[2], NK, 512), "aq": view(arena, R[3], NK, 512),
           "ak": view(arena, R[4], NK, 512), "av": view(arena, R[5], NK, 512),
           "gz": view(arena, R[6], NK, 32)}
    gA, gT_ = view(arena, R[0], 4, 512), view(arena, R[0] + 2048, 4, 512)
    gB, QD = view(arena, R[1], 4, 512), view(arena, R[1] + 2048, 4, 512)
    KD, KS = view(arena, R[2], 4, 512), view(arena, R[2] + 2048, 4, 512)
    ST = view(arena, R[0], 4, NCH, DV)
    KN = view(arena, R[1], 4, NT, P)
    AB = view(arena, R[3], 4, 512)
    OS = view(arena, R[3] + 2048, NT, 512)
    WO = view(arena, R[4], NK, D)
    W1 = view(arena, 0, NK, 2 * FF)
    W2 = view(arena, R[4], NF, D)

    at = 0

    def take(n):
        nonlocal at
        at += n
        return at - n

    o_x, o_nt, o_qk, o_av = take(4096), take(4096), take(4096), take(2048)
    o_gqk, o_gv, o_go, o_zt = take(2048), take(2048), take(2048), take(512)
    o_t, o_a = take(4 * TW), take(2048)
    X = view(fixed, o_x, NT, D)
    NTt = view(fixed, o_nt, NK, SEQ)
    MIX = view(fixed, o_nt, NK, SEQ)
    XN = view(fixed, o_qk, NT, D)
    QK = view(fixed, o_qk, NK, SEQ)
    AV = view(fixed, o_av, NT, 512)
    SG = view(fixed, o_av, NT, 512)
    GQ, GK = view(fixed, o_gqk, 2, SEQ), view(fixed, o_gqk + 1024, 2, SEQ)
    GV, GO = view(fixed, o_gv, NT, 512), view(fixed, o_go, NT, 512)
    ZT = view(fixed, o_zt, SEQ, parts=32)
    LP = [view(buf, o, NT, SEQ) for buf, o in (
        (fixed, o_gqk), (fixed, o_nt), (arena, R[4]), (arena, R[4] + 2048),
        (fixed, o_gv), (fixed, o_go), (fixed, o_gqk), (fixed, o_a))]
    PT = [view(arena, R[1] + 2048 * i, NT, SEQ) for i in range(4)]
    RELF = view(fixed, o_go, REL, parts=HA)
    OH = view(fixed, o_gv, REL, parts=33)
    TB = view(fixed, o_t, 4, TW)
    MSQ = view(fixed, o_a, 3, 512)
    HN = view(fixed, o_qk, NT, D)
    HT = view(fixed, o_gqk, 2, NK, P)
    OHT = view(fixed, o_gqk + 3584, NT, TOPK, E)
    OHV = view(fixed, o_nt + 512, NT, TOPK, E)
    MSEL = view(fixed, o_gqk + 4096, NT, E)
    RK = view(fixed, o_nt + 1152, NT, E)
    LG = view(fixed, o_gqk + 4224, NT, E)
    MX = view(fixed, o_gqk + 4352, NT, 8)
    IX = view(fixed, o_gqk + 4384, NT, 8, dt=U32)
    IXF = view(fixed, o_gqk + 4416, NT, 8)
    GT = view(fixed, o_nt + 1504, NT, TOPK)
    RA, SA, OV, CA = (view(fixed, o_nt + 1520 + 16 * i, NT * TOPK) for i in range(4))
    OVC = view(fixed, o_nt + 1584, NT * TOPK, THR)
    CMP = view(fixed, o_nt + 1664, E, THR)
    NB = view(fixed, o_nt + 1824, E)
    BE = view(fixed, o_nt + 1856, E)
    BS = view(fixed, o_nt + 1888, E)
    EF = view(fixed, o_nt + 1920, MAXB, parts=1)
    g4 = view(fixed, o_nt + 1984, NT, 1)
    EC = view(fixed, o_nt + 2048, MAXB, E, parts=1)
    GM = view(fixed, o_nt + 3800, NT, E)
    ONS = view(fixed, o_gqk + 2048, NT * TOPK, SLOTS)
    ONC = view(fixed, o_av, 2, NT * TOPK, COLS)
    T96 = view(fixed, o_av + 1760, 2, COLS, parts=SLOTS)
    XG = view(fixed, o_qk, D, parts=SLOTS)
    XT = view(fixed, o_qk + 1024, NK, SLOTS)
    HB = view(fixed, o_nt, NG, 2 * FF // NJ)
    SGM = view(fixed, o_nt + 1536, NG, FF // NJ)
    ACTV = view(fixed, o_nt + 2304, NG, FF // NJ)
    ATT = view(fixed, o_gqk, NG, 2, NJ, GR)
    YN = view(fixed, o_gqk + 768, NG, D // NJ)
    o_l = o_t + 2304
    CL = view(fixed, o_l, NCL)
    SID = view(fixed, o_l + NCL, NG, COLS, dt=I32)
    GAT = view(fixed, o_l + NCL + NG * COLS, NG, COLS)
    TOK = view(fixed, o_l + NCL + 2 * NG * COLS, COLS, parts=SLOTS, dt=I32)
    B1T = view(fixed, o_t, 2 * FF // NJ)
    B1Q = view(fixed, o_t + 512, 2 * FF // NJ)
    FG = view(fixed, o_a, D)
    CF = view(fixed, take(NCF), NCF)
    CIt = view(fixed, take(2 * P), 2 * P, dt=I32)
    VT = view(fixed, take(NV), NV)
    GI = view(fixed, take(1), 1, parts=SLOTS, dt=I32)
    SI = view(fixed, take(NG), NG, dt=I32)
    GTC = view(fixed, take(NG), NG)
    GMT = view(fixed, o_a + 1024, SEQ, parts=E)
    B2R = view(fixed, o_t + 1024, D, parts=E)
    EG = view(fixed, take(32), 4, NCH)
    st4 = view(fixed, take(NT), NT)
    st16 = view(fixed, take(16), NT, HG)
    mx4 = view(fixed, take(16), 4, NT)
    den4 = view(fixed, take(16), 4, NT)
    rden = view(fixed, take(16), 4, NT)
    EMAP = view(fixed, take(64), 64, parts=1, dt=I32)
    RB = view(fixed, take(E), E)
    held = view(fixed, take(3 + NG), 3 + NG)
    RWs = view(fixed, o_t + 2048, NK, E)
    assert at <= FIXED, at
    VRW = view(fixed, o_zt, P, parts=NV)
    RX = view(fixed, o_zt + 128, HA, parts=33)
    WGt = view(fixed, o_t + 3 * FF, 2, 256, parts=32)
    JUNK = view(fixed, o_a, D)
    ident = CF[:, CI:CI + P]
    ones = CF[:, CO:CO + P]
    above = CF[:, CU:CU + P]

    bank = [ctx.enter_context(nc.psum_tensor(f"bank{i}", [P, 512], F32)) for i in range(8)]

    rel_d = nc.dram_tensor("rel_d", [HA, REL], F32)
    hn_d = nc.dram_tensor("hn_d", [SEQ, D], F32)
    sum_d = nc.dram_tensor("sum_d", [SEQ * NJ, D // NJ], F32)

    jobs = pre_jobs()
    index = {name: j for j, (name, _) in enumerate(jobs)}
    emptied = []
    count = {"v": 0, "a": 0}
    for _, e in jobs:
        count[e] += 1
        emptied.append(count[e])
    bank_full = sem("bank_full")
    bank_empty = {"v": sem("bank_empty_v"), "a": sem("bank_empty_a")}

    def bank_of(name):
        return bank[index[name] % 8]

    def wait_empty(eng, *names):
        most = {}
        for n in names:
            j = index[n]
            most[jobs[j][1]] = max(most.get(jobs[j][1], 0), emptied[j])
        for e, v in most.items():
            eng.wait_ge(bank_empty[e], v)

    def wait_full(eng, name):
        eng.wait_ge(bank_full, index[name] + 1)

    s_const, s_vec, s_oh, s_rel, s_wg = (sem(n) for n in (
        "const_loaded", "vec_loaded", "onehot_loaded", "relbias_loaded", "gatew_loaded"))
    s_x = [sem(f"x{t}_loaded") for t in range(NT)]
    s_win = {k: sem(f"win_{k}_loaded") for k in ("gqk", "gz", "gv", "go", "aq", "ak", "av")}
    s_relst, s_wo, s_rw = sem("rel_stored"), sem("wout_loaded"), sem("router_loaded")
    s_tb = [sem(f"toeplitz{i}_loaded") for i in range(4)]
    s_ms = sem("pool_memset")
    ch_v, ch_a = sem("vector_chain"), sem("scalar_chain")
    s_sq, s_sd, s_xn = sem("squares_summed"), sem("root_taken"), sem("x_normalized")
    s_var = sem("variance_ready")
    s_ln = sem("gate_log_ready")
    s_b, s_gd, s_ex, s_k = sem("decay_sum_ready"), sem("decay_rest_ready"), sem("decay_exp_ready"), sem("decayed_ready")
    s_sge, s_sgd = sem("gate_exp_ready"), sem("silu_ready")
    s_zero = sem("score_buffer_zero")
    s_os = sem("gla_out_ready")
    s_rd, s_pn = sem("denominators_inverted"), sem("probs_normalized")
    s_p, s_neg = sem("probs_ready"), sem("row_max_ready")
    s_hst = sem("h_stored")
    s_dt, s_ons, s_onc, s_gm = sem("choices_ready"), sem("slot_onehot_ready"), sem("column_onehot_ready"), sem("gates_by_expert_ready")
    s_rw2 = sem("router_scaled")
    s_exg, s_exr = sem("top_logits_ready"), sem("top_exp_ready")
    s_tabr = sem("table_ready")
    s_acc0 = sem("residual_stored")
    s_emap = sem("expert_map_ready")
    s_w1 = [sem(f"w1_slot{k}_loaded") for k in range(NK)]
    s_w2 = [sem(f"w2_slot{k}_loaded") for k in range(NF // 2)]
    s_used = sem("weight_slot_used")
    s_idx, s_gath, s_yst = sem("indices_copied"), sem("tokens_gathered"), sem("y_added")
    s_xtp, s_xt = sem("x_transposed"), sem("xt_ready")
    s_b1 = sem("b1_loaded")
    s_b1p, s_b1z = sem("b1_spread"), sem("b1_buffer_zero")
    s_hf, s_sig, s_act = sem("hidden_full"), sem("sigmoid_ready"), sem("act_ready")
    s_gi, s_gc = sem("glu_input_ready"), sem("gates_copied")
    s_atp, s_at = sem("act_transposed"), sem("act_t_ready")
    s_yf, s_yn = sem("y_full"), sem("y_ready")
    s_b2, s_gb = sem("b2_loaded"), sem("b2_terms_full")
    s_yl = [sem(f"sum{t}_loaded") for t in range(NT)]
    s_acc, s_fin, s_out, s_fg = sem("sum_ready"), sem("final_ready"), sem("out_stored"), sem("final_g_loaded")

    PE_PER_BLOCK = NK + NF // 2
    LATE = 3
    STEPS = 9
    s_sum = sem("final_chain")

    block = ctx.enter_context(nc.Block())

    @block.sync
    def _(sp):
        for t in range(NT):
            sp.dma_start(X[:, t, :], x[t * P:(t + 1) * P, :]).then_inc(s_x[t], 16)
            if t == 0:
                sp.dma_start(CF, const_f).then_inc(s_const, 16)
        for src, at_row in ((norm1_g, V1), (norm2_g, V2), (bg_f, VB), (bg_b, VB + 2), (gla_g, VG)):
            sp.dma_start(VRW[at_row:at_row + src.shape[0], :], src).then_inc(s_vec, 16)
        wv = w_in.rearrange("(k p) n -> p k n", p=P)
        for name, off, w in (("gqk", OFF_GQK, 512), ("gz", OFF_GZ, 32), ("gv", OFF_GV, 512),
                             ("go", OFF_GO, 512), ("aq", OFF_AQ, 512), ("ak", OFF_AK, 512),
                             ("av", OFF_AV, 512)):
            sp.dma_start(win[name], wv[:, :, off:off + w]).then_inc(s_win[name], 16)
        wait_empty(sp, *[("gT", h) for h in range(HG)])

        def first_w1(slots):
            for k in slots:
                sp.dma_start(W1[:, k, :], w1[0, k * P:(k + 1) * P, :]).then_inc(s_w1[k], 16)

        first_w1((0, 1, 6, 7))
        wait_full(sp, ("pt", 3, NT - 1))
        sp.dma_start(WO, w_out.rearrange("(k p) n -> p k n", p=P)).then_inc(s_wo, 16)
        wait_full(sp, ("pv", NP - 1))
        first_w1((2, 3, 4, 5))
        wait_empty(sp, ("s", HA - 1, NT - 1))
        sp.wait_ge(s_b1z, 1)
        sp.dma_start(B1Q[::GR, :], b1[0, :].rearrange("(j n) -> j n", j=NJ)).then_inc(s_b1, 16)
        sp.dma_start(B2R, b2).then_inc(s_b2, 16)
        wait_full(sp, ("wo", NT - 1, 1))
        for f in range(NF // 2):
            sp.dma_start(W2[:, 2 * f:2 * f + 2, :],
                         w2[0, 2 * f * P:(2 * f + 2) * P, :].rearrange("(a p) n -> p a n", p=P)).then_inc(s_w2[f], 16)
        sp.wait_ge(s_emap, 1)
        blocks = sp.value_load(EMAP[0:1, MAXB:MAXB + 1], min_val=E, max_val=MAXB)
        with sp.Fori(1, blocks) as g:
            e = sp.value_load(EMAP[0:1, bass.ds(g, 1)], min_val=0, max_val=E - 1)
            sp.wait_ge(s_b1p, g)
            sp.dma_start(B1Q[::GR, :], b1[bass.ds(e, 1), :].rearrange("e (j n) -> (e j) n", j=NJ)).then_inc(s_b1, 16)
            for k in range(NK):
                sp.wait_ge(s_used, PE_PER_BLOCK * g - PE_PER_BLOCK + k + 1)
                sp.dma_start(W1[:, k, :],
                             w1[bass.ds(e, 1), k * P:(k + 1) * P, :].rearrange("e p n -> (e p) n")
                             ).then_inc(s_w1[k], 16)
            for f in range(NF // 2):
                sp.wait_ge(s_used, PE_PER_BLOCK * g - PE_PER_BLOCK + NK + f + 1)
                sp.dma_start(W2[:, 2 * f:2 * f + 2, :],
                             w2[bass.ds(e, 1), 2 * f * P:(2 * f + 2) * P, :].rearrange("e (a p) n -> p (e a) n", p=P)
                             ).then_inc(s_w2[f], 16)
        nb = sp.value_load(EMAP[0:1, MAXB:MAXB + 1], min_val=E, max_val=MAXB)
        sp.wait_ge(s_b1p, nb)
        sp.dma_start(B1Q[::GR, :], b1[0, :].rearrange("(j n) -> j n", j=NJ)).then_inc(s_b1, 16)
        sp.wait_ge(s_yst, 48 * nb)
        rows = sum_d.ap().rearrange("(t p j) n -> t p (j n)", p=P, j=NJ)
        for t in range(NT):
            sp.dma_start(X[:, t, :], rows[t]).then_inc(s_yl[t], 16)
        for t in range(NT):
            sp.wait_ge(s_fin, t + 1)
            sp.dma_start(out[t * P:(t + 1) * P, :], X[:, t, :]).then_inc(s_out, 16)
        sp.wait_ge(s_out, 16 * NT)

    @block.tensor
    def _(pe):
        done = [0]

        def begin(name):
            j = index[name]
            assert j == done[0], (name, jobs[done[0]])
            done[0] += 1
            if j >= 8:
                pe.wait_ge(bank_empty[jobs[j - 8][1]], emptied[j - 8])
            return bank[j % 8]

        def full(ins):
            ins.then_inc(bank_full, 1)

        pe.wait_ge(s_const, 32)
        pe.wait_ge(s_vec, 16 * 5)
        b = begin(("vec",))
        full(pe.transpose(b[:, 0:NV], VRW, ident[0:NV, 0:NV]))
        pe.wait_ge(s_oh, 16)
        pe.wait_ge(s_rel, 16)
        for i in range(2):
            b = begin(("rel", i))
            full(pe.matmul(b[0:HA, :], RX, OH[:, 512 * i:512 * (i + 1)], start=True, stop=True))
        for k in range(NK):
            b = begin(("nT", k))
            for t in range(NT):
                if k == 0:
                    pe.wait_ge(s_xn, t + 1)
                m = pe.transpose(b[:, t * P:(t + 1) * P], XN[:, t, k * P:(k + 1) * P], ident)
            full(m)
        wait_empty(pe, *[("nT", k) for k in range(NK)])

        def features(name, w, c):
            b = begin(name)
            for k in range(NK):
                m = pe.matmul(b[:, :], w[:, k, c * P:(c + 1) * P], NTt[:, k, :], start=k == 0, stop=k == NK - 1)
            full(m)

        def tokens(name, w, t):
            b = begin(name)
            for k in range(NK):
                m = pe.matmul(b[:, :], NTt[:, k, t * P:(t + 1) * P], w[:, k, :], start=k == 0, stop=k == NK - 1)
            full(m)

        pe.wait_ge(s_win["gqk"], 16)
        for c in range(4):
            features(("gqk", c), win["gqk"], c)
        pe.wait_ge(s_win["gz"], 16)
        b = begin(("gz",))
        for k in range(NK):
            m = pe.matmul(b[0:32, :], win["gz"][:, k, :], NTt[:, k, :], start=k == 0, stop=k == NK - 1)
        full(m)
        wait_empty(pe, ("gz",))
        pe.wait_ge(s_wg, 32)
        for i in range(4):
            b = begin(("gate", i))
            full(pe.matmul(b[:, :], WGt[:, i // 2, (i % 2) * P:(i % 2 + 1) * P], ZT, start=True, stop=True))
        for name in ("gv", "go"):
            pe.wait_ge(s_win[name], 16)
            for t in range(NT):
                tokens((name, t), win[name], t)
        for c in range(8):
            if c % 4 == 0:
                pe.wait_ge(s_win["aq" if c < 4 else "ak"], 16)
            features(("aqk", c), win["aq" if c < 4 else "ak"], c % 4)
        pe.wait_ge(s_win["av"], 16)
        for t in range(NT):
            tokens(("av", t), win["av"], t)

        def attention_scores(i):
            for t in range(NT):
                for hh in range(2):
                    r = slice(DH * hh, DH * hh + DH)
                    b = begin(("s", 2 * i + hh, t))
                    full(pe.matmul(b[:, :], QK[r, i, t * P:(t + 1) * P], QK[r, NP + i, :], start=True, stop=True))

        wait_empty(pe, ("aqk", 0), ("aqk", NP))
        attention_scores(0)

        for i in range(4):
            pe.wait_ge(s_k, i + 1)
            b = begin(("kst", i))
            for t in range(NT):
                m = pe.transpose(b[:, t * P:(t + 1) * P], KS[:, i, t * P:(t + 1) * P], ident)
            full(m)
        for i in range(4):
            wait_empty(pe, ("kst", i))
            for par in ((1, 0) if i < 2 else (0, 1)):
                b = begin(("ds", i, par))
                r = slice(CH * par, CH * par + CH)
                for t in range(NT):
                    for hh in range(2):
                        h = 2 * (i % 2) + hh
                        m = pe.matmul(b[DK * hh:DK * hh + DK, t * DV:(t + 1) * DV],
                                      KN[r, i, t, DK * hh:DK * hh + DK], GV[r, t, h * DV:(h + 1) * DV],
                                      start=True, stop=True)
                full(m)

        wait_empty(pe, ("aqk", 1), ("aqk", NP + 1))
        attention_scores(1)

        def scores(t):
            for par in range(2):
                b = begin(("at", t, par))
                r = slice(DK * par, DK * par + DK)
                for fc in range(2):
                    for d in range(2):
                        i = 2 * d + fc
                        n = 2 * fc + d
                        m = pe.matmul(b[:, n * P:(n + 1) * P], KD[r, i, t * P:(t + 1) * P],
                                      QD[r, i, t * P:(t + 1) * P], start=True, stop=True)
                full(m)

        def gla_out(t):
            wait_empty(pe, ("at", t, 1))
            if t == 0:
                wait_empty(pe, ("ds", 3, 1))
            for par in range(2):
                b = begin(("o", t, par))
                r = slice(DK * par, DK * par + DK)
                for fc in range(2):
                    col = slice(fc * DV, (fc + 1) * DV)
                    h = 2 * fc + par
                    for d in range(2):
                        slot = 2 * fc + d
                        m = pe.matmul(b[:, col], AB[:, 2 * (t % 2) + par, slot * P:(slot + 1) * P],
                                      GV[:, t, h * DV:(h + 1) * DV], start=d == 0, stop=False, skip_group_check=True)
                    parts = [(d, half) for d in range(2) for half in range(2)
                             if (d, 2 * t + half) not in ((0, 0), (1, NCH - 1))]
                    for q, (d, half) in enumerate(parts):
                        i, n = 2 * d + fc, 2 * t + half
                        m = pe.matmul(b[CH * half:CH * half + CH, col], QD[r, i, n * CH:(n + 1) * CH],
                                      ST[r, i, n, :], start=False, stop=q == len(parts) - 1, skip_group_check=True)
                full(m)

        for t in range(NT):
            scores(t)
            if t:
                gla_out(t - 1)
        gla_out(NT - 1)

        for kind, i in ATTENTION_ORDER:
            if kind == "s":
                attention_scores(i)
            if kind == "gT":
                for h in range(HG):
                    b = begin(("gT", h))
                    for t in range(NT):
                        if h == 0:
                            pe.wait_ge(s_os, t + 1)
                        m = pe.transpose(b[:, t * P:(t + 1) * P], OS[:, t, h * DV:(h + 1) * DV], ident)
                    full(m)
            if kind == "pv":
                wait_empty(pe, *[("pt", 2 * i + hh, kb) for hh in range(2) for kb in range(NT)])
                b = begin(("pv", i))
                for kb in range(NT):
                    for hh in range(2):
                        h = 2 * i + hh
                        m = pe.matmul(b[DH * hh:DH * hh + DH, :], AV[:, kb, h * DH:(h + 1) * DH], PT[h % 4][:, kb, :],
                                      start=kb == 0, stop=kb == NT - 1)
                full(m)
            if kind == "pt":
                for h in (2 * i, 2 * i + 1):
                    pe.wait_ge(s_pn, NT * h + NT)
                    for kb in range(NT):
                        b = begin(("pt", h, kb))
                        for t in range(NT):
                            m = pe.transpose(b[:, t * P:(t + 1) * P], LP[h][:, t, kb * P:(kb + 1) * P], ident)
                        full(m)
        wait_empty(pe, ("pv", NP - 1), *[("gT", h) for h in range(HG)])
        pe.wait_ge(s_wo, 16)
        for t in range(NT + 2):
            if t < NT:
                for n in range(2):
                    b = begin(("wo", t, n))
                    for k in range(NK):
                        m = pe.matmul(b[:, :], MIX[:, k, t * P:(t + 1) * P], WO[:, k, n * 512:(n + 1) * 512],
                                      start=k == 0, stop=k == NK - 1)
                    full(m)
            if t >= 2:
                u = t - 2
                pe.wait_ge(s_rw2, 1)
                wait_empty(pe, ("hT", u, 0), ("hT", u, 1))
                b = begin(("lg", u))
                for k in range(NK):
                    m = pe.matmul(b[:, 0:E], HT[:, u % 2, k, :], RWs[:, k, :], start=k == 0, stop=k == NK - 1)
                full(m)
            if 1 <= t <= NT:
                u = t - 1
                pe.wait_ge(s_xn, NT + u + 1)
                for q in range(2):
                    b = begin(("hT", u, q))
                    for c in range(4):
                        k = 4 * q + c
                        m = pe.transpose(b[:, c * P:(c + 1) * P], HN[:, u, k * P:(k + 1) * P], ident)
                    full(m)
        pe.wait_ge(s_dt, NT)
        b = begin(("total",))
        for t in range(NT):
            m = pe.matmul(b[:, 0:E], ones, MSEL[:, t, :], start=t == 0, stop=t == NT - 1)
        full(m)
        b = begin(("rank",))
        for t in range(NT):
            for u in range(t + 1):
                m = pe.matmul(b[:, t * E:(t + 1) * E], above if u == t else ones, MSEL[:, u, :],
                              start=u == 0, stop=u == t)
        full(m)
        pe.wait_ge(s_ons, 1)
        pe.wait_ge(s_onc, 2)
        b = begin(("tab",))
        for a in range(NT * TOPK):
            m = pe.matmul(b[0:SLOTS, 0:2 * COLS], ONS[:, a, :], ONC[:, :, a, :], start=a == 0, stop=a == NT * TOPK - 1)
        full(m)
        pe.wait_ge(s_gm, 1)
        b = begin(("gmT",))
        for t in range(NT):
            m = pe.transpose(b[0:E, t * P:(t + 1) * P], GM[:, t, :], ident)
        full(m)
        wait_empty(pe, ("tab",))
        b = begin(("rep",))
        for g in range(NG):
            m = pe.matmul(b[:, g * 2 * COLS:(g + 1) * 2 * COLS], CL[0:SLOTS, CSEL + g * P:CSEL + (g + 1) * P],
                          T96, start=True, stop=True)
        full(m)
        assert done[0] == len(jobs)

        def x_transposes(n):
            pe.wait_ge(s_gath, n)
            for q in range(2):
                for c in range(4):
                    k = 4 * q + c
                    m = pe.transpose(bank[6 + q][:, c * SLOTS:(c + 1) * SLOTS], XG[:, k * P:(k + 1) * P],
                                     ident[0:SLOTS, 0:SLOTS])
                m.then_inc(s_xtp, 1)

        def hidden(r, k):
            for j in range(NJ):
                m = pe.matmul(bank[r][GR * j:GR * (j + 1), :], XT[:, k, GR * r:GR * (r + 1)],
                              W1[:, k, 512 * j:512 * (j + 1)], start=k == 0, stop=k == NK - 1)
            return m

        def product(r, f2):
            for c in range(2):
                for j in range(NJ):
                    m = pe.matmul(bank[3 + r // 2][GR * j:GR * (j + 1), 256 * (r % 2):256 * (r % 2 + 1)],
                                  ATT[:, r, c, f2, :], W2[:, 2 * f2 + c, 256 * j:256 * (j + 1)],
                                  start=f2 == 0 and c == 0 and r != 1, stop=f2 == NF // 2 - 1 and c == 1,
                                  skip_group_check=True)
            return m

        wait_empty(pe, ("rep",), ("gmT",))
        x_transposes(16)
        blocks = pe.value_load(EMAP[0:1, MAXB:MAXB + 1], min_val=E, max_val=MAXB)
        with pe.Fori(0, blocks) as g:
            pe.wait_ge(s_xt, 2 * g + 2)
            for k in range(NK - LATE):
                pe.wait_ge(s_w1[k], 16 * g + 16)
                for r in range(NG):
                    m = hidden(r, k)
                m.then_inc(s_used, 1)
            for k in range(NK - LATE, NK):
                pe.wait_ge(s_w1[k], 16 * g + 16)
            for r in range(NG):
                for k in range(NK - LATE, NK):
                    m = hidden(r, k)
                    if r == NG - 1:
                        m.then_inc(s_used, 1)
                if r < NG - 1:
                    m.then_inc(s_hf, 1)

            def act_transposes(r):
                pe.wait_ge(s_act, NG * g + r + 1)
                for c in range(2):
                    m = pe.transpose(bank[r][:, c * P:(c + 1) * P], ACTV[:, r, c * P:(c + 1) * P], ident)
                m.then_inc(s_atp, 1)

            act_transposes(0)
            x_transposes(16 * g + 32)
            pe.wait_ge(s_at, NG * g + 1)
            for f2 in range(2):
                pe.wait_ge(s_w2[f2], 16 * g + 16)
                product(0, f2)
            act_transposes(1)
            pe.wait_ge(s_w2[2], 16 * g + 16)
            product(0, 2)
            pe.wait_ge(s_at, NG * g + 2)
            for f2 in range(3):
                product(1, f2)
            pe.wait_ge(s_w2[3], 16 * g + 16)
            product(0, 3)
            act_transposes(2)
            product(1, 3).then_inc(s_yf, 1)
            pe.wait_ge(s_at, NG * g + 3)
            for f2 in range(4):
                product(2, f2).then_inc(s_used, 1)
        nb = pe.value_load(EMAP[0:1, MAXB:MAXB + 1], min_val=E, max_val=MAXB)
        pe.wait_ge(s_yn, NG * nb)
        pe.wait_ge(s_xt, 2 * nb + 2)
        pe.wait_ge(s_b2, 16)
        for t in range(NT):
            for n in range(2):
                pe.matmul(bank[2 * t + n][:, :], GMT[:, t * P:(t + 1) * P], B2R[:, n * 512:(n + 1) * 512],
                          start=True, stop=True).then_inc(s_gb, 1)

    @block.gpsimd
    def _(pool):
        pool.memset(held, 0.0)
        pool.memset(RX, 1.0).then_inc(s_ms, 1)
        pool.memset(WGt, 0.0).then_inc(s_ms, 1)
        pool.wait_ge(s_ms, 2)
        pool.dma_start(RX[0:E, :], rel_bias).then_inc(s_rel, 16)
        pool.dma_start(WGt[0:RANK, 0, :], wg_f).then_inc(s_wg, 16)
        pool.dma_start(WGt[RANK:2 * RANK, 1, :], wg_b).then_inc(s_wg, 16)
        pool.wait_ge(s_sq, NT)
        pool.memset(MSQ[:, 0:2, :], 1.0).then_inc(s_ms, 1)
        pool.wait_ge(s_ms, 3)
        pool.memset(MSQ[:, 0, bass.ds(0, NCH, CH)], 0.0).then_inc(s_ms, 1)
        pool.memset(MSQ[:, 1, bass.ds(CH - 1, NCH, CH)], 0.0).then_inc(s_ms, 1)
        wait_full(pool, ("aqk", 3))
        pool.memset(AB, 0.0).then_inc(s_zero, 1)

        def hold(n):
            pool.tensor_tensor(held[:, 2 + n:3 + n], held[:, 0:1], held[:, 1:2], ALU.add)

        wait_empty(pool, ("s", HA - 1, NT - 1))
        pool.memset(B1Q, 0.0).then_inc(s_b1z, 1)
        last_token, last_row = (pool.to_reg(n - 1) for n in (SEQ, SEQ * NJ))
        pool.wait_ge(s_hst, 16)
        wait_full(pool, ("hT", NT - 1, 1))
        pool.memset(XG, 0.0).then_inc(s_idx, 1)
        pool.wait_ge(s_tabr, 1)

        def gather(column, copied):
            pool.tensor_copy(GI, TOK[:, column]).then_inc(s_idx, 1)
            pool.wait_ge(s_idx, copied)
            hold(NG)
            pool.indirect_dma_start(out=XG, out_offset=None, in_=hn_d.ap(),
                                    in_offset=bass.IndirectOffsetOnAxis(GI, 0),
                                    bounds_check=last_token, oob_is_err=False).then_inc(s_gath, 16)

        gather(slice(0, 1), 2)
        pool.wait_ge(s_xtp, 2)
        gather(slice(1, 2), 3)
        pool.wait_ge(s_tabr, 2)
        pool.wait_ge(s_acc0, 16)
        blocks = pool.value_load(EMAP[0:1, MAXB:MAXB + 1], min_val=E, max_val=MAXB)
        with pool.Fori(0, blocks) as g:
            pool.wait_ge(s_gath, 16 * g + 32)
            pool.wait_ge(s_xtp, 2 * g + 4)
            gather(bass.ds(g + 2, 1), 2 * g + 4)
            pool.tensor_copy(SI, SID[:, :, bass.ds(g, 1)].rearrange("p a b -> p (a b)")).then_inc(s_idx, 1)
            pool.wait_ge(s_idx, 2 * g + 5)
            for r in range(NG):
                pool.wait_ge(s_yn, NG * g + r + 1)
                hold(r)
                pool.indirect_dma_start(out=sum_d.ap(), out_offset=bass.IndirectOffsetOnAxis(SI[:, r:r + 1], 0),
                                        in_=YN[:, r, :], in_offset=None, bounds_check=last_row, oob_is_err=False,
                                        compute_op=ALU.add).then_inc(s_yst, 16)
            pool.wait_ge(s_yst, 48 * g + 48)

    @block.scalar
    def _(act):
        chain = [0]

        def link(ins):
            chain[0] += 1
            ins.then_inc(ch_a, 1)
            act.wait_ge(ch_a, chain[0])

        def emptied_by(ins):
            ins.then_inc(bank_empty["a"], 1)

        def plain(name, dst, scale=1.0):
            wait_full(act, name)
            emptied_by(act.activation(dst, bank_of(name)[:, :], ACT.Copy, scale=scale))

        act.dma_start(CIt, const_i).then_inc(s_const, 16)
        act.dma_start(OH, const_rel).then_inc(s_oh, 16)
        for t in range(NT):
            act.wait_ge(s_x[t], 16)
            if t:
                act.wait_ge(s_sq, t)
            act.activation(JUNK, X[:, t, :], ACT.Square, accum_out=st4[:, t:t + 1]).then_inc(s_sq, 1)
        act.wait_ge(s_var, 1)
        act.activation(st4, st4, ACT.Sqrt).then_inc(s_sd, 1)
        wait_full(act, ("rel", 1))
        emptied_by(act.activation(RELF[:, 512:1024], bank_of(("rel", 1))[0:HA, :], ACT.Copy))
        wait_empty(act, ("rel", 0), ("rel", 1))
        act.dma_start(rel_d.ap(), RELF).then_inc(s_relst, 16)
        wait_empty(act, ("vec",))
        for k in range(1, NK, 2):
            plain(("nT", k), NTt[:, k, :], VT[:, V1 + k:V1 + k + 1])
        for c in range(4):
            plain(("gqk", c), (GQ if c < 2 else GK)[:, c % 2, :], 0.125 if c < 2 else 1.0)
        for i in range(4):
            wait_empty(act, ("gate", i))
            link(act.activation(gT_[:, i, :], gA[:, i, :], ACT.Abs))
            link(act.activation(gT_[:, i, :], gT_[:, i, :], ACT.Exp, scale=-1.0))
            act.activation(gT_[:, i, :], gT_[:, i, :], ACT.Ln, bias=1.0).then_inc(s_ln, 1)
        wait_full(act, ("rel", 1))
        act.wait_ge(s_relst, 16)
        wait_full(act, ("gate", 3))
        for h in range(4):
            act.dma_start(TB[:, h, :], bass.AP(rel_d, h * REL, [[1, P], [1, TW]])).then_inc(s_tb[h], 16)
        for t in range(NT):
            plain(("gv", t), GV[:, t, :])
        for t in range(NT):
            plain(("go", t), GO[:, t, :])
        wait_empty(act, ("go", NT - 1))
        for t in range(NT):
            act.activation(SG[:, t, :], GO[:, t, :], ACT.Exp, scale=-1.0).then_inc(s_sge, 1)
        for i in range(4):
            act.wait_ge(s_b, i + 1)
            act.wait_ge(s_gd, i + 1)
            first = 0 if i >= 2 else CH - 1
            act.activation(EG[:, i, :], gB[:, i, bass.ds(first, NCH, CH)], ACT.Exp, scale=1.0 / TAU).then_inc(s_ex, 1)
            act.activation(QD[:, i, :], gB[:, i, :], ACT.Exp, scale=1.0 / TAU).then_inc(s_ex, 1)
            act.activation(KD[:, i, :], gB[:, i, :], ACT.Exp, scale=-1.0 / TAU).then_inc(s_ex, 1)
            act.activation(KS[:, i, :], KS[:, i, :], ACT.Exp, scale=1.0 / TAU).then_inc(s_ex, 1)
        for c in range(8):
            plain(("aqk", c), QK[:, c, :], 0.125 if c < 4 else 1.0)
        act.wait_ge(s_sgd, NT)
        for t in range(NT):
            plain(("av", t), AV[:, t, :])
        for i in range(4):
            wait_full(act, ("kst", i))
            emptied_by(act.activation(KN[:, i, :, :], bank_of(("kst", i))[:, :].rearrange("p (a b) -> p a b", b=P), ACT.Copy))
        def probs(h):
            act.wait_ge(s_neg, h // 2 + 1)
            for t in range(NT):
                act.activation(LP[h][:, t, :], LP[h][:, t, :], ACT.Exp, bias=mx4[:, h % 4, t:t + 1],
                               accum_out=den4[:, h % 4, t:t + 1]).then_inc(s_p, 1)
            if h < 4:
                act.dma_start(TB[:, h, :], bass.AP(rel_d, (h + 4) * REL, [[1, P], [1, TW]])
                              ).then_inc(s_tb[h], 16)

        probs(0)
        probs(1)
        for t in range(NT):
            for par in range(2):
                wait_full(act, ("o", t, par))
                emptied_by(act.activation(OS[:, t, :].rearrange("p (f q e) -> p q f e", f=2, q=2)[:, par, :, :],
                                          bank_of(("o", t, par))[:, 0:256].rearrange("p (f e) -> p f e", f=2), ACT.Copy))
            if t < 2:
                probs(2 + t)
        act.wait_ge(s_var, 2)
        act.activation(st16, st16, ACT.Sqrt).then_inc(s_sd, 1)

        def transposed_probs(*heads):
            for h in heads:
                for kb in range(1, NT):
                    plain(("pt", h, kb), PT[h % 4][:, kb, :])

        def attention_out(i):
            plain(("pv", i), MIX[:, i, :])

        probs(4)
        transposed_probs(0, 1)
        probs(5)
        for h in range(HG):
            plain(("gT", h), MIX[:, 4 + h, :], VT[:, VG + h:VG + h + 1])
        transposed_probs(2, 3)
        attention_out(0)
        probs(6)
        transposed_probs(4, 5)
        probs(7)
        attention_out(1)
        attention_out(2)
        transposed_probs(6, 7)
        attention_out(3)
        wait_full(act, ("s", HA - 1, NT - 1))
        act.wait_ge(s_neg, NP)
        act.dma_start(RWs, router_w.rearrange("(k p) e -> p k e", p=P)).then_inc(s_rw, 16)
        act.dma_start(CL, const_late).then_inc(s_rw, 16)
        act.dma_start(RB, bass.AP(router_b.tensor, 0, [[0, P], [1, E]])).then_inc(s_rw, 16)
        def transposed(t):
            wait_full(act, ("hT", t, 1))
            emptied_by(act.activation(HT[:, t % 2, 4:8, :],
                                      bank_of(("hT", t, 1))[:, :].rearrange("p (a b) -> p a b", b=P), ACT.Copy))

        wait_full(act, ("pt", HA - 1, NT - 1))
        for t in range(NT):
            wait_empty(act, ("wo", t, 1))
            act.activation(JUNK, X[:, t, :], ACT.Square, accum_out=st4[:, t:t + 1]).then_inc(s_sq, 1)
            act.wait_ge(s_var, 3 + t)
            act.activation(st4[:, t:t + 1], st4[:, t:t + 1], ACT.Sqrt).then_inc(s_sd, 1)
            if t:
                transposed(t - 1)
        transposed(NT - 1)
        act.wait_ge(s_xn, 2 * NT)
        act.dma_start(hn_d.ap().rearrange("(t p) d -> p t d", p=P), HN).then_inc(s_hst, 16)
        act.dma_start(sum_d.ap().rearrange("(t p j) n -> p t (j n)", p=P, j=NJ), X).then_inc(s_acc0, 16)
        act.wait_ge(s_exg, 1)
        act.activation(GT, GT, ACT.Exp).then_inc(s_exr, 1)
        wait_full(act, ("gmT",))
        emptied_by(act.activation(GMT, bank_of(("gmT",))[0:E, :], ACT.Copy))
        act.dma_start(FG, bass.AP(final_g.tensor, 0, [[0, P], [1, D]])).then_inc(s_fg, 16)

        act.wait_ge(s_emap, 1)
        blocks = act.value_load(EMAP[0:1, MAXB:MAXB + 1], min_val=E, max_val=MAXB)
        with act.Fori(0, blocks) as g:
            def sigmoid(r):
                act.wait_ge(s_gi, NG * g + r + 1)
                act.activation(SGM[:, r, :], HB[:, r, 0:512:2], ACT.Sigmoid, scale=ALPHA).then_inc(s_sig, 1)

            def transposed_act(r):
                act.wait_ge(s_atp, NG * g + r + 1)
                act.activation(ATT[:, r, :, :, :].rearrange("p c j t -> p (c j t)"),
                               bank[r][:, 0:256], ACT.Copy).then_inc(s_at, 1)

            sigmoid(0)
            sigmoid(1)
            transposed_act(0)
            sigmoid(2)
            transposed_act(1)
            transposed_act(2)
            act.wait_ge(s_idx, 2 * g + 4)
            act.wait_ge(s_gc, g + 1)
            for r in range(NG):
                if r < 2:
                    act.wait_ge(s_yf, g + 1)
                else:
                    act.wait_ge(s_used, PE_PER_BLOCK * g + PE_PER_BLOCK)
                act.activation(YN[:, r, :], bank[3 + r // 2][:, 256 * (r % 2):256 * (r % 2 + 1)], ACT.Copy,
                               scale=GTC[:, r:r + 1]).then_inc(s_yn, 1)
        for t in range(NT):
            act.wait_ge(s_acc, t + 1)
            act.activation(HB[:, 0:2, :].rearrange("p a b -> p (a b)"), X[:, t, :], ACT.Square,
                           accum_out=st4[:, t:t + 1]).then_inc(s_sq, 1)
            act.wait_ge(s_var, 7 + t)
            act.activation(st4[:, t:t + 1], st4[:, t:t + 1], ACT.Sqrt).then_inc(s_sd, 1)

    @block.vector
    def _(v):
        chain = [0]

        def link(ins):
            chain[0] += 1
            ins.then_inc(ch_v, 1)
            v.wait_ge(ch_v, chain[0])

        def emptied_by(ins):
            ins.then_inc(bank_empty["v"], 1)

        def chunks(a):
            return a.rearrange("p (n c) -> p n c", c=CH)

        def bcast(a, n):
            return a.unsqueeze(len(a.shape)).to_broadcast([*a.shape, n])

        def inv_root(stat, n, nth, k):
            v.tensor_scalar(stat, stat, 1.0 / k, EPS, ALU.mult, ALU.add).then_inc(s_var, 1)
            v.wait_ge(s_sd, nth)
            link(v.reciprocal(stat, stat))

        v.wait_ge(s_const, 32)
        wait_full(v, ("vec",))
        emptied_by(v.tensor_copy(VT, bank_of(("vec",))[:, 0:NV]))
        wait_full(v, ("rel", 0))
        emptied_by(v.tensor_copy(RELF[:, 0:512], bank_of(("rel", 0))[0:HA, :]))
        v.wait_ge(s_sq, NT)
        inv_root(st4, NT, 1, D)
        for t in range(NT):
            v.tensor_scalar(XN[:, t, :], X[:, t, :], st4[:, t:t + 1], None, ALU.mult).then_inc(s_xn, 1)
        wait_empty(v, ("vec",))
        for k in range(0, NK, 2):
            wait_full(v, ("nT", k))
            emptied_by(v.tensor_scalar(NTt[:, k, :], bank_of(("nT", k))[:, :], VT[:, V1 + k:V1 + k + 1], None, ALU.mult))
        wait_full(v, ("gz",))
        emptied_by(v.tensor_copy(ZT, bank_of(("gz",))[0:32, :]))
        for i in range(4):
            wait_full(v, ("gate", i))
            emptied_by(v.tensor_scalar(gA[:, i, :], bank_of(("gate", i))[:, :], VT[:, VB + i:VB + i + 1], None,
                                       ALU.add))
        v.wait_ge(s_ms, 5)
        wait_full(v, ("go", NT - 1))
        for i in range(4):
            v.wait_ge(s_ln, i + 1)
            link(v.scalar_tensor_tensor(gA[:, i, :], gA[:, i, :], 0.0, gT_[:, i, :], ALU.min, ALU.subtract))
            rev = slice(None, None, -1 if i >= 2 else 1)
            v.tensor_tensor_scan(gB[:, i, rev], MSQ[:, i // 2, rev], gA[:, i, rev], 0.0,
                                 ALU.mult, ALU.add).then_inc(s_b, 1)
            v.wait_ge(s_b, i + 1)
            first = 0 if i >= 2 else CH - 1
            v.tensor_tensor(chunks(KS[:, i, :]), bcast(gB[:, i, bass.ds(first, NCH, CH)], CH), chunks(gB[:, i, :]),
                            ALU.subtract).then_inc(s_gd, 1)
        for t in range(NT):
            v.wait_ge(s_sge, t + 1)
            link(v.tensor_scalar(SG[:, t, :], SG[:, t, :], 1.0, None, ALU.add))
            link(v.reciprocal(SG[:, t, :], SG[:, t, :]))
            v.tensor_tensor(GO[:, t, :], GO[:, t, :], SG[:, t, :], ALU.mult).then_inc(s_sgd, 1)
        wait_empty(v, ("gqk", 3))
        for i in range(4):
            v.wait_ge(s_ex, 4 * i + 4)
            v.tensor_tensor(KS[:, i, :], KS[:, i, :], GK[:, i % 2, :], ALU.mult).then_inc(s_k, 1)
            v.tensor_tensor(KD[:, i, :], KD[:, i, :], GK[:, i % 2, :], ALU.mult).then_inc(ch_v, 1)
            v.tensor_tensor(QD[:, i, :], QD[:, i, :], GQ[:, i % 2, :], ALU.mult).then_inc(ch_v, 1)
            chain[0] += 2
        v.wait_ge(ch_v, chain[0])
        def logits(i):
            pair = slice(2 * (i % 2), 2 * (i % 2) + 2)
            for t in range(NT):
                for h in (2 * i, 2 * i + 1):
                    if t == 0:
                        v.wait_ge(s_tb[h % 4], 16 * (h // 4 + 1))
                    wait_full(v, ("s", h, t))
                    emptied_by(v.tensor_tensor_reduce(
                        out=LP[h][:, t, :], in0=bank_of(("s", h, t))[:, :],
                        in1=TB[:, h % 4, t * P:t * P + SEQ][:, ::-1], scale=1.0, scalar=-3.0e38,
                        op0=ALU.add, op1=ALU.max, accum_out=mx4[:, h % 4, t:t + 1]))
            wait_empty(v, ("s", 2 * i + 1, NT - 1))
            v.tensor_scalar(mx4[:, pair, :], mx4[:, pair, :], -1.0, None, ALU.mult).then_inc(s_neg, 1)

        def normalize(i):
            for h in (2 * i, 2 * i + 1):
                v.wait_ge(s_p, NT * (h + 1))
                v.reciprocal(rden[:, h % 4, :], den4[:, h % 4, :]).then_inc(s_rd, 1)
                v.wait_ge(s_rd, h + 1)
                for t in range(NT):
                    v.tensor_scalar(LP[h][:, t, :], LP[h][:, t, :], rden[:, h % 4, t:t + 1], None,
                                    ALU.mult).then_inc(s_pn, 1)

        def gla_squares(t):
            wait_empty(v, ("o", t, 1))
            link(v.tensor_tensor(MSQ[:, 2, :], OS[:, t, :], OS[:, t, :], ALU.mult))
            link(v.tensor_reduce(st16[:, t, :], MSQ[:, 2, :].rearrange("p (h e) -> p h e", h=HG), AX.X, ALU.add))

        logits(0)
        for i in range(4):
            back = i >= 2
            wait_full(v, ("ds", i, 1 if back else 0))
            v.wait_ge(s_ex, 4 * i + 4)
            order = range(NCH - 1, 0, -1) if back else range(NCH - 1)
            for q, n in enumerate(order):
                add = bank_of(("ds", i, n % 2))[:, (n // 2) * DV:(n // 2 + 1) * DV]
                to = n - 1 if back else n + 1
                if q == 0:
                    ins = v.tensor_copy(ST[:, i, to, :], add)
                else:
                    ins = v.scalar_tensor_tensor(ST[:, i, to, :], ST[:, i, n, :], EG[:, i, n:n + 1], add,
                                                 ALU.mult, ALU.add)
                if q < NCH - 3:
                    link(ins)
                else:
                    emptied_by(ins)
                    wait_empty(v, ("ds", i, n % 2))
        logits(1)
        mask = CIt[:, 0:2 * P].rearrange("p (d c) -> p d c", d=2)
        v.wait_ge(s_zero, 1)
        for t in range(NT):
            for par in range(2):
                wait_full(v, ("at", t, par))
                if t >= 2:
                    wait_full(v, ("o", t - 2, 1))
                for fc in range(2):
                    ins = v.copy_predicated(
                        AB[:, 2 * (t % 2) + par, fc * 256:(fc + 1) * 256].rearrange("p (d c) -> p d c", d=2), mask,
                        bank_of(("at", t, par))[:, fc * 256:(fc + 1) * 256].rearrange("p (d c) -> p d c", d=2))
                    if fc == 0:
                        link(ins)
                emptied_by(ins)
            if t == 1:
                normalize(0)
            if t >= 2:
                gla_squares(t - 2)
        gla_squares(NT - 2)
        gla_squares(NT - 1)
        inv_root(st16, 16, 2, DV)
        for t in range(NT):
            o3 = OS[:, t, :].rearrange("p (h e) -> p h e", h=HG)
            link(v.tensor_tensor(o3, o3, bcast(st16[:, t, :], DV), ALU.mult))
            v.tensor_tensor(OS[:, t, :], OS[:, t, :], GO[:, t, :], ALU.mult).then_inc(s_os, 1)
        def transposed_probs(*heads):
            for h in heads:
                wait_full(v, ("pt", h, 0))
                emptied_by(v.tensor_copy(PT[h % 4][:, 0, :], bank_of(("pt", h, 0))[:, :]))

        normalize(1)
        logits(2)
        transposed_probs(0, 1, 2, 3)
        normalize(2)
        logits(3)
        transposed_probs(4, 5)
        normalize(3)
        transposed_probs(6, 7)
        v.wait_ge(s_rw, 48)
        for k in range(NK):
            ins = v.tensor_scalar(RWs[:, k, :], RWs[:, k, :], VT[:, V2 + k:V2 + k + 1], None, ALU.mult)
        ins.then_inc(s_rw2, 1)
        io = CF[:, CIO:CIO + E]

        def top4(t):
            wait_full(v, ("lg", t))
            emptied_by(v.tensor_tensor(LG[:, t, :], bank_of(("lg", t))[:, 0:E], RB, ALU.add))
            wait_empty(v, ("lg", t))
            link(v.max(MX[:, t, :], LG[:, t, :]))
            link(v.max_index(IX[:, t, :], MX[:, t, :], LG[:, t, :]))
            link(v.tensor_copy(IXF[:, t, :], IX[:, t, :]))
            link(v.tensor_tensor(OHT[:, t, :, :], bcast(IXF[:, t, 0:TOPK], E),
                                 io.unsqueeze(1).to_broadcast([P, TOPK, E]), ALU.is_equal))
            v.tensor_reduce(MSEL[:, t, :], OHT[:, t, :, :].rearrange("p k e -> p e k"), AX.X, ALU.add).then_inc(s_dt, 1)

        for t in range(NT + 2):
            if t < NT:
                for n in range(2):
                    wait_full(v, ("wo", t, n))
                    emptied_by(v.tensor_tensor(X[:, t, n * 512:(n + 1) * 512], bank_of(("wo", t, n))[:, :],
                                               X[:, t, n * 512:(n + 1) * 512], ALU.add))
                wait_empty(v, ("wo", t, 1))
                v.wait_ge(s_sq, NT + t + 1)
                inv_root(st4[:, t:t + 1], 1, 3 + t, D)
                v.tensor_scalar(HN[:, t, :], X[:, t, :], st4[:, t:t + 1], None, ALU.mult).then_inc(s_xn, 1)
            if t >= 2:
                top4(t - 2)
            if 1 <= t <= NT:
                wait_full(v, ("hT", t - 1, 0))
                emptied_by(v.tensor_copy(HT[:, (t - 1) % 2, 0:4, :],
                                         bank_of(("hT", t - 1, 0))[:, :].rearrange("p (a b) -> p a b", b=P)))
        v.tensor_tensor(GT, MX[:, :, 0:TOPK], MX[:, :, 0:1].to_broadcast([P, NT, TOPK]), ALU.subtract).then_inc(s_exg, 1)
        wait_full(v, ("total",))
        cnt = bank_of(("total",))[:, 0:E]
        thr = CF[:, CTH:CTH + THR].unsqueeze(1)
        emptied_by(v.tensor_tensor(CMP, bcast(cnt, THR), thr.to_broadcast([P, E, THR]), ALU.is_gt))
        wait_empty(v, ("total",))
        link(v.tensor_reduce(NB, CMP, AX.X, ALU.add))
        link(v.tensor_scalar(NB, NB, 1.0, None, ALU.add))
        link(v.tensor_tensor_scan(BE, ones[:, 0:E], NB, 0.0, ALU.mult, ALU.add))
        link(v.tensor_tensor(BS, BE, NB, ALU.subtract))
        wait_full(v, ("rank",))
        emptied_by(v.tensor_copy(RK, bank_of(("rank",))[:, 0:NT * E].rearrange("p (t e) -> p t e", t=NT)))
        wait_empty(v, ("rank",))

        def chosen(dst, by_expert):
            link(v.tensor_tensor(OHV, OHT, by_expert, ALU.mult))
            link(v.tensor_reduce(dst.rearrange("p (t k) -> p t k", t=NT), OHV, AX.X, ALU.add))

        chosen(RA, RK.unsqueeze(2).to_broadcast([P, NT, TOPK, E]))
        link(v.tensor_tensor(OVC, bcast(RA, THR), thr.to_broadcast([P, NT * TOPK, THR]), ALU.is_ge))
        link(v.tensor_reduce(OV, OVC, AX.X, ALU.add))
        link(v.scalar_tensor_tensor(SA, OV, -float(SLOTS), RA, ALU.mult, ALU.add))
        slots = CF[:, CIO:CIO + SLOTS].unsqueeze(1).to_broadcast([P, NT * TOPK, SLOTS])
        v.tensor_tensor(ONS, bcast(SA, SLOTS), slots, ALU.is_equal).then_inc(s_ons, 1)
        chosen(CA, BS.unsqueeze(1).unsqueeze(1).to_broadcast([P, NT, TOPK, E]))
        link(v.tensor_tensor(CA, CA, OV, ALU.add))
        v.wait_ge(s_exr, 1)
        link(v.tensor_reduce(g4[:, :, 0], GT, AX.X, ALU.add))
        link(v.reciprocal(g4[:, :, 0], g4[:, :, 0]))
        link(v.tensor_tensor(GT, GT, g4[:, :, 0:1].to_broadcast([P, NT, TOPK]), ALU.mult))
        cols = CF[:, CIO:CIO + COLS].unsqueeze(1).to_broadcast([P, NT * TOPK, COLS])
        link(v.tensor_tensor(ONC[:, 0, :, :], bcast(CA, COLS), cols, ALU.is_equal))
        v.tensor_tensor(ONC[:, 1, :, :], ONC[:, 0, :, :], bcast(GT.rearrange("p t k -> p (t k)"), COLS),
                        ALU.mult).then_inc(s_onc, 1)
        v.wait_ge(s_onc, 1)
        v.tensor_tensor(ONC[:, 0, :, :], ONC[:, 0, :, :], bcast(CL[:, CTK:CTK + NT * TOPK], COLS),
                        ALU.mult).then_inc(s_onc, 1)
        link(v.tensor_tensor(OHV, OHT, bcast(GT, E), ALU.mult))
        v.tensor_reduce(GM, OHV.rearrange("p t k e -> p t e k"), AX.X, ALU.add).then_inc(s_gm, 1)
        ends = BE[0:1, :].unsqueeze(1).to_broadcast([1, MAXB, E])
        link(v.tensor_tensor(EC, ends, bcast(CF[0:1, CIO:CIO + MAXB], E), ALU.is_le))
        link(v.tensor_reduce(EF, EC, AX.X, ALU.add))
        link(v.tensor_scalar(EF, EF, float(E - 1), None, ALU.min))
        link(v.tensor_copy(EMAP[:, 0:MAXB], EF))
        v.tensor_copy(EMAP[:, MAXB:MAXB + 1], BE[0:1, E - 1:E]).then_inc(s_emap, 1)
        wait_full(v, ("tab",))
        emptied_by(v.tensor_copy(T96, bank_of(("tab",))[0:SLOTS, 0:2 * COLS].rearrange("p (a b) -> p a b", a=2)))
        wait_empty(v, ("tab",))
        v.tensor_scalar(TOK, T96[:, 0, :], float(PAD), None, ALU.add).then_inc(s_tabr, 1)
        wait_full(v, ("rep",))
        rep_ = bank_of(("rep",))[:, 0:NG * 2 * COLS].rearrange("p (g a b) -> p g a b", g=NG, a=2)
        v.tensor_scalar(SID, rep_[:, :, 0, :], float(NJ), CL[:, CJ:CJ + 1], ALU.mult, ALU.add).then_inc(s_tabr, 1)
        emptied_by(v.tensor_copy(GAT, rep_[:, :, 1, :]))
        wait_empty(v, ("rep",))

        def gain(q):
            return bcast(VT[:, V2 + 4 * q:V2 + 4 * q + 4], SLOTS)

        def four(b):
            return b[:, 0:4 * SLOTS].rearrange("p (a b) -> p a b", a=4)

        def next_tokens(base, n):
            v.wait_ge(s_b1, n)
            for q in range(2):
                v.wait_ge(s_xtp, base + q + 1)
                v.tensor_tensor(XT[:, 4 * q:4 * q + 4, :], four(bank[6 + q]), gain(q), ALU.mult).then_inc(s_xt, 1)
            v.stream_shuffle(B1T, B1Q, [0] * GR).then_inc(s_b1p, 1)

        v.wait_ge(s_b1z, 1)
        next_tokens(0, 16)
        blocks = v.value_load(EMAP[0:1, MAXB:MAXB + 1], min_val=E, max_val=MAXB)
        before = chain[0]
        with v.Fori(0, blocks) as g:
            steps = [0]

            def step(ins):
                steps[0] += 1
                ins.then_inc(ch_v, 1)
                v.wait_ge(ch_v, STEPS * g + before + steps[0])

            v.wait_ge(s_xt, 2 * g + 2)
            v.wait_ge(s_b1p, g + 1)

            def clamp(r):
                if r < NG - 1:
                    v.wait_ge(s_hf, 2 * g + r + 1)
                else:
                    v.wait_ge(s_used, PE_PER_BLOCK * g + NK)
                z = HB[:, r, :]
                glu, lin = z[:, 0:512:2], z[:, 1:512:2]
                step(v.tensor_tensor(z, bank[r][:, :], B1T, ALU.add))
                v.tensor_scalar(glu, glu, LIMIT, None, ALU.min).then_inc(s_gi, 1)
                step(v.tensor_scalar(lin, lin, LIMIT, -LIMIT, ALU.min, ALU.max))
                v.wait_ge(s_gi, NG * g + r + 1)
                step(v.scalar_tensor_tensor(lin, lin, 1.0, glu, ALU.add, ALU.mult))

            def swiglu(r):
                v.wait_ge(s_sig, NG * g + r + 1)
                v.tensor_tensor(ACTV[:, r, :], HB[:, r, 1:512:2], SGM[:, r, :], ALU.mult).then_inc(s_act, 1)

            for r in range(NG):
                clamp(r)
                swiglu(r)
                if r == 0:
                    v.tensor_copy(GTC, GAT[:, :, bass.ds(g, 1)].rearrange("p a b -> p (a b)")).then_inc(s_gc, 1)
            next_tokens(2 * g + 2, 16 * g + 32)
            assert steps[0] == STEPS
        sums = [0]

        def final_step(ins):
            sums[0] += 1
            ins.then_inc(s_sum, 1)
            v.wait_ge(s_sum, sums[0])

        def add_rows(t):
            v.wait_ge(s_yl[t], 16)
            for n in range(2):
                half = X[:, t, 512 * n:512 * (n + 1)]
                v.wait_ge(s_gb, 2 * t + n + 1)
                ins = v.tensor_tensor(half, bank[2 * t + n][:, :], half, ALU.add)
            ins.then_inc(s_acc, 1)

        def final_norm(t):
            v.wait_ge(s_sq, 2 * NT + t + 1)
            st = st4[:, t:t + 1]
            v.tensor_scalar(st, st, 1.0 / D, EPS, ALU.mult, ALU.add).then_inc(s_var, 1)
            v.wait_ge(s_sd, 7 + t)
            final_step(v.reciprocal(st, st))
            v.scalar_tensor_tensor(X[:, t, :], X[:, t, :], st, FG, ALU.mult, ALU.mult).then_inc(s_fin, 1)

        v.wait_ge(s_fg, 16)
        for t in range(NT):
            add_rows(t)
            if t:
                final_norm(t - 1)
        final_norm(NT - 1)

    ctx.close()


def kernel(**inputs):
    import concourse.bacc as bacc
    from concourse.bass_utils import run_bass_kernel_spmd

    cf, cl, ci, oh = shape_constants()
    a = {k: np.ascontiguousarray(v) for k, v in inputs.items()}
    arrays = {
        "x": a["x"].reshape(SEQ, D), "norm1_g": a["norm1_g"].reshape(NK, P), "norm2_g": a["norm2_g"].reshape(NK, P),
        "bg_f": a["gla_bg_fwd"].reshape(2, P), "bg_b": a["gla_bg_bwd"].reshape(2, P),
        "gla_g": a["gla_norm_g"].reshape(4, P), "w_in": a["w_in"].reshape(D, IN_W), "rel_bias": a["rel_bias"],
        "wg_f": a["gla_wg_fwd"].reshape(RANK, 256), "wg_b": a["gla_wg_bwd"].reshape(RANK, 256),
        "w_out": a["w_out"].reshape(D, D), "router_w": a["router_w"].reshape(D, E),
        "router_b": a["router_b"].reshape(1, E), "w1": a["moe_w1"].reshape(E, D, 2 * FF),
        "b1": a["moe_b1"].reshape(E, 2 * FF), "w2": a["moe_w2"].reshape(E, FF, D), "b2": a["moe_b2"].reshape(E, D),
        "final_g": a["final_g"].reshape(1, D), "const_f": cf, "const_late": cl, "const_i": ci, "const_rel": oh,
    }
    nc = bacc.Bacc("TRN2", target_bir_lowering=False, num_devices=1)
    args = [nc.dram_tensor(f"in_{n}", v.shape, mybir.dt.from_np(v.dtype), kind="ExternalInput").ap()
            for n, v in arrays.items()]
    args.append(nc.dram_tensor("out_y", (SEQ, D), F32, kind="ExternalOutput").ap())
    encoder_block(nc, *args)
    r = run_bass_kernel_spmd(nc, [{f"in_{n}": v for n, v in arrays.items()}], core_ids=[0])
    return r.results[0]["out_y"].reshape(1, SEQ, D)
```
